# Optimizing a Trainium2 kernel written in Bass

```python
import jax, jax.numpy as jnp
from jax import lax
import numpy as np

D_MODEL = 1024
BATCH = 1
SEQ = 512
DEPTH = 1
DEC_BATCH = 8
DEC_SEQ = 1
PAST_LEN = 256
PAGE_SIZE = 128

HEAD_DIM = 64
NSA_HEADS = 8
NSA_KV_HEADS = 2
NSA_REP = NSA_HEADS // NSA_KV_HEADS
NSA_WIDTH = NSA_HEADS * HEAD_DIM
RWKV_HEADS = 8
RWKV_WIDTH = RWKV_HEADS * HEAD_DIM
CMP_BLOCK = 32
CMP_STRIDE = 16
CMP_HIDDEN = 256
SEL_BLOCK = 64
SEL_TOPN = 16
WINDOW = 512
Q_BLOCK = 128
DECAY_RANK = 64
A_RANK = 64
GATE_RANK = 128
FFN_HIDDEN = -(-8 * D_MODEL // (3 * 256)) * 256
PLE_DIM = 256
Q_COLS = NSA_WIDTH
KV_COLS = 4 * NSA_KV_HEADS * HEAD_DIM
WIN_COLS = 2 * NSA_KV_HEADS * HEAD_DIM
GATE_COLS = 3 * NSA_HEADS
RWKV_PROJ = 3 * RWKV_WIDTH + DECAY_RANK + A_RANK + GATE_RANK
IN_COLS = Q_COLS + KV_COLS + WIN_COLS + GATE_COLS + RWKV_PROJ
NORM_EPS = 1e-6
GN_EPS = 64e-5
BIG = 1e9

kernel_name = 'hybrid_nsa_rwkv7_decoder_step'

def rmsnorm(x, g):
    x32 = x.astype(jnp.float32)
    y = x32 * lax.rsqrt(jnp.mean(x32 * x32, axis=-1, keepdims=True) + NORM_EPS)
    return (y * g.astype(jnp.float32)).astype(x.dtype)

def masked_softmax(s, mask):
    s = jnp.where(mask, s.astype(jnp.float32), -jnp.inf)
    m = jnp.max(s, axis=-1, keepdims=True)
    m = jnp.where(jnp.isfinite(m), m, 0.0)
    e = jnp.where(mask, jnp.exp(s - m), 0.0)
    return e / jnp.maximum(jnp.sum(e, axis=-1, keepdims=True), 1e-30)

def compress(rows, pe, w1, b1, w2, b2):
    B, L, G, hd = rows.shape
    xw = jnp.transpose(rows, (0, 2, 1, 3)).reshape(B * G, L, hd)
    k1 = w1.reshape(CMP_BLOCK, hd, CMP_HIDDEN)
    hcv = lax.conv_general_dilated(xw, k1, (CMP_STRIDE,), 'VALID', dimension_numbers=('NWC', 'WIO', 'NWC'))
    hcv = jax.nn.gelu(hcv + (pe.reshape(-1) @ w1 + b1))
    out = hcv @ w2 + b2
    nb = out.shape[1]
    return jnp.transpose(out.reshape(B, G, nb, hd), (0, 2, 1, 3))

def nsa_mixer(q, gate_logits, kv_full, kw_pad, q_pos0, lp):
    B, Tq = q.shape[0], q.shape[1]
    L = kv_full.shape[1]
    G, R = NSA_KV_HEADS, NSA_REP
    qn = (rmsnorm(q, lp['q_norm']) * (HEAD_DIM ** -0.5)).reshape(B, Tq, G, R, HEAD_DIM)
    kc = rmsnorm(compress(kv_full[:, :, 0], lp['cmp_pe'][0], lp['cmp_w1'][0], lp['cmp_b1'][0],
                          lp['cmp_w2'][0], lp['cmp_b2'][0]), lp['k_norm'][0])
    vc = compress(kv_full[:, :, 1], lp['cmp_pe'][1], lp['cmp_w1'][1], lp['cmp_b1'][1],
                  lp['cmp_w2'][1], lp['cmp_b2'][1])
    nb = kc.shape[1]
    c_start = jnp.arange(nb) * CMP_STRIDE
    c_end = c_start + CMP_BLOCK - 1
    ns = -(-L // SEL_BLOCK)
    n_sel = min(SEL_TOPN, ns)
    s_start = jnp.arange(ns) * SEL_BLOCK
    overlap = ((c_start[:, None] < s_start[None] + SEL_BLOCK)
               & (c_start[:, None] + CMP_BLOCK > s_start[None])).astype(jnp.float32)
    pad = ns * SEL_BLOCK - L
    ks = jnp.pad(rmsnorm(kv_full[:, :, 2], lp['k_norm'][1]), ((0, 0), (0, pad), (0, 0), (0, 0)))
    vs = jnp.pad(kv_full[:, :, 3], ((0, 0), (0, pad), (0, 0), (0, 0)))
    kw = rmsnorm(kw_pad[:, :, 0], lp['k_norm'][2])
    vw = kw_pad[:, :, 1]
    gates = jax.nn.sigmoid(gate_logits.astype(jnp.float32)).astype(q.dtype).reshape(B, Tq, G, R, 3)
    chunk = Q_BLOCK if Tq % Q_BLOCK == 0 else Tq
    bi = jnp.arange(B)[:, None, None, None]
    gi = jnp.arange(G)[None, None, :, None]
    jsel = jnp.arange(ns)

    def attend_chunk(c):
        qs = c * chunk
        q_c = lax.dynamic_slice_in_dim(qn, qs, chunk, 1)
        pos = q_pos0 + qs + jnp.arange(chunk)
        s_c = jnp.einsum('bcgrd,bngd->bcgrn', q_c, kc)
        m_c = (c_end[None] <= pos[:, None])[None, :, None, None, :]
        p_c = masked_softmax(s_c, m_c)
        o_c = jnp.einsum('bcgrn,bngd->bcgrd', p_c.astype(vc.dtype), vc)
        imp = jnp.einsum('bcgn,ns->bcgs', jnp.sum(p_c, axis=3), overlap)
        cur = pos // SEL_BLOCK
        forced = (jsel[None] == 0) | (jsel[None] == cur[:, None]) | (jsel[None] == cur[:, None] - 1)
        causal = s_start[None] <= pos[:, None]
        score = jnp.where(forced[None, :, None], BIG, jnp.where(causal[None, :, None], imp, -BIG))
        _, idx = lax.top_k(score, n_sel)
        kpos = (idx[..., None] * SEL_BLOCK + jnp.arange(SEL_BLOCK)).reshape(B, chunk, G, n_sel * SEL_BLOCK)
        k_g = ks[bi, kpos, gi]
        v_g = vs[bi, kpos, gi]
        s_s = jnp.einsum('bcgrd,bcgkd->bcgrk', q_c, k_g)
        m_s = (kpos <= pos[None, :, None, None])[:, :, :, None, :]
        p_s = masked_softmax(s_s, m_s)
        o_s = jnp.einsum('bcgrk,bcgkd->bcgrd', p_s.astype(v_g.dtype), v_g)
        k_w = lax.dynamic_slice_in_dim(kw, qs, chunk + WINDOW, 1)
        v_w = lax.dynamic_slice_in_dim(vw, qs, chunk + WINDOW, 1)
        wpos = q_pos0 - WINDOW + qs + jnp.arange(chunk + WINDOW)
        dist = pos[:, None] - wpos[None]
        m_w = ((dist >= 0) & (dist <= WINDOW) & (wpos[None] >= 0))[None, :, None, None, :]
        s_w = jnp.einsum('bcgrd,bkgd->bcgrk', q_c, k_w)
        p_w = masked_softmax(s_w, m_w)
        o_w = jnp.einsum('bcgrk,bkgd->bcgrd', p_w.astype(v_w.dtype), v_w)
        g_c = lax.dynamic_slice_in_dim(gates, qs, chunk, 1)
        return g_c[..., 0:1] * o_c + g_c[..., 1:2] * o_s + g_c[..., 2:3] * o_w

    out = lax.map(attend_chunk, jnp.arange(Tq // chunk))
    return jnp.moveaxis(out, 0, 1).reshape(B, Tq, NSA_WIDTH)

def rwkv_mixer(xr, shift0, wkv0, lp):
    B, T = xr.shape[0], xr.shape[1]
    H, N, RW = RWKV_HEADS, HEAD_DIM, RWKV_WIDTH
    prev = jnp.concatenate([shift0[:, None].astype(xr.dtype), xr[:, :-1]], axis=1)
    xs = xr + (prev - xr) * lp['shift_mu']
    r, k, v, wd, ad, gd = jnp.split(xs, [RW, 2 * RW, 3 * RW, 3 * RW + DECAY_RANK, 3 * RW + DECAY_RANK + A_RANK], axis=-1)
    w_log = -jax.nn.softplus(-(lp['w0'] + jnp.tanh(wd) @ lp['w2'])) - 0.5
    decay = jnp.exp(-jnp.exp(w_log.astype(jnp.float32)))
    a = jax.nn.sigmoid(lp['a0'] + ad @ lp['a2'])
    gate = jax.nn.sigmoid(gd) @ lp['g2']
    heads = lambda t: t.reshape(B, T, H, N)
    kk = heads(k * lp['k_k']).astype(jnp.float32)
    kk = kk / jnp.maximum(jnp.sqrt(jnp.sum(kk * kk, axis=-1, keepdims=True)), 1e-12)
    k = k * (1 + (a - 1) * lp['k_a'])
    r_h, k_h, v_h, a_h = heads(r), heads(k), heads(v), heads(a)
    tmaj = lambda t: jnp.moveaxis(t.astype(jnp.float32), 1, 0)

    def step(S, inp):
        r_t, w_t, k_t, v_t, a_t, b_t = inp
        sa = jnp.einsum('bhij,bhj->bhi', S, a_t)
        S = S * w_t[:, :, None, :] + sa[..., None] * b_t[:, :, None, :] + v_t[..., None] * k_t[:, :, None, :]
        return S, jnp.einsum('bhij,bhj->bhi', S, r_t)

    S, y = lax.scan(step, wkv0.astype(jnp.float32),
                    (tmaj(r_h), tmaj(heads(decay)), tmaj(k_h), tmaj(v_h), tmaj(-kk), tmaj(kk * a_h)))
    y = jnp.moveaxis(y, 0, 1)
    mu = jnp.mean(y, axis=-1, keepdims=True)
    var = jnp.mean(jnp.square(y - mu), axis=-1, keepdims=True)
    y = ((y - mu) * lax.rsqrt(var + GN_EPS)).reshape(B, T, RW) * lp['ln_w'] + lp['ln_b']
    bonus = jnp.sum(r_h * k_h * lp['r_k'], axis=-1, keepdims=True) * v_h
    y = (y + bonus.reshape(B, T, RW).astype(jnp.float32)) * gate
    return y.astype(xr.dtype), S, xr[:, -1]

def trunk_layer(x, pe, lp, past_kv, win_buf, wkv0, shift0, n_keep_win):
    B, T = x.shape[0], x.shape[1]
    G = NSA_KV_HEADS
    q_pos0 = past_kv.shape[1]
    h = rmsnorm(x, lp['norm_mix'])
    z = h @ lp['w_in']
    c1 = Q_COLS
    c2 = c1 + KV_COLS
    c3 = c2 + WIN_COLS
    c4 = c3 + GATE_COLS
    q, kv_new, kw_new, gl, xr = jnp.split(z, [c1, c2, c3, c4], axis=-1)
    q = q.reshape(B, T, NSA_HEADS, HEAD_DIM)
    kv_new = kv_new.reshape(B, T, 4, G, HEAD_DIM)
    kw_new = kw_new.reshape(B, T, 2, G, HEAD_DIM)
    gl = gl.reshape(B, T, NSA_HEADS, 3)
    kv_full = jnp.concatenate([past_kv.astype(kv_new.dtype), kv_new], axis=1)
    w_rows = jnp.concatenate([win_buf.astype(kw_new.dtype), kw_new], axis=1)
    kw_pad = jnp.pad(w_rows, ((0, 0), (WINDOW - win_buf.shape[1], 0), (0, 0), (0, 0), (0, 0)))
    o_nsa = nsa_mixer(q, gl, kv_full, kw_pad, q_pos0, lp)
    o_rwkv, wkv, shift = rwkv_mixer(xr, shift0, wkv0, lp)
    x = x + jnp.concatenate([o_nsa, o_rwkv], axis=-1) @ lp['w_out']
    hf = rmsnorm(x, lp['norm_ffn'])
    x = x + (jax.nn.silu(hf @ lp['w_gate']) * (hf @ lp['w_up'])) @ lp['w_down']
    pg = jax.nn.sigmoid(rmsnorm(x, lp['norm_ple']) @ lp['w_ple_gate'])
    x = x + pg * (pe @ lp['w_ple'])
    new_win = w_rows[:, w_rows.shape[1] - n_keep_win:]
    return x, kv_new, new_win, wkv, shift

def setup_inputs(seed: int = 0) -> dict:
    key = jax.random.key(seed)
    keys = iter(jax.random.split(key, 64))
    nrm = lambda shape, scale: jax.random.normal(next(keys), shape, jnp.float32) * scale
    gain = lambda shape: 1.0 + nrm(shape, 0.1)
    n_pages = PAST_LEN // PAGE_SIZE
    n_phys = (DEC_BATCH * n_pages * 5) // 4
    w_buf = min(WINDOW, PAST_LEN)
    G, RW = NSA_KV_HEADS, RWKV_WIDTH
    page_table = jax.random.permutation(next(keys), n_phys)[:DEC_BATCH * n_pages]
    page_table = page_table.reshape(DEC_BATCH, n_pages).astype(jnp.int32)
    return {
        'x_prompt': nrm((BATCH, SEQ, D_MODEL), 1.0),
        'x_sample': nrm((DEC_BATCH, DEC_SEQ, D_MODEL), 1.0),
        'p_prompt': nrm((DEPTH, BATCH, SEQ, PLE_DIM), 1.0),
        'p_sample': nrm((DEPTH, DEC_BATCH, DEC_SEQ, PLE_DIM), 1.0),
        'cache_kv': nrm((DEPTH, n_phys, PAGE_SIZE, 4, G, HEAD_DIM), 1.0),
        'cache_win': nrm((DEPTH, DEC_BATCH, w_buf, 2, G, HEAD_DIM), 1.0),
        'state_wkv': nrm((DEPTH, DEC_BATCH, RWKV_HEADS, HEAD_DIM, HEAD_DIM), 0.3),
        'state_shift': nrm((DEPTH, DEC_BATCH, RWKV_PROJ), 1.0),
        'page_table': page_table,
        'norm_mix': gain((DEPTH, D_MODEL)),
        'w_in': nrm((DEPTH, D_MODEL, IN_COLS), D_MODEL ** -0.5),
        'q_norm': gain((DEPTH, HEAD_DIM)),
        'k_norm': gain((DEPTH, 3, HEAD_DIM)),
        'cmp_pe': nrm((DEPTH, 2, CMP_BLOCK, HEAD_DIM), 0.1),
        'cmp_w1': nrm((DEPTH, 2, CMP_BLOCK * HEAD_DIM, CMP_HIDDEN), (CMP_BLOCK * HEAD_DIM) ** -0.5),
        'cmp_b1': nrm((DEPTH, 2, CMP_HIDDEN), 0.01),
        'cmp_w2': nrm((DEPTH, 2, CMP_HIDDEN, HEAD_DIM), CMP_HIDDEN ** -0.5),
        'cmp_b2': nrm((DEPTH, 2, HEAD_DIM), 0.01),
        'shift_mu': jax.random.uniform(next(keys), (DEPTH, RWKV_PROJ), jnp.float32),
        'w0': jax.random.uniform(next(keys), (DEPTH, RW), jnp.float32, -6.0, 0.0),
        'w2': nrm((DEPTH, DECAY_RANK, RW), 0.1),
        'a0': nrm((DEPTH, RW), 0.1),
        'a2': nrm((DEPTH, A_RANK, RW), 0.1),
        'g2': nrm((DEPTH, GATE_RANK, RW), GATE_RANK ** -0.5),
        'k_k': 0.85 + nrm((DEPTH, RW), 0.05),
        'k_a': 1.0 + nrm((DEPTH, RW), 0.05),
        'r_k': nrm((DEPTH, RWKV_HEADS, HEAD_DIM), 0.1),
        'ln_w': gain((DEPTH, RW)),
        'ln_b': nrm((DEPTH, RW), 0.01),
        'w_out': nrm((DEPTH, D_MODEL, D_MODEL), D_MODEL ** -0.5),
        'norm_ffn': gain((DEPTH, D_MODEL)),
        'w_gate': nrm((DEPTH, D_MODEL, FFN_HIDDEN), D_MODEL ** -0.5),
        'w_up': nrm((DEPTH, D_MODEL, FFN_HIDDEN), D_MODEL ** -0.5),
        'w_down': nrm((DEPTH, FFN_HIDDEN, D_MODEL), FFN_HIDDEN ** -0.5),
        'norm_ple': gain((DEPTH, D_MODEL)),
        'w_ple_gate': nrm((DEPTH, D_MODEL, D_MODEL), D_MODEL ** -0.5),
        'w_ple': nrm((DEPTH, PLE_DIM, D_MODEL), PLE_DIM ** -0.5),
    }

def reference(x_prompt, x_sample, p_prompt, p_sample, cache_kv, cache_win, state_wkv, state_shift,
              page_table, norm_mix, w_in, q_norm, k_norm, cmp_pe, cmp_w1, cmp_b1, cmp_w2, cmp_b2,
              shift_mu, w0, w2, a0, a2, g2, k_k, k_a, r_k, ln_w, ln_b, w_out, norm_ffn, w_gate,
              w_up, w_down, norm_ple, w_ple_gate, w_ple):
    B, T = x_prompt.shape[0], x_prompt.shape[1]
    DB = x_sample.shape[0]
    G = NSA_KV_HEADS
    past_len = page_table.shape[1] * cache_kv.shape[2]
    dt = x_prompt.dtype
    empty_kv = jnp.zeros((B, 0, 4, G, HEAD_DIM), dt)
    empty_win = jnp.zeros((B, 0, 2, G, HEAD_DIM), dt)
    zero_wkv = jnp.zeros((B, RWKV_HEADS, HEAD_DIM, HEAD_DIM), jnp.float32)
    zero_shift = jnp.zeros((B, RWKV_PROJ), dt)
    xp, xs = x_prompt, x_sample
    kv_p, kv_s, win_p, win_s, wkv_p, wkv_s, sh_p, sh_s = [], [], [], [], [], [], [], []
    for i in range(DEPTH):
        lp = dict(norm_mix=norm_mix[i], w_in=w_in[i], q_norm=q_norm[i], k_norm=k_norm[i],
                  cmp_pe=cmp_pe[i], cmp_w1=cmp_w1[i], cmp_b1=cmp_b1[i], cmp_w2=cmp_w2[i], cmp_b2=cmp_b2[i],
                  shift_mu=shift_mu[i], w0=w0[i], w2=w2[i], a0=a0[i], a2=a2[i], g2=g2[i],
                  k_k=k_k[i], k_a=k_a[i], r_k=r_k[i], ln_w=ln_w[i], ln_b=ln_b[i], w_out=w_out[i],
                  norm_ffn=norm_ffn[i], w_gate=w_gate[i], w_up=w_up[i], w_down=w_down[i],
                  norm_ple=norm_ple[i], w_ple_gate=w_ple_gate[i], w_ple=w_ple[i])
        xp, kv1, win1, wkv1, sh1 = trunk_layer(xp, p_prompt[i], lp, empty_kv, empty_win, zero_wkv,
                                              zero_shift, min(WINDOW, T))
        past = cache_kv[i][page_table].reshape(DB, past_len, 4, G, HEAD_DIM)
        xs, kv2, win2, wkv2, sh2 = trunk_layer(xs, p_sample[i], lp, past, cache_win[i], state_wkv[i],
                                              state_shift[i], cache_win.shape[2])
        kv_p.append(kv1); kv_s.append(kv2); win_p.append(win1); win_s.append(win2)
        wkv_p.append(wkv1); wkv_s.append(wkv2); sh_p.append(sh1); sh_s.append(sh2)
    return (xp, xs, jnp.stack(kv_p), jnp.stack(kv_s), jnp.stack(win_p), jnp.stack(win_s),
            jnp.stack(wkv_p), jnp.stack(wkv_s), jnp.stack(sh_p), jnp.stack(sh_s))


_drawn_inputs = setup_inputs


def setup_inputs(seed=0):
    import zlib

    import numpy as np

    out = dict(_drawn_inputs(seed))
    spreads = {}
    factors = {'q_norm': 5.919,
     'k_norm': 6.223,
     'cmp_pe': 3.108,
     'cmp_b1': 8.0,
     'cmp_b2': 8.0,
     'ln_b': 8.0,
     'norm_ple': 3.613}
    for name, (base, spread) in spreads.items():
        noise = np.random.default_rng([zlib.crc32(name.encode()), seed]).standard_normal(out[name].shape)
        drawn = base * np.exp(spread * noise) if base else spread * noise
        out[name] = __import__('jax').numpy.asarray(drawn.astype(out[name].dtype))
    for name, factor in factors.items():
        out[name] = (out[name] * factor).astype(out[name].dtype)
    return out
```

```python
from contextlib import ExitStack

import concourse.bass as bass
from concourse import mybir

F32 = mybir.dt.float32
I32 = mybir.dt.int32
ALU = mybir.AluOpType
ACT = mybir.ActivationFunctionType
AX = mybir.AxisListType

P = 128
D = 1024
KD = D // P
T = 512
QT = T // P
NB = 8
NT = T + NB
HALF = NT // 2
HD = 64
NH = 8
G = 2
R = NH // G
PAST = 256
PAGE = 128
NPG = NB * PAST // PAGE
KV = 768
GATES = 3 * NH
XRC = 1792
XF = XRC // P
C_KV, C_GATE, C_XR = 512, 1280, 1304
STRIDE, BLOCK = 16, 32
NCP = (T - BLOCK) // STRIDE + 1
NCD = (PAST + 1 - BLOCK) // STRIDE + 1
FF = 2816
FT = FF // P
PLE = 256
PAIR_SEQ = NB * P + T // 2
XCMP = G * PAIR_SEQ + BLOCK // 2
NWIN = XCMP // 8 - 1
NEG = -1e30
EPS = 1e-6
GN_EPS = 64e-5
HALFS = ((0, HALF), (HALF, NT))
LEVELS = (2, 4, 8, 16, 32, 64)

ROWS = {}
for _name, _n in (("norm_mix", 8), ("norm_ffn", 8), ("norm_ple", 8), ("shift_mu", XF), ("w0", 4), ("a0", 4),
                  ("k_k", 4), ("k_a", 4), ("r_k", 4), ("ln_w", 4), ("ln_b", 4), ("q_norm", 1), ("k_norm", 3),
                  ("cmp_b1", 4), ("cmp_b2", 2)):
    ROWS[_name] = (sum(n for _, n in ROWS.values()), _n)
NROWS = sum(n for _, n in ROWS.values())


class Points:

    def __init__(self, known=None):
        self.known = known
        self.new = {}


class Steps:

    def __init__(self, name, points, sem):
        self.name, self.points, self.sem = name, points, sem
        self.count = {}
        self.key = None

    def stage(self, name):
        self.key = f"{self.name}_{name}"
        self.done = self.sem(self.key)
        self.count.setdefault(self.key, 0)

    def tick(self, *names):
        self.count[self.key] += 1
        for n in names:
            self.points.new[n] = (self.key, self.count[self.key])
        return 1

    def landed(self, key, *names):
        self.count[key] = self.count.get(key, 0) + 16
        for n in names:
            self.points.new[n] = (key, self.count[key])
        return 16

    def latest(self):
        return self.done, self.count[self.key]

    def end(self, phase):
        self.points.new[f"end:{phase}:{self.name}"] = (self.key, self.count[self.key])


def build(nc, a, out, points):
    ctx = ExitStack()
    with ctx:
        sems = {}

        def sem(name):
            if name not in sems:
                sems[name] = ctx.enter_context(nc.semaphore(name))
            return sems[name]

        def sb(name, shape, dt=F32):
            return ctx.enter_context(nc.sbuf_tensor(name, shape, dt))

        xT = sb("xT", [P, KD, NT])
        hT = sb("hT", [P, KD, NT])
        oT = hT
        NSLOT = 3
        ring = sb("ring", [P, NSLOT, 8 * 256])
        XR = sb("XR", [P, XF, 1 + NT])
        par_rows = sb("par_rows", [P, P])
        par = sb("par", [P, NROWS])
        ident = sb("ident", [P, P])
        ones = sb("ones", [P, P])
        blk = sb("blk", [P, P])
        causal = sb("causal", [P, P])
        us_ui = sb("us_ui", [P, 2, P])
        level = sb("level", [P, 7, P])
        level1T = sb("level1T", [P, P])
        cmp_keep = sb("cmp_keep", [P, QT, NCP])
        cmp_add = sb("cmp_add", [P, QT, NCP])
        dec_add = sb("dec_add", [64, NB, 16])
        dec_own = sb("dec_own", [64, NB])
        eps = sb("eps", [P, 2])
        qgain = sb("qgain", [P, 1])
        ka1 = sb("ka1", [P, 4])
        rstd = sb("rstd", [P, NT])
        sq = sb("sq", [P, 2, NT])
        ARENA = 29952
        arena = sb("arena", [P, ARENA])

        class Place:

            def __init__(self, at=0):
                self.at = at

            def __call__(self, n, rows=P):
                self.at += n
                assert self.at <= ARENA, self.at
                return arena[0:rows, self.at - n:self.at]

        new = Place()
        zkv = new(5 * KV).rearrange("p (t n) -> p t n", t=5)
        gate = new(5 * GATES).rearrange("p (t n) -> p t n", t=5)
        late = Place(new.at)
        xstage = Place(new.at)(5 * D).rearrange("p (t n) -> p t n", t=5)
        xcmp = new(2 * XCMP).rearrange("p (v n) -> p v n", v=2)
        csq = late(NPG * P).rearrange("p (t n) -> p t n", t=NPG)
        pbuf = late(4 * T).rearrange("p (i n) -> p i n", i=4)
        ptb = late(2 * T).rearrange("p (i n) -> p i n", i=2)
        assert late.at <= new.at
        diag = new(4 * P).rearrange("p (i n) -> p i n", i=4)
        qT = new(R * NT).rearrange("p (r n) -> p r n", r=R)
        kT = new(2 * T).rearrange("p (v n) -> p v n", v=2)
        over = Place(new.at)
        pairs = new(10 * 512).rearrange("p (s w a d) -> p s w a d", s=10, w=4, a=2)
        kTd = over(2 * NB * 257).rearrange("p (v b n) -> p v b n", v=2, b=NB)
        assert over.at <= new.at
        over = Place(new.at)
        cache = new(2 * NPG * 256).rearrange("p (v g n) -> p v g n", v=2, g=NPG)
        ptcb = over(2 * NH * P).rearrange("p (i h n) -> p i h n", i=2, h=NH)
        kn = new(2 * QT * P).rearrange("p (v t n) -> p v t n", v=2, t=QT)
        dkn = new(256, NB)
        w2c = new(256).rearrange("p (v m d) -> p v m d", v=2, m=2)
        krs = new(16).rearrange("p (v t g) -> p v t g", v=2, t=QT)
        drs = new(4, NB)
        crs = new(32).rearrange("p (t g) -> p t g", g=G)
        pcm = new(NH * NCP).rearrange("p (h n) -> p h n", h=NH)
        st = new(96)
        stc = new(32)
        scol = new(16)
        sst = new(XRC, 9)
        att_end = new.at
        spare = oT[:, 4:8, :].rearrange("p f n -> p (f n)")
        gel = spare[:, 0:640].rearrange("p (m n) -> p m n", m=2)
        kc, kcn, vc = spare[:, 640:800], spare[:, 800:960], spare[:, 960:1120]
        vcd, vcp = spare[:, 1120:1248], spare[:, 1248:1376]
        qall = spare[:, 1376:1440]
        qb = spare[:, 1440:1952].rearrange("p (b n) -> p b n", b=NB)
        pcs = pbuf[0:64, 2, 0:P]

        new = Place()
        gg = new(4 * NT).rearrange("p (f n) -> p f n", f=4)
        AR = new(4 * QT * 256).rearrange("p (f c n) -> p f c n", f=4, c=QT)
        BH = new(4 * T).rearrange("p (f n) -> p f n", f=4)
        KH = new(4 * T).rearrange("p (f n) -> p f n", f=4)
        tm = new(4 * QT * T).rearrange("p (w c n) -> p w c n", w=4, c=QT)
        rwkv_w, g2w = new(T), new(T)
        S = new(2048).rearrange("p (i j) -> p i j", i=32)
        S2 = new(1024).rearrange("p (i j) -> p i j", i=16)
        ydt = new(T, NB)
        Hs = new(256).rearrange("p (f n) -> p f n", f=4)
        Hm = new(256).rearrange("p (f n) -> p f n", f=4)
        Hd = new(256).rearrange("p (f n) -> p f n", f=4)
        em, ec, ecr = (new(4 * QT).rearrange("p (f c) -> p f c", f=4) for _ in range(3))
        dv = new(6 * 4 * NB).rearrange("p (w f b) -> p w f b", w=6, f=4)
        dvr = new(6 * HD).rearrange("p (w n) -> p w n", w=6)
        vrow, sa, yd = new(32), new(32), new(32)
        over = Place(new.at)
        Tsb = new(2 * T).rearrange("p (g n) -> p g n", g=2)
        TTsb = new(2 * T).rearrange("p (g n) -> p g n", g=2)
        Xs = new(2 * T).rearrange("p (g n) -> p g n", g=2)
        U, ApT, SA, MV = new(T), new(T).rearrange("p (f n) -> p f n", f=4), new(T), new(T)
        tmp = [over(NT) for _ in range(9)]
        assert over.at <= new.at
        wkt = Tsb[0:HD, 0, :]
        rwkv_end = new.at
        LN = XR[:, 0:4, :].rearrange("p f n -> p (f n)")[:, 0:2048].rearrange("p (h n) -> p h n", h=8)
        MQ = XR[:, 4:8, :].rearrange("p f n -> p (f n)")[:, 0:2048].rearrange("p (h n) -> p h n", h=8)
        dvt = XR[0:NB, 0:6, :].rearrange("p f n -> p (f n)")[:, 0:6 * T].rearrange("p (w n) -> p w n", w=6)
        shf = par_rows

        new = Place()
        actv = new(FT * NT).rearrange("p (f n) -> p f n", f=FT)
        silu = new(2 * NT).rearrange("p (i n) -> p i n", i=2)
        pst = new(5 * PLE).rearrange("p (t n) -> p t n", t=5)
        pT = new(2 * NT).rearrange("p (k n) -> p k n", k=2)
        new = Place()
        pep = new(KD * NT).rearrange("p (f n) -> p f n", f=KD)
        ot = new(5 * D).rearrange("p (t n) -> p t n", t=5)
        ssf = sb("ssf", [P, XF, NB])
        page_sb = sb("page_sb", [1, NPG], I32)

        psum = ctx.enter_context(nc.psum_tensor("psum", [P, 8, 512], F32))

        def col(name, i=0, lo=0, hi=P):
            c = ROWS[name][0] + i
            return par[lo:hi, c:c + 1]

        scratch = nc.dram_tensor("dec_scratch", (NB, NH, 6, HD), F32).ap()
        scratch_y = nc.dram_tensor("dec_scratch_y", (NB, T), F32).ap()

        chunks = [("kv", i) for i in range(3)] + [("gates", 0)] + [("q", i) for i in range(2)]
        chunks += [("xr", i) for i in range(7)] + [("w1", i) for i in range(4)]
        chunks += [("wo", i) for i in range(4)]
        for i in range(11):
            chunks += [("wg", i), ("wu", i)]
        chunks += [("wd", i, j) for i in range(4) for j in range(3)]
        chunks += [("wp", 0)] + [("wpg", i) for i in range(4)]
        slot_of = {c: i % NSLOT for i, c in enumerate(chunks)}

        def slot(c, n=256):
            return ring[:, slot_of[c], :].rearrange("p (k n) -> p k n", n=n)

        bank_user = {}
        turn = {"banks": list(range(8)), "next": 0}

        def bank(name):
            return psum[:, points.known[("bank", name)] if points.known else 0, :]

        def at(name):
            key, value = points.known[name] if points.known else ("pe_load", 0)
            return sem(key), value

        steps = {n: Steps(n, points, sem) for n in ("pe", "dve", "act", "pool", "sp")}
        block = ctx.enter_context(nc.Block())

        @block.sync
        def _(eng):
            sp = steps["sp"]

            def kp(w, c0, n, k0=0, kn=KD):
                return w[k0 * P:(k0 + kn) * P, c0:c0 + n].rearrange("(k p) n -> p k n", p=P)

            for i, c in enumerate(chunks):
                if i >= NSLOT:
                    eng.wait_ge(*at(("used", chunks[i - NSLOT])))
                dst, key, mark = slot(c), f"ring{i % NSLOT}", ("got", c)
                kind = c[0]
                if kind == "kv":
                    eng.dma_start(dst, kp(a["w_in"][0], C_KV + 256 * c[1], 256))\
                        .then_inc(sem(key), sp.landed(key, mark))
                elif kind == "gates":
                    eng.dma_start(dst[:, :, 0:GATES], kp(a["w_in"][0], C_GATE, GATES))\
                        .then_inc(sem(key), sp.landed(key, mark))
                elif kind == "q":
                    for j in range(2):
                        for g in range(G):
                            eng.dma_start(dst[:, :, j * P + g * HD:j * P + (g + 1) * HD], kp(a["w_in"][0], (g * R + 2 * c[1] + j) * HD, HD))\
                                .then_inc(sem(key), sp.landed(key, mark))
                elif kind == "xr":
                    eng.dma_start(dst, kp(a["w_in"][0], C_XR + 256 * c[1], 256))\
                        .then_inc(sem(key), sp.landed(key, mark))
                elif kind == "w1":
                    v, part = c[1] // 2, c[1] % 2
                    eng.dma_start(dst, kp(a["cmp_w1"][0, v], 0, 256, part * 8))\
                        .then_inc(sem(key), sp.landed(key, mark))
                elif kind == "wo":
                    for g in range(G):
                        src = a["w_out"][0, g * R * HD:(g + 1) * R * HD, 256 * c[1]:256 * c[1] + 256]
                        eng.dma_start(dst[g * HD:(g + 1) * HD, 0:4, :], src.rearrange("(r d) n -> d r n", d=HD))\
                            .then_inc(sem(key), sp.landed(key, mark))
                    eng.dma_start(dst[:, 4:8, :], kp(a["w_out"][0], 256 * c[1], 256, 4, 4))\
                        .then_inc(sem(key), sp.landed(key, mark))
                elif kind in ("wg", "wu"):
                    w = a["w_gate" if kind == "wg" else "w_up"][0]
                    eng.dma_start(dst, kp(w, 256 * c[1], 256))\
                        .then_inc(sem(key), sp.landed(key, mark))
                elif kind == "wd":
                    kn = min(8, FT - 8 * c[2])
                    eng.dma_start(dst[:, 0:kn, :], kp(a["w_down"][0], 256 * c[1], 256, 8 * c[2], kn))\
                        .then_inc(sem(key), sp.landed(key, mark))
                elif kind == "wp":
                    eng.dma_start(slot(c, D)[:, 0:2, :], kp(a["w_ple"][0], 0, D, 0, 2))\
                        .then_inc(sem(key), sp.landed(key, mark))
                else:
                    eng.dma_start(dst, kp(a["w_ple_gate"][0], 256 * c[1], 256))\
                        .then_inc(sem(key), sp.landed(key, mark))

        @block.gpsimd
        def _(eng):
            pl = steps["pool"]
            pl.stage("init")
            eng.memset(ident[:, :], 0.0)\
                .then_inc(pl.done, pl.tick())
            eng.memset(ones[:, :], 1.0)\
                .then_inc(pl.done, pl.tick())
            eng.memset(eps[:, 0:1], EPS)\
                .then_inc(pl.done, pl.tick())
            eng.memset(eps[:, 1:2], GN_EPS)\
                .then_inc(pl.done, pl.tick("eps"))
            eng.memset(par_rows[:, :], 0.0)\
                .then_inc(pl.done, pl.tick("par_zero"))
            eng.wait_ge(*pl.latest())
            eng.affine_select(out=ident[:, :], in_=ident[:, :], compare_op=ALU.not_equal, fill=1.0, base=0, pattern=[[-1, P]], channel_multiplier=1)\
                .then_inc(pl.done, pl.tick("ident"))
            eng.dma_start(page_sb[:, :], a["page_table"].rearrange("b n -> (b n)").rearrange("(o n) -> o n", o=1))\
                .then_inc(sem("load_page"), pl.landed("load_page", "page"))
            eng.dma_start(w2c, a["cmp_w2"][0].rearrange("v (m p) d -> p v m d", p=P))\
                .then_inc(sem("load_w2c"), pl.landed("load_w2c", "w2c"))
            eng.memset(blk[:, :], 1.0)\
                .then_inc(pl.done, pl.tick())
            eng.memset(causal[:, :], 0.0)\
                .then_inc(pl.done, pl.tick())
            eng.memset(us_ui[:, :, :], 1.0)\
                .then_inc(pl.done, pl.tick())
            eng.memset(level[:, :, :], 0.0)\
                .then_inc(pl.done, pl.tick())
            eng.memset(level1T[:, :], 0.0)\
                .then_inc(pl.done, pl.tick())
            eng.memset(cmp_keep[:, :, :], 1.0)\
                .then_inc(pl.done, pl.tick())
            eng.memset(dec_add[:, :, :], 0.0)\
                .then_inc(pl.done, pl.tick())
            eng.memset(dec_own[:, :], 1.0)\
                .then_inc(pl.done, pl.tick())
            eng.memset(XR[:, :, 0:1], 0.0)\
                .then_inc(pl.done, pl.tick())
            eng.wait_ge(*pl.latest())
            bv = blk[:, :].rearrange("p (s n) -> p s n", s=2)
            eng.affine_select(out=bv, in_=bv, compare_op=ALU.is_ge, fill=0.0, base=0, pattern=[[-HD, 2], [0, HD]], channel_multiplier=1)\
                .then_inc(pl.done, pl.tick())
            lv = {}
            for i, n in enumerate((1,) + LEVELS):
                lv[i] = level[:, i, :].rearrange("p (j s n) -> p j s n", s=2, n=n)
                eng.memset(lv[i][:, :, 0, :], 1.0)\
                    .then_inc(pl.done, pl.tick())
            lt = level1T[:, :].rearrange("p (j s) -> p j s", s=2)
            eng.memset(lt[:, :, 1:2], 1.0)\
                .then_inc(pl.done, pl.tick())
            eng.affine_select(out=causal[:, :], in_=causal[:, :], compare_op=ALU.is_ge, fill=NEG, base=0, pattern=[[-1, P]], channel_multiplier=1)\
                .then_inc(pl.done, pl.tick())
            eng.affine_select(out=us_ui[:, 0, :], in_=us_ui[:, 0, :], compare_op=ALU.is_gt, fill=0.0, base=0, pattern=[[1, P]], channel_multiplier=-1)\
                .then_inc(pl.done, pl.tick())
            eng.affine_select(out=us_ui[:, 1, :], in_=us_ui[:, 1, :], compare_op=ALU.is_ge, fill=0.0, base=0, pattern=[[1, P]], channel_multiplier=-1)\
                .then_inc(pl.done, pl.tick())
            eng.affine_select(out=cmp_keep[:, :, :], in_=cmp_keep[:, :, :], compare_op=ALU.is_ge, fill=0.0, base=-(BLOCK - 1), pattern=[[P, QT], [-STRIDE, NCP]], channel_multiplier=1)\
                .then_inc(pl.done, pl.tick())
            eng.affine_select(out=dec_add[:, :, :], in_=dec_add[:, :, :], compare_op=ALU.is_ge, fill=NEG, base=0, pattern=[[-NH, NB], [0, 16]], channel_multiplier=1)\
                .then_inc(pl.done, pl.tick())
            eng.affine_select(out=dec_own[:, :], in_=dec_own[:, :], compare_op=ALU.is_ge, fill=0.0, base=0, pattern=[[-NH, NB]], channel_multiplier=1)\
                .then_inc(pl.done, pl.tick())
            eng.wait_ge(*pl.latest())
            eng.affine_select(out=dec_add[:, :, :], in_=dec_add[:, :, :], compare_op=ALU.is_ge, fill=NEG, base=NH - 1, pattern=[[NH, NB], [0, 16]], channel_multiplier=-1)\
                .then_inc(pl.done, pl.tick())
            eng.affine_select(out=dec_own[:, :], in_=dec_own[:, :], compare_op=ALU.is_ge, fill=0.0, base=NH - 1, pattern=[[NH, NB]], channel_multiplier=-1)\
                .then_inc(pl.done, pl.tick())
            eng.affine_select(out=bv, in_=bv, compare_op=ALU.is_ge, fill=0.0, base=HD - 1, pattern=[[HD, 2], [0, HD]], channel_multiplier=-1)\
                .then_inc(pl.done, pl.tick())
            for i, n in enumerate((1,) + LEVELS):
                eng.affine_select(out=lv[i], in_=lv[i], compare_op=ALU.is_ge, fill=0.0, base=-n, pattern=[[-2 * n, P // (2 * n)], [0, 2], [0, n]], channel_multiplier=1)\
                    .then_inc(pl.done, pl.tick())
            eng.affine_select(out=lt, in_=lt, compare_op=ALU.is_equal, fill=0.0, base=0, pattern=[[-2, P // 2], [0, 2]], channel_multiplier=1)\
                .then_inc(pl.done, pl.tick())
            eng.tensor_scalar(cmp_add[:, :, :], cmp_keep[:, :, :], -NEG, NEG, ALU.mult, ALU.add)\
                .then_inc(pl.done, pl.tick())
            eng.wait_ge(*pl.latest())
            for i, n in enumerate((1,) + LEVELS):
                eng.affine_select(out=lv[i], in_=lv[i], compare_op=ALU.is_ge, fill=0.0, base=2 * n - 1, pattern=[[2 * n, P // (2 * n)], [0, 2], [0, n]], channel_multiplier=-1)\
                    .then_inc(pl.done, pl.tick())
            eng.affine_select(out=dec_add[:, :, :], in_=dec_add[:, :, :], compare_op=ALU.is_ge, fill=NEG, base=NCD - 1, pattern=[[0, NB], [-1, 16]], channel_multiplier=0)\
                .then_inc(pl.done, pl.tick("masks"))
            pl.stage("att")
            eng.wait_ge(*at("page"))
            for i in range(NPG):
                pg = eng.value_load(page_sb[0:1, i:i + 1], min_val=0, max_val=a["cache_kv"].shape[1] - 1)
                src = a["cache_kv"][0, bass.ds(pg, 1)].rearrange("o (t a) v g d -> (o t) (v g) a d", a=2)
                s, h = i // 2, i % 2
                for par_ in range(2):
                    eng.dma_start(pairs[h * 64:(h + 1) * 64, s, :, par_, :], src[:, 0:4, par_, :])\
                        .then_inc(sem("load_pairs"), pl.landed("load_pairs"))
                src = a["cache_kv"][0, bass.ds(pg, 1)].rearrange("o t v g d -> (o t) (v g d)")
                eng.dma_start(cache[:, 0, i, :], src[:, 256:512])\
                    .then_inc(sem("load_cache"), pl.landed("load_cache"))
                src = a["cache_win"][0, s, h * P:(h + 1) * P].rearrange("t v g d -> t (v g d)")
                eng.dma_start(cache[:, 1, i, :], src)\
                    .then_inc(sem("load_cache"), pl.landed("load_cache", "cache"))
            for b in range(NB):
                eng.dma_start(out["win_sample"][0, b, 0:PAST - 1].rearrange("t v g d -> t (v g d)"), a["cache_win"][0, b, 1:PAST].rearrange("t v g d -> t (v g d)"))\
                    .then_inc(sem("store_att"), pl.landed("store_att"))
            eng.wait_ge(*at("zkv"))
            for t in range(QT):
                eng.dma_start(out["kv_prompt"][0, 0, t * P:(t + 1) * P].rearrange("t v g d -> t (v g d)"), zkv[:, t, 0:512])\
                    .then_inc(sem("store_kv"), pl.landed("store_kv", "kv_stored"))
            for t in range(QT):
                eng.dma_start(out["win_prompt"][0, 0, t * P:(t + 1) * P].rearrange("t v g d -> t (v g d)"), zkv[:, t, 512:768])\
                    .then_inc(sem("store_att"), pl.landed("store_att"))
            eng.dma_start(out["kv_sample"][0, :, 0].rearrange("b v g d -> b (v g d)"), zkv[0:NB, QT, 0:512])\
                .then_inc(sem("store_att"), pl.landed("store_att"))
            eng.dma_start(out["win_sample"][0, :, PAST - 1].rearrange("b v g d -> b (v g d)"), zkv[0:NB, QT, 512:768])\
                .then_inc(sem("store_att"), pl.landed("store_att"))
            eng.wait_ge(*at("kv_stored"))
            for h in range(2):
                src = out["kv_prompt"][0, 0, h * 256:(h + 1) * 256].rearrange("(t a) v g d -> t (v g) a d", a=2)
                for par_ in range(2):
                    eng.dma_start(pairs[:, NB + h, :, par_, :], src[:, 0:4, par_, :])\
                        .then_inc(sem("load_pairs"), pl.landed("load_pairs", "pairs"))
            eng.wait_ge(*at("pairs_turned"))
            for v in range(2):
                eng.dma_start(shf[v * 16:(v + 1) * 16, :], a["cmp_pe"][0, v].rearrange("(l a) d -> l (a d)", a=2))\
                    .then_inc(sem("load_pe"), pl.landed("load_pe", "pe_rows"))
            eng.wait_ge(*at("gates"))
            for b in range(NB):
                eng.dma_start(scol[b * NH:(b + 1) * NH, 0:3], gate[b:b + 1, QT, :].rearrange("p (h n) -> p h n", n=3))\
                    .then_inc(sem("load_gd"), pl.landed("load_gd", "gd"))
            eng.wait_ge(*at("shift_rows"))
            eng.dma_start(out["shift_prompt"][0], sst[0:1, :])\
                .then_inc(sem("store_att"), pl.landed("store_att"))
            eng.dma_start(out["shift_sample"][0], sst[1:9, :])\
                .then_inc(sem("store_att"), pl.landed("store_att", "stored_att"))
            for f in (12, 13, 0, 4, 8, 1, 5, 9, 2, 6, 10, 3, 7, 11):
                d = kn.rearrange("p v t n -> p (v t n)")[:, 0:NT]
                eng.wait_ge(*at(f"xrl{f // 4}"))
                eng.wait_ge(*at("kT1"))
                eng.wait_ge(*pl.latest())
                eng.tensor_tensor(d[:, 0:T], XR[:, f, 0:T], XR[:, f, 1:1 + T], ALU.subtract)\
                    .then_inc(pl.done, pl.tick())
                eng.tensor_tensor(d[:, T:NT], ssf[:, f, :], XR[:, f, 1 + T:1 + NT], ALU.subtract)\
                    .then_inc(pl.done, pl.tick())
                eng.wait_ge(*pl.latest())
                eng.tensor_scalar(d, d, col("shift_mu", f), None, ALU.mult)\
                    .then_inc(pl.done, pl.tick())
                eng.wait_ge(*pl.latest())
                eng.tensor_tensor(XR[:, f, 1:1 + NT], XR[:, f, 1:1 + NT], d, ALU.add)\
                    .then_inc(pl.done, pl.tick(f"sh{f}"))
            pl.stage("rwkv")
            eng.wait_ge(*at("end:att:pe"))
            eng.wait_ge(*at("end:att:dve"))
            eng.wait_ge(*at("end:att:act"))
            eng.wait_ge(*at("stored_att"))
            eng.wait_ge(*at("sh11"))
            eng.dma_start(rwkv_w[0:HD, :], a["w2"][0])\
                .then_inc(sem("load_lr"), pl.landed("load_lr"))
            eng.dma_start(rwkv_w[HD:P, :], a["a2"][0])\
                .then_inc(sem("load_lr"), pl.landed("load_lr"))
            eng.dma_start(g2w, a["g2"][0])\
                .then_inc(sem("load_lr"), pl.landed("load_lr", "lr_w"))
            eng.dma_start(S.rearrange("p i j -> p (i j)"), a["state_wkv"][0].rearrange("b h (s i) j -> (b h s) (i j)", s=2))\
                .then_inc(sem("load_S"), pl.landed("load_S", "S"))
            eng.wait_ge(*at("dvt"))
            for b in range(NB):
                eng.dma_start(scratch[b].rearrange("h w d -> w h d").rearrange("(o w) h d -> o w h d", o=1), dvt[b:b + 1].rearrange("p w (h d) -> p w h d", h=NH))\
                    .then_inc(sem("store_dv"), pl.landed("store_dv", "dv_stored"))
            eng.wait_ge(*at("dv_stored"))
            for s in range(2):
                eng.dma_start(dvr[s:P:2, :, :], scratch.rearrange("b h w d -> (b h) w d"))\
                    .then_inc(sem("load_dv"), pl.landed("load_dv", "dvr"))
            for h in range(2):
                eng.dma_start(vrow[h:P:2, :], scratch[:, :, 5, h * 32:(h + 1) * 32].rearrange("b h i -> (b h) i"))\
                    .then_inc(sem("load_dv"), pl.landed("load_dv", "dvr"))
            eng.wait_ge(*at("dvr"))
            eng.wait_ge(*at("S"))

            def rows_of(v, h):
                return v[:, h * 16:(h + 1) * 16].unsqueeze(2).to_broadcast([P, 16, HD])

            def over_rows(w):
                return dvr[:, w, :].unsqueeze(1).to_broadcast([P, 16, HD])

            for h in range(2):
                Sh = S[:, h * 16:(h + 1) * 16, :]
                eng.tensor_tensor(S2, Sh, over_rows(1), ALU.mult)\
                    .then_inc(pl.done, pl.tick(f"sa_in{h}"))
                eng.wait_ge(*at(f"sa_sum{h}"))
                eng.tensor_tensor(Sh, Sh, over_rows(0), ALU.mult)\
                    .then_inc(pl.done, pl.tick())
                eng.tensor_tensor(S2, rows_of(sa, h), over_rows(2), ALU.mult)\
                    .then_inc(pl.done, pl.tick())
                eng.wait_ge(*pl.latest())
                eng.tensor_tensor(Sh, Sh, S2, ALU.add)\
                    .then_inc(pl.done, pl.tick())
                eng.wait_ge(*pl.latest())
                eng.tensor_tensor(S2, rows_of(vrow, h), over_rows(3), ALU.mult)\
                    .then_inc(pl.done, pl.tick())
                eng.wait_ge(*pl.latest())
                eng.tensor_tensor(Sh, Sh, S2, ALU.add)\
                    .then_inc(pl.done, pl.tick())
                eng.wait_ge(*pl.latest())
                eng.tensor_tensor(S2, Sh, over_rows(4), ALU.mult)\
                    .then_inc(pl.done, pl.tick(f"yd_in{h}"))
                eng.wait_ge(*at(f"yd_sum{h}"))
            eng.wait_ge(*pl.latest())
            eng.dma_start(out["wkv_sample"][0].rearrange("b h (s i) j -> (b h s) (i j)", s=2), S.rearrange("p i j -> p (i j)"))\
                .then_inc(sem("store_rwkv"), pl.landed("store_rwkv"))
            eng.dma_start(scratch_y.rearrange("b (q i) -> (b q) i", i=32), yd)\
                .then_inc(sem("store_y"), pl.landed("store_y", "y_stored"))
            eng.wait_ge(*at("y_stored"))
            eng.dma_start(ydt, scratch_y)\
                .then_inc(sem("load_y"), pl.landed("load_y", "ydt"))
            eng.wait_ge(*at("wkt"))
            eng.dma_start(out["wkv_prompt"][0, 0].rearrange("h i j -> i h j"), wkt.rearrange("p (h j) -> p h j", h=NH))\
                .then_inc(sem("store_rwkv"), pl.landed("store_rwkv", "stored_rwkv"))
            pl.end("rwkv")
            eng.wait_ge(*at("end:rwkv:pe"))
            eng.wait_ge(*at("end:rwkv:dve"))
            eng.wait_ge(*at("end:rwkv:act"))
            eng.wait_ge(*at("stored_rwkv"))
            eng.wait_ge(*at("ydt"))
            for t in range(QT):
                eng.dma_start(pst[:, t, :], a["p_prompt"][0, 0, t * P:(t + 1) * P, :])\
                    .then_inc(sem("load_p"), pl.landed("load_p", "p"))
            eng.dma_start(pst[0:NB, QT, :], a["p_sample"][0, :, 0, :])\
                .then_inc(sem("load_p"), pl.landed("load_p", "p"))
            for t in range(QT):
                eng.wait_ge(*at(f"y{t}"))
                eng.dma_start(out["y_prompt"][0, t * P:(t + 1) * P, :], ot[:, t, :])\
                    .then_inc(sem("store_end"), pl.landed("store_end"))
            eng.wait_ge(*at(f"y{QT}"))
            eng.dma_start(out["y_sample"][:, 0, :], ot[0:NB, QT, :])\
                .then_inc(sem("store_end"), pl.landed("store_end", "stored_all"))
            eng.wait_ge(*at("stored_all"))

        def place(h):
            return h // 4 * 4 + h % 2 * 2 + h // 2 % 2

        @block.tensor
        def _(eng):
            pe = steps["pe"]
            mm = eng.matmul

            def banks(b):
                turn["banks"], turn["next"] = list(b), 0

            def open_(name, fixed=None):
                which = fixed
                if which is None:
                    which = turn["banks"][turn["next"] % len(turn["banks"])]
                    turn["next"] += 1
                if which in bank_user:
                    eng.wait_ge(*at(("free", bank_user[which])))
                bank_user[which] = name
                points.new[("bank", name)] = which
                return psum[:, which, :]

            def turn_(dst, src, n=P):
                return mm(dst, src, ident[0:n, 0:n], is_transpose=True, start=True, stop=True)

            pe.stage("load")
            eng.wait_ge(*at("x"))
            eng.wait_ge(*at("ident"))
            for k in range(KD):
                ps = open_(f"x{k}")
                for t in range(QT):
                    turn_(ps[:, t * P:(t + 1) * P], xstage[:, t, k * P:(k + 1) * P])\
                        .then_inc(pe.done, pe.tick(*([f"x{k}"] if t == QT - 1 else ())))
            ps = open_("xd")
            for k in range(KD):
                turn_(ps[:, k * NB:(k + 1) * NB], xstage[0:NB, QT, k * P:(k + 1) * P], NB)\
                    .then_inc(pe.done, pe.tick(*(["xd"] if k == KD - 1 else ())))
            eng.wait_ge(*at("par"))
            ps = open_("par_t")
            turn_(ps[:, 0:P], par_rows[:, :], P)\
                .then_inc(pe.done, pe.tick("par_t"))
            eng.wait_ge(*at("ss"))
            ps = open_("ss_t")
            for f in range(XF):
                turn_(ps[:, f * NB:(f + 1) * NB], sst[0:NB, f * P:(f + 1) * P], NB)\
                    .then_inc(pe.done, pe.tick(*(["ss_t"] if f == XF - 1 else ())))

            def mean_square(which):
                pe.stage("norm")
                pss = [open_(f"{which}ms{h}") for h in range(2)]
                for k in range(KD):
                    eng.wait_ge(*at(f"{which}sq{k}"))
                    for h, (lo, hi) in enumerate(HALFS):
                        mm(pss[h][:, 0:hi - lo], ones[:, :], sq[:, k % 2, lo:hi], start=(k == 0), stop=(k == KD - 1))\
                            .then_inc(pe.done, pe.tick(f"{which}ms{h}" if k == KD - 1 else f"{which}sqd{k}"))

            def dense(group, c, j, rhs, nk=KD, k0=0, start=True, stop=True, pss=None, used=False):
                w = slot(c)
                pss = pss or [open_(f"{group}h{h}") for h in range(2)]
                for h, (lo, hi) in enumerate(HALFS):
                    for k in range(nk):
                        names = []
                        if stop and k == nk - 1:
                            names.append(f"{group}h{h}")
                        if used and k == nk - 1 and h == 1:
                            names.append(("used", c))
                        mm(pss[h][:, 0:hi - lo], w[:, k, j * P:(j + 1) * P], rhs[:, k0 + k, lo:hi], start=(start and k == 0), stop=(stop and k == nk - 1))\
                            .then_inc(pe.done, pe.tick(*names))

            mean_square("mix")
            pe.stage("proj")
            eng.wait_ge(*at("mixh"))
            for c in range(3):
                eng.wait_ge(*at(("got", ("kv", c))))
                w = slot(("kv", c))
                for t in range(QT + 1):
                    m = P if t < QT else NB
                    ps = open_(f"kv{c}_{t}")
                    for k in range(KD):
                        names = [f"kv{c}_{t}"] if k == KD - 1 else []
                        if k == KD - 1 and t == QT:
                            names.append(("used", ("kv", c)))
                        mm(ps[0:m, 0:256], hT[:, k, t * P:t * P + m], w[:, k, :], start=(k == 0), stop=(k == KD - 1))\
                            .then_inc(pe.done, pe.tick(*names))
            eng.wait_ge(*at(("got", ("gates", 0))))
            w = slot(("gates", 0))
            ps = open_("gates_p")
            for t in range(QT + 1):
                m = P if t < QT else NB
                for k in range(KD):
                    last = t == QT and k == KD - 1
                    mm(ps[0:m, t * GATES:(t + 1) * GATES], hT[:, k, t * P:t * P + m], w[:, k, 0:GATES], start=(k == 0), stop=(k == KD - 1))\
                        .then_inc(pe.done, pe.tick(*(["gates_p", ("used", ("gates", 0))] if last else [])))
            for c in range(2):
                eng.wait_ge(*at(("got", ("q", c))))
                for j in range(2):
                    dense(f"q{2 * c + j}", ("q", c), j, hT, used=(j == 1))
            for c in range(7):
                eng.wait_ge(*at(("got", ("xr", c))))
                for j in range(2):
                    dense(f"xr{2 * c + j}", ("xr", c), j, hT, used=(j == 1))
            pe.stage("att")
            eng.wait_ge(*at("masks"))
            for r in range(R):
                eng.wait_ge(*at(f"qsq{r}"))
                for h, (lo, hi) in enumerate(HALFS):
                    ps = open_(f"qms{r}h{h}")
                    mm(ps[:, 0:hi - lo], blk[:, :], sq[:, r % 2, lo:hi], start=True, stop=True)\
                        .then_inc(pe.done, pe.tick(f"qms{r}h{h}"))
            for f in range(XF):
                if f % 4 == 0:
                    ps = open_(f"xrl{f // 4}")
                    eng.wait_ge(*at(f"xr_s{min(f + 3, XF - 1)}"))
                turn_(ps[0:9, (f % 4) * P:(f % 4 + 1) * P], XR[:, f, T:T + 9], P)\
                    .then_inc(pe.done, pe.tick(*([f"xrl{f // 4}"] if f % 4 == 3 or f == XF - 1 else ())))
            for v in range(2):
                eng.wait_ge(*at(f"kn{v}"))
                ps = open_(f"kT{v}")
                for t in range(QT):
                    turn_(ps[:, t * P:(t + 1) * P], kn[:, v, t, :], P)\
                        .then_inc(pe.done, pe.tick(*([f"kT{v}"] if t == QT - 1 else ())))
            eng.wait_ge(*at("pairs"))
            for v in range(2):
                for g in range(G):
                    for s0 in (0, 4, 8):
                        n = min(4, 10 - s0)
                        ps = open_(f"pair{v}{g}{s0}")
                        for s in range(n):
                            turn_(ps[:, s * P:(s + 1) * P], pairs[:, s0 + s, 2 * v + g, :, :].rearrange("p a d -> p (a d)"), P)\
                                .then_inc(pe.done, pe.tick(*([f"pair{v}{g}{s0}", "pairs_turned"] if s == n - 1 else ())))
            eng.wait_ge(*at("pe_rows"))
            ps = open_("pe_t")
            turn_(ps[:, 0:32], shf[0:32, :], 32)\
                .then_inc(pe.done, pe.tick("pe_t"))
            eng.wait_ge(*at("xcmp"))
            for v in range(2):
                pss = [open_(f"conv{v}{m}") for m in range(2)]
                xv = xcmp[:, v, :].rearrange("p (w i) -> p w i", i=8)
                for l in range(16):
                    c = ("w1", 2 * v + l // 8)
                    eng.wait_ge(*at(("got", c)))
                    for m in range(2):
                        names = [("used", c)] if l % 8 == 7 and m == 1 else []
                        if l == 15:
                            names.append(f"conv{v}{m}")
                        mm(pss[m][:, 0:NWIN], slot(c)[:, l % 8, m * P:(m + 1) * P], xv[:, l // 8:l // 8 + NWIN, l % 8], start=(l == 0), stop=(l == 15))\
                            .then_inc(pe.done, pe.tick(*names))
                eng.wait_ge(*at(f"gel{v}"))
                eng.wait_ge(*at("w2c"))
                ps = open_(f"cmp{v}")
                for g in range(G):
                    for m in range(2):
                        mm(ps[g * HD:(g + 1) * HD, 0:160], w2c[:, v, m, :], gel[:, m, g * 160:(g + 1) * 160], start=(m == 0), stop=(m == 1))\
                            .then_inc(pe.done, pe.tick(f"cmp{v}"))
            eng.wait_ge(*at("kcsq"))
            ps = open_("kcms")
            mm(ps[:, 0:160], blk[:, :], sq[:, 0, 0:160], start=True, stop=True)\
                .then_inc(pe.done, pe.tick("kcms"))
            eng.wait_ge(*at("vc"))
            ps = open_("vc_t")
            turn_(ps[:, 0:P], vc[:, 0:P])\
                .then_inc(pe.done, pe.tick())
            turn_(ps[0:NCP, P:2 * P], vc[:, P:P + NCP], P)\
                .then_inc(pe.done, pe.tick("vc_t"))
            for v in range(2):
                for i0 in range(0, NPG, 4):
                    ps = open_(f"ck{v}_{i0}")
                    for i in range(4):
                        eng.wait_ge(*at(f"ckn{v}"))
                        turn_(ps[:, i * P:(i + 1) * P], cache[:, v, i0 + i, 0:P], P)\
                            .then_inc(pe.done, pe.tick(*([f"ck{v}_{i0}"] if i == 3 else ())))
                eng.wait_ge(*at(f"dkn{v}"))
                ps = open_(f"dk{v}")
                turn_(ps[:, 0:NB], dkn[:, v * P:(v + 1) * P], NB)\
                    .then_inc(pe.done, pe.tick(f"dk{v}"))
            eng.wait_ge(*at("qb"))
            for v in range(2):
                eng.wait_ge(*at(f"kTd{v}"))
                ps = open_(f"sd{v}")
                for b in range(NB):
                    mm(ps[0:64, 0:257], qb[:, b, :], kTd[:, v, b, :], start=(b == 0), stop=(b == NB - 1))\
                        .then_inc(pe.done, pe.tick(*([f"sd{v}"] if b == NB - 1 else [])))
            eng.wait_ge(*at("kcn"))
            ps = open_("sdc")
            mm(ps[0:64, 0:P], qall, kcn[:, 0:P], start=True, stop=True)\
                .then_inc(pe.done, pe.tick("sdc"))
            eng.wait_ge(*at("pdc"))
            ps = open_("ptc")
            mm(ps[:, 0:64], pcs[:, 0:P], diag[0:64, 2, 0:64], start=True, stop=True)\
                .then_inc(pe.done, pe.tick("ptc"))
            od = open_("od")
            eng.wait_ge(*at("ptcs"))
            eng.wait_ge(*at("vcd"))
            mm(od[:, 0:64], vcd, ptb[:, 0, 448:512], start=True, stop=True, skip_group_check=True)\
                .then_inc(pe.done, pe.tick())
            for v in range(2):
                eng.wait_ge(*at(f"pd{v}"))
                ps = open_(f"ptd{v}")
                for t in range(2):
                    mm(ps[:, t * 64:(t + 1) * 64], pbuf[0:64, v, t * P:(t + 1) * P], diag[0:64, v, 0:64], start=True, stop=True)\
                        .then_inc(pe.done, pe.tick())
                mm(ps[0:NB, 128:192], st[0:64, 64 + v * NB:64 + (v + 1) * NB], diag[0:64, v, 0:64], start=True, stop=True)\
                    .then_inc(pe.done, pe.tick(f"ptd{v}"))
                eng.wait_ge(*at(f"ptds{v}"))
                mm(od[:, 0:64], zkv[0:NB, QT, 384 + 256 * v:512 + 256 * v], ptb[0:NB, v, 128:192], start=False, stop=True, skip_group_check=True)\
                    .then_inc(pe.done, pe.tick())
                for b in range(NB):
                    for t in range(2):
                        last = v == 1 and b == NB - 1 and t == 1
                        mm(od[:, b * NH:(b + 1) * NH], cache[:, v, 2 * b + t, P:2 * P], ptb[:, v, t * 64 + b * NH:t * 64 + (b + 1) * NH], start=False, stop=True, skip_group_check=True)\
                            .then_inc(pe.done, pe.tick(*(["od"] if last else [])))
            banks(range(6))
            units = [(qt, r, g, v) for qt in range(QT) for r in range(R) for g in range(G) for v in range(2)]
            PER = len(units) // QT
            AHEAD = 3

            def scores(i):
                qt, r, g, v = units[i]
                n = (qt + 1) * P
                ps = open_(f"s{i}")
                mm(ps[:, 0:n], qT[g * HD:(g + 1) * HD, r, qt * P:(qt + 1) * P], kT[g * HD:(g + 1) * HD, v, 0:n], start=True, stop=True)\
                    .then_inc(pe.done, pe.tick(f"s{i}"))

            def block_scores(qt):
                ps = open_(f"sc{qt}")
                for g in range(G):
                    if g:
                        eng.wait_ge(*pe.latest())
                    for r in range(R):
                        h = g * R + r
                        mm(ps[:, h * NCP:(h + 1) * NCP], qT[g * HD:(g + 1) * HD, r, qt * P:(qt + 1) * P], kcn[g * HD:(g + 1) * HD, P:P + NCP], start=True, stop=True)\
                            .then_inc(pe.done, pe.tick(f"sc{qt}"))

            def block_turn(qt):
                eng.wait_ge(*at(f"pc{qt}"))
                for h2 in range(2):
                    ps = open_(f"ptc{qt}_{h2}")
                    for i in range(4):
                        turn_(ps[0:NCP, i * P:(i + 1) * P], pcm[:, h2 * 4 + i, :], P)\
                            .then_inc(pe.done, pe.tick(f"ptc{qt}_{h2}"))

            def turned(i):
                eng.wait_ge(*at(f"p{i}"))
                ps = open_(f"pt{i}")
                for j in range(units[i][0] + 1):
                    mm(ps[:, j * P:(j + 1) * P], pbuf[:, i % 4, j * P:(j + 1) * P], diag[:, i % 4, :], start=True, stop=True)\
                        .then_inc(pe.done, pe.tick(f"pt{i}"))

            def values(i):
                qt, r, g, v = units[i]
                if i % PER == 0:
                    open_(f"o{qt}", 6 + qt % 2)
                o = psum[g * HD:(g + 1) * HD, 6 + qt % 2, r * P:(r + 1) * P]
                if v == 0:
                    eng.wait_ge(*at(f"ptcs{qt}_{g}"))
                    mm(o, vcp[0:NCP, g * HD:(g + 1) * HD], ptcb[0:NCP, qt % 2, g * R + r, :], start=True, stop=True, skip_group_check=True)\
                        .then_inc(pe.done, pe.tick())
                eng.wait_ge(*at(f"pts{i}"))
                for j in range(qt + 1):
                    mm(o, zkv[:, j, 384 + 256 * v + g * HD:384 + 256 * v + (g + 1) * HD], ptb[:, i % 2, j * P:(j + 1) * P], start=False, stop=True, skip_group_check=True)\
                        .then_inc(pe.done, pe.tick(f"pv{i}", f"o{qt}"))

            eng.wait_ge(*at("kTs"))
            eng.wait_ge(*at("qTs"))
            block_scores(0)
            for i in range(AHEAD):
                scores(i)
            block_turn(0)
            for i in range(len(units)):
                qt, u = divmod(i, PER)
                if qt + 1 < QT and u == 8:
                    block_scores(qt + 1)
                if qt + 1 < QT and u == 12:
                    block_turn(qt + 1)
                if i + AHEAD < len(units):
                    scores(i + AHEAD)
                turned(i)
                if i:
                    values(i - 1)
            values(len(units) - 1)
            pe.end("att")

            pe.stage("rwkv")
            eng.wait_ge(*at("end:att:dve"))
            eng.wait_ge(*at("end:att:act"))
            eng.wait_ge(*at("stored_att"))
            banks(range(8))
            lr = rwkv_w
            eng.wait_ge(*at("lr_w"))
            eng.wait_ge(*at("lr_in"))
            for f in range(4):
                for h, (lo, hi) in enumerate(HALFS):
                    ps = open_(f"dec{f}h{h}")
                    mm(ps[:, 0:hi - lo], lr[0:HD, f * P:(f + 1) * P], XR[0:HD, 12, 1 + lo:1 + hi], start=True, stop=True)\
                        .then_inc(pe.done, pe.tick(f"dec{f}h{h}"))
                for h, (lo, hi) in enumerate(HALFS):
                    ps = open_(f"av{f}h{h}")
                    mm(ps[:, 0:hi - lo], lr[HD:P, f * P:(f + 1) * P], XR[HD:P, 12, 1 + lo:1 + hi], start=True, stop=True)\
                        .then_inc(pe.done, pe.tick(f"av{f}h{h}"))
                for h, (lo, hi) in enumerate(HALFS):
                    ps = open_(f"gg{f}h{h}")
                    mm(ps[:, 0:hi - lo], g2w[:, f * P:(f + 1) * P], XR[:, 13, 1 + lo:1 + hi], start=True, stop=True)\
                        .then_inc(pe.done, pe.tick(f"gg{f}h{h}"))
                eng.wait_ge(*at(f"kksq{f}"))
                for h, (lo, hi) in enumerate(HALFS):
                    ps = open_(f"kks{f}h{h}")
                    mm(ps[:, 0:hi - lo], blk[:, :], sq[:, 0, lo:hi], start=True, stop=True)\
                        .then_inc(pe.done, pe.tick(f"kks{f}h{h}"))
                eng.wait_ge(*at(f"bon{f}"))
                for h, (lo, hi) in enumerate(HALFS):
                    ps = open_(f"bs{f}h{h}")
                    mm(ps[:, 0:hi - lo], blk[:, :], sq[:, 1, lo:hi], start=True, stop=True)\
                        .then_inc(pe.done, pe.tick(f"bs{f}h{h}"))
                eng.wait_ge(*at(f"tmf{f}"))
                for w in range(4):
                    ps = open_(f"tm{f}{w}")
                    src = [None, BH[:, f, :], KH[:, f, :], XR[:, 8 + f, 1:1 + T]][w]
                    for c in range(QT):
                        s_ = AR[:, f, c, 0:P] if w == 0 else src[:, c * P:(c + 1) * P]
                        turn_(ps[:, c * P:(c + 1) * P], s_, P)\
                            .then_inc(pe.done, pe.tick(*([f"tm{f}{w}"] if c == QT - 1 else ())))
            eng.wait_ge(*at("dv"))
            for w in range(6):
                ps = open_(f"dv{w}")
                for f in range(4):
                    turn_(ps[0:NB, f * P:(f + 1) * P], dv[:, w, f, :], P)\
                        .then_inc(pe.done, pe.tick(*([f"dv{w}"] if f == 3 else ())))
            pe.end("prep")
            eng.wait_ge(*at("end:prep:dve"))
            eng.wait_ge(*at("end:prep:act"))
            banks(range(4))
            for c in range(QT):
                for hg in range(2):
                    for name, lhs in (("ln", BH), ("mq", KH)):
                        for i in range(2):
                            ps = open_(f"{name}{c}{hg}{i}")
                            lo = i * HD
                            for fp in range(2):
                                f = hg * 2 + fp
                                mm(ps[:, fp * 256:(fp + 1) * 256], lhs[lo:lo + HD, f, c * P:(c + 1) * P], AR[lo:lo + HD, f, c, :], start=True, stop=True)\
                                    .then_inc(pe.done, pe.tick(f"{name}{c}{hg}{i}"))
                    ps = open_(f"l{c}{hg}")
                    for i in range(2):
                        if i:
                            eng.wait_ge(*pe.latest())
                        lo = i * HD
                        for fp in range(2):
                            f = hg * 2 + fp
                            mm(ps[:, (i * 2 + fp) * P:(i * 2 + fp + 1) * P], AR[lo:lo + HD, f, c, 0:P], BH[lo:lo + HD, f, c * P:(c + 1) * P], start=True, stop=True)\
                                .then_inc(pe.done, pe.tick(f"l{c}{hg}"))
                Tb, TTb = {}, {}
                for hg in range(2):
                    Tb[hg] = open_(f"T{c}{hg}", 4 + hg)
                    TTb[hg] = open_(f"TT{c}{hg}", 6 + hg)
                    eng.wait_ge(*at(f"Ts{c}{hg}_1"))
                    mm(Tb[hg], ident[:, :], Tsb[:, hg, :], start=True, stop=True, skip_group_check=True)\
                        .then_inc(pe.done, pe.tick())
                    eng.wait_ge(*at(f"TTs{c}{hg}_1"))
                    mm(TTb[hg], ident[:, :], TTsb[:, hg, :], start=True, stop=True, skip_group_check=True)\
                        .then_inc(pe.done, pe.tick())
                for n in LEVELS:
                    for hg in range(2):
                        ps = open_(f"X{c}{hg}_{n}")
                        eng.wait_ge(*at(f"Ts{c}{hg}_{n // 2}"))
                        for i in range(4):
                            mm(ps[:, i * P:(i + 1) * P], LN[:, hg * 4 + i, 0:P], Tsb[:, hg, i * P:(i + 1) * P], start=True, stop=True)\
                                .then_inc(pe.done, pe.tick(f"X{c}{hg}_{n}"))
                    for hg in range(2):
                        eng.wait_ge(*at(f"Xs{c}{hg}_{n}"))
                        eng.wait_ge(*at(f"TTs{c}{hg}_{n // 2}"))
                        if n < 64:
                            for i in range(4):
                                s_ = slice(i * P, (i + 1) * P)
                                mm(Tb[hg][:, s_], TTsb[:, hg, s_], Xs[:, hg, s_], start=False, stop=True, skip_group_check=True)\
                                    .then_inc(pe.done, pe.tick(f"T{c}{hg}_{n}"))
                        for i in range(4):
                            s_ = slice(i * P, (i + 1) * P)
                            mm(TTb[hg][:, s_], Xs[:, hg, s_], TTsb[:, hg, s_], start=False, stop=True, skip_group_check=True)\
                                .then_inc(pe.done, pe.tick(f"TT{c}{hg}_{n}"))
                ps = open_(f"mv{c}")
                for h in range(NH):
                    mm(ps[:, h * HD:(h + 1) * HD], MQ[:, place(h), 0:P], tm[:, 3, c, h * HD:(h + 1) * HD], start=True, stop=True)\
                        .then_inc(pe.done, pe.tick(f"mv{c}"))
                ps = open_(f"ap{c}")
                eng.wait_ge(*at(f"TTs{c}0_64"))
                eng.wait_ge(*at(f"TTs{c}1_64"))
                for h in range(NH):
                    lo = (h % 2) * HD
                    mm(ps[lo:lo + HD, (h // 2) * P:(h // 2 + 1) * P], tm[:, 0, c, h * HD:(h + 1) * HD], TTsb[:, h // 4, (place(h) % 4) * P:(place(h) % 4 + 1) * P], start=True, stop=True)\
                        .then_inc(pe.done, pe.tick(f"ap{c}"))
                eng.wait_ge(*at(f"mvs{c}"))
                ps = open_(f"u{c}")
                for h in range(NH):
                    mm(ps[:, h * HD:(h + 1) * HD], TTsb[:, h // 4, (place(h) % 4) * P:(place(h) % 4 + 1) * P], MV[:, h * HD:(h + 1) * HD], start=True, stop=True)\
                        .then_inc(pe.done, pe.tick(f"u{c}"))
                eng.wait_ge(*at(f"aps{c}"))
                eng.wait_ge(*at(f"Hm{c}"))
                ps = open_(f"sa{c}")
                for h in (0, 2, 4, 6, 1, 3, 5, 7):
                    if h == 1:
                        eng.wait_ge(*pe.latest())
                    lo, f = (h % 2) * HD, h // 2
                    mm(ps[:, h * HD:(h + 1) * HD], ApT[lo:lo + HD, f, :], Hm[lo:lo + HD, f, :], start=True, stop=True)\
                        .then_inc(pe.done, pe.tick(f"sa{c}"))
                eng.wait_ge(*at(f"sas{c}"))
                ps = open_(f"H{c}")
                for h in range(NH):
                    lo, f = (h % 2) * HD, h // 2
                    o = ps[lo:lo + HD, f * HD:(f + 1) * HD]
                    mm(o, tm[:, 1, c, h * HD:(h + 1) * HD], SA[:, h * HD:(h + 1) * HD], start=True, stop=False)\
                        .then_inc(pe.done, pe.tick())
                    mm(o, tm[:, 2, c, h * HD:(h + 1) * HD], tm[:, 3, c, h * HD:(h + 1) * HD], start=False, stop=True)\
                        .then_inc(pe.done, pe.tick(f"H{c}"))
                ps = open_(f"y{c}p")
                for h in range(NH):
                    lo, f = (h % 2) * HD, h // 2
                    o = ps[lo:lo + HD, f * P:(f + 1) * P]
                    mm(o, Hm[lo:lo + HD, f, :], AR[lo:lo + HD, f, c, P:2 * P], start=True, stop=False)\
                        .then_inc(pe.done, pe.tick())
                    mm(o, SA[:, h * HD:(h + 1) * HD], LN[:, place(h), P:2 * P], start=False, stop=False)\
                        .then_inc(pe.done, pe.tick())
                    mm(o, tm[:, 3, c, h * HD:(h + 1) * HD], MQ[:, place(h), P:2 * P], start=False, stop=True)\
                        .then_inc(pe.done, pe.tick(f"y{c}p"))
            eng.wait_ge(*at("Hend"))
            ps = open_("wk")
            for f in range(4):
                turn_(ps[0:HD, f * P:(f + 1) * P], Hs[:, f, :], P)\
                    .then_inc(pe.done, pe.tick(*(["wk"] if f == 3 else ())))
            eng.wait_ge(*at("ydt"))
            ps = open_("yd")
            for f in range(4):
                turn_(ps[:, f * NB:(f + 1) * NB], ydt[:, f * P:(f + 1) * P], NB)\
                    .then_inc(pe.done, pe.tick(*(["yd"] if f == 3 else ())))
            banks(range(8))
            for f in range(4):
                eng.wait_ge(*at(f"yall"))
                for h, (lo, hi) in enumerate(HALFS):
                    ps = open_(f"gm{f}h{h}")
                    mm(ps[:, 0:hi - lo], blk[:, :], oT[:, 4 + f, lo:hi], start=True, stop=True)\
                        .then_inc(pe.done, pe.tick(f"gm{f}h{h}"))
                eng.wait_ge(*at(f"gsq{f}"))
                for h, (lo, hi) in enumerate(HALFS):
                    ps = open_(f"gv{f}h{h}")
                    mm(ps[:, 0:hi - lo], blk[:, :], sq[:, f % 2, lo:hi], start=True, stop=True)\
                        .then_inc(pe.done, pe.tick(f"gv{f}h{h}"))
            pe.end("rwkv")

            pe.stage("ffn")
            eng.wait_ge(*at("end:rwkv:dve"))
            eng.wait_ge(*at("end:rwkv:act"))
            eng.wait_ge(*at("end:rwkv:pool"))
            eng.wait_ge(*at("stored_rwkv"))
            for c in range(4):
                eng.wait_ge(*at(("got", ("wo", c))))
                for j in range(2):
                    dense(f"wo{2 * c + j}", ("wo", c), j, oT, used=(j == 1))
            mean_square("ffn")
            pe.stage("ffn")
            eng.wait_ge(*at("ffnh"))
            for c in range(11):
                eng.wait_ge(*at(("got", ("wg", c))))
                eng.wait_ge(*at(("got", ("wu", c))))
                for j in range(2):
                    dense(f"wg{2 * c + j}", ("wg", c), j, hT, used=(j == 1))
                    dense(f"wu{2 * c + j}", ("wu", c), j, hT, used=(j == 1))
            eng.wait_ge(*at(f"actv{FT - 1}"))
            for c in range(4):
                pss = [[open_(f"wd{2 * c + j}h{h}") for h in range(2)] for j in range(2)]
                for i in range(3):
                    eng.wait_ge(*at(("got", ("wd", c, i))))
                    for j in range(2):
                        dense(f"wd{2 * c + j}", ("wd", c, i), j, actv, min(8, FT - 8 * i), 8 * i, start=(i == 0),
                              stop=(i == 2), pss=pss[j], used=(j == 1))
            eng.wait_ge(*at("p"))
            for k in range(2):
                ps = open_(f"pe{k}")
                for t in range(QT):
                    turn_(ps[:, t * P:(t + 1) * P], pst[:, t, k * P:(k + 1) * P], P)\
                        .then_inc(pe.done, pe.tick(*([f"pe{k}"] if t == QT - 1 else ())))
            ps = open_("pd")
            for k in range(2):
                turn_(ps[:, k * NB:(k + 1) * NB], pst[0:NB, QT, k * P:(k + 1) * P], NB)\
                    .then_inc(pe.done, pe.tick("pd"))
            mean_square("ple")
            pe.stage("ffn")
            eng.wait_ge(*at("pTs"))
            eng.wait_ge(*at(("got", ("wp", 0))))
            w = slot(("wp", 0), D)
            for m in range(KD):
                for h, (lo, hi) in enumerate(HALFS):
                    ps = open_(f"wp{m}h{h}")
                    for k in range(2):
                        names = [f"wp{m}h{h}"] if k == 1 else []
                        if m == KD - 1 and h == 1 and k == 1:
                            names.append(("used", ("wp", 0)))
                        mm(ps[:, 0:hi - lo], w[:, k, m * P:(m + 1) * P], pT[:, k, lo:hi], start=(k == 0), stop=(k == 1))\
                            .then_inc(pe.done, pe.tick(*names))
            eng.wait_ge(*at("pleh"))
            for c in range(4):
                eng.wait_ge(*at(("got", ("wpg", c))))
                for j in range(2):
                    dense(f"wpg{2 * c + j}", ("wpg", c), j, hT, used=(j == 1))
            for t in range(QT + 1):
                m = P if t < QT else NB
                for k2 in range(2):
                    ps = open_(f"out{t}{k2}")
                    for k in range(4):
                        eng.wait_ge(*at(f"xfin{k2 * 4 + k}"))
                        turn_(ps[0:m, k * P:(k + 1) * P], xT[:, k2 * 4 + k, t * P:t * P + m], P)\
                            .then_inc(pe.done, pe.tick(*([f"out{t}{k2}"] if k == 3 else ())))


        @block.scalar
        def _(eng):
            ac = steps["act"]

            def squares(which, xs):
                ac.stage("norm")
                for k in range(KD):
                    eng.wait_ge(*at(xs(k)))
                    if k >= 2:
                        eng.wait_ge(*at(f"{which}sqd{k - 2}"))
                    eng.activation(sq[:, k % 2, :], xT[:, k, :], ACT.Square)\
                        .then_inc(ac.done, ac.tick(f"{which}sq{k}"))
                for h, (lo, hi) in enumerate(HALFS):
                    eng.wait_ge(*at(f"{which}ms{h}"))
                    eng.activation(rstd[:, lo:hi], bank(f"{which}ms{h}")[:, 0:hi - lo], ACT.Sqrt, scale=1.0 / D, bias=eps[:, 0:1])\
                        .then_inc(ac.done, ac.tick(f"{which}rt{h}", ("free", f"{which}ms{h}")))

            for t in range(QT):
                eng.dma_start(xstage[:, t, :], a["x_prompt"][0, t * P:(t + 1) * P, :])\
                    .then_inc(sem("load_x"), ac.landed("load_x"))
            eng.dma_start(xstage[0:NB, QT, :], a["x_sample"][:, 0, :])\
                .then_inc(sem("load_x"), ac.landed("load_x", "x"))
            eng.wait_ge(*at("par_zero"))
            for name, (r0, n) in ROWS.items():
                src = a[name][0]
                if name in ("q_norm", "cmp_b2", "k_norm"):
                    src = src.rearrange("(r d) -> r d", r=1) if name == "q_norm" else src
                    for g in range(G):
                        eng.dma_start(par_rows[r0:r0 + n, g * HD:(g + 1) * HD], src)\
                            .then_inc(sem("load_par"), ac.landed("load_par", "par"))
                    continue
                if name == "r_k":
                    src = src.rearrange("(f h) d -> f (h d)", h=2)
                elif name == "cmp_b1":
                    src = src.rearrange("v (m c) -> (v m) c", c=P)
                else:
                    src = src.rearrange("(f c) -> f c", c=P)
                eng.dma_start(par_rows[r0:r0 + n, :], src)\
                    .then_inc(sem("load_par"), ac.landed("load_par", "par"))
            eng.dma_start(sst[0:NB, :], a["state_shift"][0])\
                .then_inc(sem("load_ss"), ac.landed("load_ss", "ss"))
            eng.wait_ge(*at("eps"))
            squares("mix", lambda k: "xT")
            ac.stage("proj")
            for c in range(3):
                for t in range(QT + 1):
                    m = P if t < QT else NB
                    eng.wait_ge(*at(f"kv{c}_{t}"))
                    eng.activation(zkv[0:m, t, c * 256:(c + 1) * 256], bank(f"kv{c}_{t}")[0:m, 0:256], ACT.Copy)\
                        .then_inc(ac.done, ac.tick(("free", f"kv{c}_{t}"), "zkv"))
            eng.wait_ge(*at("gates_p"))
            ps = bank("gates_p")
            eng.activation(gate[:, 0:QT, :], ps[:, 0:QT * GATES].rearrange("p (t n) -> p t n", t=QT), ACT.Sigmoid)\
                .then_inc(ac.done, ac.tick())
            eng.activation(gate[0:NB, QT, :], ps[0:NB, QT * GATES:(QT + 1) * GATES], ACT.Sigmoid)\
                .then_inc(ac.done, ac.tick("gates", ("free", "gates_p")))
            for r in range(R):
                for h, (lo, hi) in enumerate(HALFS):
                    eng.wait_ge(*at(f"q{r}h{h}"))
                    eng.activation(qT[:, r, lo:hi], bank(f"q{r}h{h}")[:, 0:hi - lo], ACT.Copy)\
                        .then_inc(ac.done, ac.tick(("free", f"q{r}h{h}"), f"q_s{r}"))
            ac.stage("att")
            for r in range(R):
                eng.wait_ge(*at(f"q_s{r}"))
                eng.wait_ge(*at(f"qms{r - 2}h1" if r >= 2 else "mixms1"))
                eng.activation(sq[:, r % 2, :], qT[:, r, :], ACT.Square)\
                    .then_inc(ac.done, ac.tick(f"qsq{r}"))
            for r in range(R):
                for h, (lo, hi) in enumerate(HALFS):
                    eng.wait_ge(*at(f"qms{r}h{h}"))
                    eng.wait_ge(*at(f"q_n{r - 1}" if r else "mixh"))
                    eng.activation(rstd[:, lo:hi], bank(f"qms{r}h{h}")[:, 0:hi - lo], ACT.Sqrt, scale=1.0 / HD, bias=eps[:, 0:1])\
                        .then_inc(ac.done, ac.tick(f"qrt{r}", ("free", f"qms{r}h{h}")))
            eng.wait_ge(*at("kss"))
            eng.activation(krs, krs, ACT.Sqrt, scale=1.0 / HD, bias=eps[:, 0:1])\
                .then_inc(ac.done, ac.tick())
            eng.activation(drs, drs, ACT.Sqrt, scale=1.0 / HD, bias=eps[0:NB, 0:1])\
                .then_inc(ac.done, ac.tick("krt"))
            for v in range(2):
                eng.wait_ge(*at(f"kT{v}"))
                eng.activation(kT[:, v, :], bank(f"kT{v}"), ACT.Copy, scale=col("k_norm", 1 + v))\
                    .then_inc(ac.done, ac.tick(("free", f"kT{v}"), "kTs"))
            for v in range(2):
                for g in range(G):
                    for s0 in (0, 4, 8):
                        n = min(4, 10 - s0) * P
                        eng.wait_ge(*at(f"pair{v}{g}{s0}"))
                        col0 = g * PAIR_SEQ + s0 * P
                        eng.activation(xcmp[:, v, col0:col0 + n], bank(f"pair{v}{g}{s0}")[:, 0:n], ACT.Copy)\
                            .then_inc(ac.done, ac.tick(("free", f"pair{v}{g}{s0}")))
            eng.wait_ge(*at("pe_t"))
            eng.activation(xcmp[:, :, G * PAIR_SEQ:XCMP], bank("pe_t")[:, 0:32].rearrange("p (v n) -> p v n", v=2), ACT.Copy)\
                .then_inc(ac.done, ac.tick(("free", "pe_t"), "xcmp"))
            for v in range(2):
                for m in range(2):
                    eng.wait_ge(*at(f"cb{v}{m}"))
                    if v:
                        eng.wait_ge(*at("cmp0"))
                    eng.activation(gel[:, m, :], bank(f"conv{v}{m}")[:, 0:320], ACT.Gelu_apprx_tanh, bias=stc[:, 2 * v + m:2 * v + m + 1])\
                        .then_inc(ac.done, ac.tick(f"gel{v}", ("free", f"conv{v}{m}")))
            eng.wait_ge(*at("kcms"))
            eng.activation(kcn, bank("kcms")[:, 0:160], ACT.Sqrt, scale=1.0 / HD, bias=eps[:, 0:1])\
                .then_inc(ac.done, ac.tick("kcrt", ("free", "kcms")))
            for v in range(2):
                eng.wait_ge(*at(f"css{v}"))
                eng.activation(crs, crs, ACT.Sqrt, scale=1.0 / HD, bias=eps[:, 0:1])\
                    .then_inc(ac.done, ac.tick(f"crt{v}"))
                if v == 0:
                    eng.wait_ge(*at("pairs_turned"))
                for i0 in range(0, NPG, 4):
                    eng.wait_ge(*at(f"ck{v}_{i0}"))
                    eng.activation(kTd[:, v, i0 // 2:i0 // 2 + 2, 0:PAST], bank(f"ck{v}_{i0}").rearrange("p (b n) -> p b n", b=2), ACT.Copy, scale=col("k_norm", 1 + v))\
                        .then_inc(ac.done, ac.tick(("free", f"ck{v}_{i0}")))
                eng.wait_ge(*at(f"dk{v}"))
                eng.activation(kTd[:, v, :, PAST], bank(f"dk{v}")[:, 0:NB], ACT.Copy, scale=col("k_norm", 1 + v))\
                    .then_inc(ac.done, ac.tick(("free", f"dk{v}"), f"kTd{v}"))
            for v in range(2):
                eng.wait_ge(*at(f"sdm{v}"))
                eng.activation(pbuf[0:64, v, 0:257], bank(f"sd{v}")[0:64, 0:257], ACT.Exp, bias=st[0:64, v:v + 1], accum_out=st[0:64, 4 + v:5 + v])\
                    .then_inc(ac.done, ac.tick(f"sde{v}", ("free", f"sd{v}")))
            eng.wait_ge(*at("sdm2"))
            eng.activation(pcs, pcs, ACT.Exp, bias=st[0:64, 2:3], accum_out=st[0:64, 6:7])\
                .then_inc(ac.done, ac.tick("sde2"))
            eng.wait_ge(*at("ptc"))
            eng.activation(ptb[:, 0, 448:512], bank("ptc")[:, 0:64], ACT.Copy)\
                .then_inc(ac.done, ac.tick(("free", "ptc"), "ptcs"))
            for v in range(2):
                eng.wait_ge(*at(f"ptd{v}"))
                eng.activation(ptb[:, v, 0:128], bank(f"ptd{v}")[:, 0:128], ACT.Copy)\
                    .then_inc(ac.done, ac.tick())
                eng.activation(ptb[0:NB, v, 128:192], bank(f"ptd{v}")[0:NB, 128:192], ACT.Copy)\
                    .then_inc(ac.done, ac.tick(("free", f"ptd{v}"), f"ptds{v}"))
            PER, AHEAD = 16, 3
            UNITS = QT * PER

            def exp_unit(i):
                n = (i // PER + 1) * P
                eng.wait_ge(*at(f"sm{i}"))
                eng.wait_ge(*at("od" if i < 4 else f"pt{i - 4}"))
                eng.activation(pbuf[:, i % 4, 0:n], bank(f"s{i}")[:, 0:n], ACT.Exp, bias=st[:, i % 4:i % 4 + 1], accum_out=st[:, 8 + i % 4:9 + i % 4])\
                    .then_inc(ac.done, ac.tick(f"se{i}", ("free", f"s{i}")))

            def evac_unit(i):
                n = (i // PER + 1) * P
                eng.wait_ge(*at(f"pt{i}"))
                eng.wait_ge(*at("od" if i < 2 else f"pv{i - 2}"))
                eng.activation(ptb[:, i % 2, 0:n], bank(f"pt{i}")[:, 0:n], ACT.Copy)\
                    .then_inc(ac.done, ac.tick(f"pts{i}", ("free", f"pt{i}")))

            def block_exp(qt):
                eng.wait_ge(*at(f"scm{qt}"))
                eng.activation(pcm, pcm, ACT.Exp)\
                    .then_inc(ac.done, ac.tick(f"sce{qt}"))

            def block_evac(qt):
                for h2 in range(2):
                    eng.wait_ge(*at(f"ptc{qt}_{h2}"))
                    eng.wait_ge(*at("od" if qt < 2 else f"o{qt - 2}"))
                    eng.activation(ptcb[0:NCP, qt % 2, h2 * 4:h2 * 4 + 4, :], bank(f"ptc{qt}_{h2}")[0:NCP, :].rearrange("p (h n) -> p h n", h=4), ACT.Copy)\
                        .then_inc(ac.done, ac.tick(("free", f"ptc{qt}_{h2}"), f"ptcs{qt}_{h2}"))

            block_exp(0)
            for i in range(AHEAD):
                exp_unit(i)
            block_evac(0)
            for i in range(UNITS):
                qt, u = divmod(i, PER)
                if qt + 1 < QT and u == 9:
                    block_exp(qt + 1)
                if qt + 1 < QT and u == 12:
                    block_evac(qt + 1)
                if i + AHEAD < UNITS:
                    exp_unit(i + AHEAD)
                evac_unit(i)
            ac.end("att")

            ac.stage("rwkv")
            eng.wait_ge(*at("end:att:pe"))
            eng.wait_ge(*at("end:att:dve"))
            eng.wait_ge(*at("stored_att"))
            eng.wait_ge(*at("sh11"))
            eng.wait_ge(*at("sh12"))
            eng.activation(XR[0:HD, 12, 1:1 + NT], XR[0:HD, 12, 1:1 + NT], ACT.Tanh)\
                .then_inc(ac.done, ac.tick())
            eng.wait_ge(*at("sh13"))
            eng.activation(XR[:, 13, 1:1 + NT], XR[:, 13, 1:1 + NT], ACT.Sigmoid)\
                .then_inc(ac.done, ac.tick("lr_in"))
            for f in range(4):
                if f:
                    eng.wait_ge(*at(f"prep{f - 1}"))
                for h, (lo, hi) in enumerate(HALFS):
                    eng.wait_ge(*at(f"dec{f}h{h}"))
                    eng.activation(tmp[2][:, lo:hi], bank(f"dec{f}h{h}")[:, 0:hi - lo], ACT.Sigmoid, bias=col("w0", f))\
                        .then_inc(ac.done, ac.tick(("free", f"dec{f}h{h}")))
                for h, (lo, hi) in enumerate(HALFS):
                    eng.wait_ge(*at(f"av{f}h{h}"))
                    eng.activation(tmp[3][:, lo:hi], bank(f"av{f}h{h}")[:, 0:hi - lo], ACT.Sigmoid, bias=col("a0", f))\
                        .then_inc(ac.done, ac.tick(("free", f"av{f}h{h}"), f"sig{f}"))
                for h, (lo, hi) in enumerate(HALFS):
                    eng.wait_ge(*at(f"gg{f}h{h}"))
                    eng.activation(gg[:, f, lo:hi], bank(f"gg{f}h{h}")[:, 0:hi - lo], ACT.Copy)\
                        .then_inc(ac.done, ac.tick(("free", f"gg{f}h{h}")))
                for h, (lo, hi) in enumerate(HALFS):
                    eng.wait_ge(*at(f"kks{f}h{h}"))
                    eng.activation(tmp[5][:, lo:hi], bank(f"kks{f}h{h}")[:, 0:hi - lo], ACT.Sqrt)\
                        .then_inc(ac.done, ac.tick(("free", f"kks{f}h{h}"), f"kkn{f}"))
                eng.wait_ge(*at(f"cl{f}"))
                cl = tmp[6][:, 0:T].rearrange("p (c n) -> p c n", c=QT)
                eng.activation(em[:, f, :], cl[:, :, 63], ACT.Exp)\
                    .then_inc(ac.done, ac.tick())
                eng.activation(ec[:, f, :], cl[:, :, 127], ACT.Exp)\
                    .then_inc(ac.done, ac.tick())
                eng.activation(dv[:, 0, f, :], tmp[2][:, T:NT], ACT.Exp)\
                    .then_inc(ac.done, ac.tick(f"dvw{f}"))
                eng.wait_ge(*at(f"clm{f}"))
                clm = tmp[7][:, 0:T].rearrange("p (c n) -> p c n", c=QT)
                eng.activation(ecr[:, f, :], clm[:, :, 127], ACT.Exp)\
                    .then_inc(ac.done, ac.tick())
                eng.activation(tmp[8][:, 0:T], tmp[8][:, 0:T], ACT.Exp)\
                    .then_inc(ac.done, ac.tick())
                eng.wait_ge(*ac.latest())
                eng.activation(tmp[6][:, 0:T], tmp[7][:, 0:T], ACT.Exp)\
                    .then_inc(ac.done, ac.tick())
                eng.activation(tmp[1][:, 0:T], tmp[7][:, 0:T], ACT.Exp, scale=-1.0)\
                    .then_inc(ac.done, ac.tick(f"E{f}"))
                for w in range(4):
                    eng.wait_ge(*at(f"tm{f}{w}"))
                    eng.activation(tm[:, w, :, f * P:(f + 1) * P], bank(f"tm{f}{w}").rearrange("p (c n) -> p c n", c=QT), ACT.Copy)\
                        .then_inc(ac.done, ac.tick(("free", f"tm{f}{w}"), f"tms{f}"))
            ac.end("prep")
            for c in range(QT):
                for n in LEVELS:
                    for hg in range(2):
                        if n < 64:
                            eng.wait_ge(*at(f"T{c}{hg}_{n}"))
                            eng.activation(Tsb[:, hg, :], bank(f"T{c}{hg}"), ACT.Copy)\
                                .then_inc(ac.done, ac.tick(f"Ts{c}{hg}_{n}", *([("free", f"T{c}{hg}")] if n == 32 else [])))
                        eng.wait_ge(*at(f"TT{c}{hg}_{n}"))
                        eng.activation(TTsb[:, hg, :], bank(f"TT{c}{hg}"), ACT.Copy)\
                            .then_inc(ac.done, ac.tick(f"TTs{c}{hg}_{n}", *([("free", f"TT{c}{hg}")] if n == 64 else [])))
                eng.wait_ge(*at(f"ap{c}"))
                eng.activation(ApT.rearrange("p f n -> p (f n)"), bank(f"ap{c}"), ACT.Copy)\
                    .then_inc(ac.done, ac.tick(f"aps{c}", ("free", f"ap{c}")))
                eng.wait_ge(*at(f"u{c}"))
                eng.activation(U, bank(f"u{c}"), ACT.Copy)\
                    .then_inc(ac.done, ac.tick(f"us{c}", ("free", f"u{c}")))
                eng.wait_ge(*at(f"y{c}p"))
                eng.activation(oT[:, 4:8, c * P:(c + 1) * P], bank(f"y{c}p").rearrange("p (f n) -> p f n", f=4), ACT.Copy)\
                    .then_inc(ac.done, ac.tick(("free", f"y{c}p")))
            eng.wait_ge(*at("yd"))
            eng.activation(oT[:, 4:8, T:NT], bank("yd")[:, 0:4 * NB].rearrange("p (f b) -> p f b", f=4), ACT.Copy)\
                .then_inc(ac.done, ac.tick(("free", "yd"), "yall"))
            for f in range(4):
                if f:
                    eng.wait_ge(*at(f"gn{f - 1}"))
                for h, (lo, hi) in enumerate(HALFS):
                    eng.wait_ge(*at(f"gv{f}h{h}"))
                    eng.activation(rstd[:, lo:hi], bank(f"gv{f}h{h}")[:, 0:hi - lo], ACT.Sqrt, scale=1.0 / HD, bias=eps[:, 1:2])\
                        .then_inc(ac.done, ac.tick(f"grt{f}", ("free", f"gv{f}h{h}")))
            ac.end("rwkv")

            eng.wait_ge(*at("end:rwkv:dve"))
            squares("ffn", lambda k: f"x1_{k}")
            ac.stage("ffn")
            eng.wait_ge(*at("end:rwkv:pe"))
            eng.wait_ge(*at("end:rwkv:pool"))
            eng.wait_ge(*at("stored_rwkv"))
            for m in range(FT):
                if m >= 2:
                    eng.wait_ge(*at(f"actv{m - 2}"))
                for h, (lo, hi) in enumerate(HALFS):
                    eng.wait_ge(*at(f"wg{m}h{h}"))
                    eng.activation(silu[:, m % 2, lo:hi], bank(f"wg{m}h{h}")[:, 0:hi - lo], ACT.Silu)\
                        .then_inc(ac.done, ac.tick(f"silu{m}h{h}", ("free", f"wg{m}h{h}")))
            for k in range(2):
                eng.wait_ge(*at(f"pe{k}"))
                eng.activation(pT[:, k, 0:T], bank(f"pe{k}"), ACT.Copy)\
                    .then_inc(ac.done, ac.tick(("free", f"pe{k}")))
            eng.wait_ge(*at("pd"))
            eng.activation(pT[:, :, T:NT], bank("pd")[:, 0:2 * NB].rearrange("p (k b) -> p k b", k=2), ACT.Copy)\
                .then_inc(ac.done, ac.tick(("free", "pd"), "pTs"))
            squares("ple", lambda k: f"x2_{k}")
            ac.stage("ffn")
            for m in range(KD):
                for h, (lo, hi) in enumerate(HALFS):
                    eng.wait_ge(*at(f"wp{m}h{h}"))
                    eng.activation(pep[:, m, lo:hi], bank(f"wp{m}h{h}")[:, 0:hi - lo], ACT.Copy)\
                        .then_inc(ac.done, ac.tick(f"pep{m}", ("free", f"wp{m}h{h}")))
            eng.wait_ge(*at(f"actv{FT - 1}"))
            for m in range(KD):
                if m >= 2:
                    eng.wait_ge(*at(f"xfin{m - 2}"))
                for h, (lo, hi) in enumerate(HALFS):
                    eng.wait_ge(*at(f"wpg{m}h{h}"))
                    eng.activation(silu[:, m % 2, lo:hi], bank(f"wpg{m}h{h}")[:, 0:hi - lo], ACT.Sigmoid)\
                        .then_inc(ac.done, ac.tick(f"sg{m}h{h}", ("free", f"wpg{m}h{h}")))
            for t in range(QT + 1):
                m = P if t < QT else NB
                eng.wait_ge(*at(f"out{t}1"))
                eng.activation(ot[0:m, t, T:2 * T], bank(f"out{t}1")[0:m, :], ACT.Copy)\
                    .then_inc(ac.done, ac.tick(("free", f"out{t}1"), f"ya{t}"))

        @block.vector
        def _(eng):
            v_ = steps["dve"]
            tt, ts, stt, cp = eng.tensor_tensor, eng.tensor_scalar, eng.scalar_tensor_tensor, eng.tensor_copy

            def normalise(which, gain, reads):
                v_.stage("norm")
                for h, (lo, hi) in enumerate(HALFS):
                    eng.wait_ge(*at(f"{which}rt{h}"))
                    eng.reciprocal(rstd[:, lo:hi], rstd[:, lo:hi])\
                        .then_inc(v_.done, v_.tick())
                eng.wait_ge(*v_.latest())
                for k in range(KD):
                    stt(out=hT[:, k, :], in0=xT[:, k, :], scalar=col(gain, k), in1=rstd[:, :], op0=ALU.mult, op1=ALU.mult)\
                        .then_inc(v_.done, v_.tick(f"{which}h"))

            v_.stage("load")
            for k in range(KD):
                eng.wait_ge(*at(f"x{k}"))
                cp(xT[:, k, 0:T], bank(f"x{k}"))\
                    .then_inc(v_.done, v_.tick(("free", f"x{k}")))
            eng.wait_ge(*at("xd"))
            cp(xT[:, :, T:NT], bank("xd")[:, 0:KD * NB].rearrange("p (k b) -> p k b", k=KD))\
                .then_inc(v_.done, v_.tick(("free", "xd"), "xT"))
            eng.wait_ge(*at("par_t"))
            cp(par[:, :], bank("par_t")[:, 0:NROWS])\
                .then_inc(v_.done, v_.tick(("free", "par_t")))
            eng.wait_ge(*at("ss_t"))
            cp(ssf[:, :, :], bank("ss_t")[:, 0:XF * NB].rearrange("p (f b) -> p f b", f=XF))\
                .then_inc(v_.done, v_.tick(("free", "ss_t")))
            eng.wait_ge(*v_.latest())
            ts(qgain[:, :], col("q_norm"), HD ** -0.5, None, ALU.mult)\
                .then_inc(v_.done, v_.tick())
            c0 = ROWS["k_a"][0]
            ts(ka1[:, :], par[:, c0:c0 + 4], -1.0, 1.0, ALU.mult, ALU.add)\
                .then_inc(v_.done, v_.tick())
            eng.wait_ge(*v_.latest())
            normalise("mix", "norm_mix", None)
            v_.stage("proj")
            for f in range(XF):
                for h, (lo, hi) in enumerate(HALFS):
                    eng.wait_ge(*at(f"xr{f}h{h}"))
                    cp(XR[:, f, 1 + lo:1 + hi], bank(f"xr{f}h{h}")[:, 0:hi - lo])\
                        .then_inc(v_.done, v_.tick(("free", f"xr{f}h{h}"), f"xr_s{f}"))
            v_.stage("att")
            eng.wait_ge(*at("masks"))
            for r in range(R):
                eng.wait_ge(*at(f"qrt{r}"))
                eng.reciprocal(rstd[:, :], rstd[:, :])\
                    .then_inc(v_.done, v_.tick())
                eng.wait_ge(*v_.latest())
                stt(out=qT[:, r, :], in0=qT[:, r, :], scalar=qgain[:, 0:1], in1=rstd[:, :], op0=ALU.mult, op1=ALU.mult)\
                    .then_inc(v_.done, v_.tick(f"q_n{r}", "qTs"))
            for i in range(4):
                n = min(4, XF - 4 * i) * P
                eng.wait_ge(*at(f"xrl{i}"))
                cp(sst[:, i * 512:i * 512 + n], bank(f"xrl{i}")[0:9, 0:n])\
                    .then_inc(v_.done, v_.tick(("free", f"xrl{i}"), "shift_rows"))
            eng.wait_ge(*at("zkv"))
            for v in range(2):
                k_ = zkv[:, 0:QT, 256 + 256 * v:384 + 256 * v]
                tt(kn[:, v, :, :], k_, k_, ALU.mult)\
                    .then_inc(v_.done, v_.tick())
                k_ = zkv[0:NB, QT, 256 + 256 * v:384 + 256 * v]
                tt(dkn[:, v * P:(v + 1) * P], k_, k_, ALU.mult)\
                    .then_inc(v_.done, v_.tick())
            eng.wait_ge(*v_.latest())
            eng.tensor_reduce(krs.rearrange("p v t g -> p (v t g)"), kn.rearrange("p v t (g d) -> p (v t g) d", d=HD), AX.X, ALU.add)\
                .then_inc(v_.done, v_.tick())
            eng.tensor_reduce(drs, dkn.rearrange("p (j d) -> p j d", d=HD), AX.X, ALU.add)\
                .then_inc(v_.done, v_.tick("kss"))
            eng.wait_ge(*at("krt"))
            eng.reciprocal(krs, krs)\
                .then_inc(v_.done, v_.tick())
            eng.reciprocal(drs, drs)\
                .then_inc(v_.done, v_.tick())
            eng.wait_ge(*v_.latest())
            for v in range(2):
                tt(kn[:, v, :, :].rearrange("p t (g d) -> p t g d", d=HD), zkv[:, 0:QT, 256 + 256 * v:384 + 256 * v].rearrange("p t (g d) -> p t g d", d=HD), krs[:, v, :, :].unsqueeze(3).to_broadcast([P, QT, G, HD]), ALU.mult)\
                    .then_inc(v_.done, v_.tick(f"kn{v}"))
                tt(dkn[:, v * P:(v + 1) * P].rearrange("p (g d) -> p g d", d=HD), zkv[0:NB, QT, 256 + 256 * v:384 + 256 * v].rearrange("p (g d) -> p g d", d=HD), drs[:, 2 * v:2 * v + 2].unsqueeze(2).to_broadcast([NB, G, HD]), ALU.mult)\
                    .then_inc(v_.done, v_.tick(f"dkn{v}"))
            for v in range(2):
                for m in range(2):
                    eng.wait_ge(*at(f"conv{v}{m}"))
                    tt(stc[:, 2 * v + m:2 * v + m + 1], bank(f"conv{v}{m}")[:, 320:321], col("cmp_b1", 2 * v + m), ALU.add)\
                        .then_inc(v_.done, v_.tick(f"cb{v}{m}"))
                eng.wait_ge(*at(f"cmp{v}"))
                ts([kc, vc][v], bank(f"cmp{v}")[:, 0:160], col("cmp_b2", v), None, ALU.add)\
                    .then_inc(v_.done, v_.tick(("free", f"cmp{v}"), *(["vc"] if v else [])))
            eng.wait_ge(*v_.latest())
            eng.wait_ge(*at("qms2h1"))
            eng.wait_ge(*at("qms3h1"))
            tt(sq[:, 0, 0:160], kc, kc, ALU.mult)\
                .then_inc(v_.done, v_.tick("kcsq"))
            eng.wait_ge(*at("kcrt"))
            eng.reciprocal(kcn, kcn)\
                .then_inc(v_.done, v_.tick())
            eng.wait_ge(*v_.latest())
            stt(out=kcn, in0=kc, scalar=col("k_norm", 0), in1=kcn, op0=ALU.mult, op1=ALU.mult)\
                .then_inc(v_.done, v_.tick("kcn"))
            eng.wait_ge(*at("vc_t"))
            cp(vcd, bank("vc_t")[:, 0:P])\
                .then_inc(v_.done, v_.tick())
            cp(vcp[0:NCP, :], bank("vc_t")[0:NCP, P:2 * P])\
                .then_inc(v_.done, v_.tick("vcd", ("free", "vc_t")))
            eng.memset(qall, 0.0)\
                .then_inc(v_.done, v_.tick())
            eng.memset(qb, 0.0)\
                .then_inc(v_.done, v_.tick())
            eng.wait_ge(*v_.latest())
            for g in range(G):
                lo, hi = g * HD, (g + 1) * HD
                cp(qall[lo:hi, :].rearrange("p (b h) -> p b h", h=NH)[:, :, g * R:(g + 1) * R], qT[lo:hi, :, T:NT].rearrange("p r b -> p b r"))\
                    .then_inc(v_.done, v_.tick())
            eng.wait_ge(*v_.latest())
            for b in range(NB):
                cp(qb[:, b, b * NH:(b + 1) * NH], qall[:, b * NH:(b + 1) * NH])\
                    .then_inc(v_.done, v_.tick("qb"))
            eng.wait_ge(*at("cache"))
            for v in range(2):
                if v:
                    eng.wait_ge(*at(f"crt{v - 1}"))
                tt(csq, cache[:, v, :, 0:P], cache[:, v, :, 0:P], ALU.mult)\
                    .then_inc(v_.done, v_.tick())
                eng.wait_ge(*v_.latest())
                eng.tensor_reduce(crs, csq.rearrange("p t (g d) -> p (t g) d", d=HD).rearrange("p (t g) d -> p t g d", g=G), AX.X, ALU.add)\
                    .then_inc(v_.done, v_.tick(f"css{v}"))
                eng.wait_ge(*at(f"crt{v}"))
                eng.reciprocal(crs, crs)\
                    .then_inc(v_.done, v_.tick())
                eng.wait_ge(*v_.latest())
                k_ = cache[:, v, :, 0:P].rearrange("p t (g d) -> p t g d", d=HD)
                tt(k_, k_, crs.unsqueeze(3).to_broadcast([P, NPG, G, HD]), ALU.mult)\
                    .then_inc(v_.done, v_.tick(f"ckn{v}"))
                eng.wait_ge(*v_.latest())
            for v in range(2):
                eng.wait_ge(*at(f"sd{v}"))
                eng.tensor_reduce(st[0:64, v:v + 1], bank(f"sd{v}")[0:64, 0:257], AX.X, ALU.max, negate=True)\
                    .then_inc(v_.done, v_.tick(f"sdm{v}"))
            eng.wait_ge(*at("sdc"))
            tt(pcs, bank("sdc")[0:64, 0:P], dec_add[:, :, :].rearrange("p b n -> p (b n)"), ALU.add)\
                .then_inc(v_.done, v_.tick(("free", "sdc")))
            eng.wait_ge(*v_.latest())
            eng.tensor_reduce(st[0:64, 2:3], pcs, AX.X, ALU.max, negate=True)\
                .then_inc(v_.done, v_.tick("sdm2"))
            eng.wait_ge(*at("sde0"))
            eng.wait_ge(*at("sde1"))
            eng.wait_ge(*at("sde2"))
            eng.wait_ge(*at("gd"))
            eng.reciprocal(st[0:64, 8:11], st[0:64, 4:7])\
                .then_inc(v_.done, v_.tick())
            eng.wait_ge(*v_.latest())
            for i, br in enumerate((1, 2, 0)):
                tt(st[0:64, 12 + i:13 + i], st[0:64, 8 + i:9 + i], scol[0:64, br:br + 1], ALU.mult)\
                    .then_inc(v_.done, v_.tick())
            eng.wait_ge(*v_.latest())
            ts(diag[0:64, 2, 0:64], ident[0:64, 0:64], st[0:64, 14:15], None, ALU.mult)\
                .then_inc(v_.done, v_.tick("pdc"))
            for v in range(2):
                ts(diag[0:64, v, 0:64], ident[0:64, 0:64], st[0:64, 12 + v:13 + v], None, ALU.mult)\
                    .then_inc(v_.done, v_.tick())
                ts(st[0:64, 64 + v * NB:64 + (v + 1) * NB], dec_own[:, :], pbuf[0:64, v, 256:257], None, ALU.mult)\
                    .then_inc(v_.done, v_.tick(f"pd{v}"))
            eng.wait_ge(*at("od"))
            for g in range(G):
                lo, hi = g * HD, (g + 1) * HD
                cp(oT[lo:hi, 0:R, T:NT], bank("od")[lo:hi, 0:64].rearrange("p (b g r) -> p g r b", g=G, r=R)[:, g])\
                    .then_inc(v_.done, v_.tick(("free", "od")))
            eng.wait_ge(*v_.latest())

            PER, AHEAD = 16, 3
            UNITS = QT * PER

            def max_unit(i):
                qt = i // PER
                eng.wait_ge(*at(f"s{i}"))
                if i >= 4:
                    eng.wait_ge(*at(f"se{i - 4}"))
                ps = bank(f"s{i}")
                tt(ps[:, qt * P:(qt + 1) * P], ps[:, qt * P:(qt + 1) * P], causal[:, :], ALU.add)\
                    .then_inc(v_.done, v_.tick())
                eng.wait_ge(*v_.latest())
                eng.tensor_reduce(st[:, i % 4:i % 4 + 1], ps[:, 0:(qt + 1) * P], AX.X, ALU.max, negate=True)\
                    .then_inc(v_.done, v_.tick(f"sm{i}"))

            def scale_unit(i):
                qt, u = divmod(i, PER)
                r, g, v = u // 4, u // 2 % 2, u % 2
                h = g * R + r
                eng.wait_ge(*at(f"se{i}"))
                eng.reciprocal(st[:, 16 + i % 4:17 + i % 4], st[:, 8 + i % 4:9 + i % 4])\
                    .then_inc(v_.done, v_.tick())
                if i >= 4:
                    eng.wait_ge(*at(f"pt{i - 4}"))
                eng.wait_ge(*v_.latest())
                ts(diag[:, i % 4, :], ident[:, :], st[:, 16 + i % 4:17 + i % 4], gate[:, qt, 3 * h + 1 + v:3 * h + 2 + v], ALU.mult, ALU.mult)\
                    .then_inc(v_.done, v_.tick(f"p{i}"))

            def block_max(qt):
                eng.wait_ge(*at(f"sc{qt}"))
                if qt:
                    eng.wait_ge(*at(f"ptc{qt - 1}_1"))
                tt(pcm, bank(f"sc{qt}")[:, 0:NH * NCP].rearrange("p (h n) -> p h n", h=NH), cmp_add[:, qt, :].unsqueeze(1).to_broadcast([P, NH, NCP]), ALU.add)\
                    .then_inc(v_.done, v_.tick(("free", f"sc{qt}")))
                eng.wait_ge(*v_.latest())
                eng.tensor_reduce(stc[:, 8:16], pcm, AX.X, ALU.max)\
                    .then_inc(v_.done, v_.tick())
                eng.wait_ge(*v_.latest())
                tt(pcm, pcm, stc[:, 8:16].unsqueeze(2).to_broadcast([P, NH, NCP]), ALU.subtract)\
                    .then_inc(v_.done, v_.tick(f"scm{qt}"))

            def block_scale(qt):
                eng.wait_ge(*at(f"sce{qt}"))
                tt(pcm, pcm, cmp_keep[:, qt, :].unsqueeze(1).to_broadcast([P, NH, NCP]), ALU.mult)\
                    .then_inc(v_.done, v_.tick())
                eng.wait_ge(*v_.latest())
                eng.tensor_reduce(stc[:, 16:24], pcm, AX.X, ALU.add)\
                    .then_inc(v_.done, v_.tick())
                eng.wait_ge(*v_.latest())
                ts(stc[:, 16:24], stc[:, 16:24], 1e-30, None, ALU.max)\
                    .then_inc(v_.done, v_.tick())
                eng.wait_ge(*v_.latest())
                eng.reciprocal(stc[:, 16:24], stc[:, 16:24])\
                    .then_inc(v_.done, v_.tick())
                eng.wait_ge(*v_.latest())
                tt(stc[:, 16:24], stc[:, 16:24], gate[:, qt, :].rearrange("p (h n) -> p h n", n=3)[:, :, 0], ALU.mult)\
                    .then_inc(v_.done, v_.tick())
                eng.wait_ge(*v_.latest())
                tt(pcm, pcm, stc[:, 16:24].unsqueeze(2).to_broadcast([P, NH, NCP]), ALU.mult)\
                    .then_inc(v_.done, v_.tick(f"pc{qt}"))

            def mixed(qt):
                eng.wait_ge(*at(f"o{qt}"))
                cp(oT[:, 0:R, qt * P:(qt + 1) * P], bank(f"o{qt}").rearrange("p (r n) -> p r n", r=R))\
                    .then_inc(v_.done, v_.tick(("free", f"o{qt}")))

            block_max(0)
            for i in range(AHEAD):
                max_unit(i)
            block_scale(0)
            for i in range(UNITS):
                qt, u = divmod(i, PER)
                if qt + 1 < QT and u == 8:
                    block_max(qt + 1)
                if qt + 1 < QT and u == 10:
                    block_scale(qt + 1)
                scale_unit(i)
                if i + AHEAD < UNITS:
                    max_unit(i + AHEAD)
                if qt and u == 2:
                    mixed(qt - 1)
            mixed(QT - 1)
            v_.end("att")

            v_.stage("rwkv")
            eng.wait_ge(*at("end:att:pe"))
            eng.wait_ge(*at("end:att:act"))
            eng.wait_ge(*at("stored_att"))
            for f in range(XF):
                eng.wait_ge(*at(f"sh{f}"))
            for f in range(4):
                r_, k_, vv = XR[:, f, 1:1 + NT], XR[:, 4 + f, 1:1 + NT], XR[:, 8 + f, 1:1 + NT]
                ts(tmp[4], k_, col("k_k", f), None, ALU.mult)\
                    .then_inc(v_.done, v_.tick())
                eng.wait_ge(*v_.latest())
                tt(sq[:, 0, :], tmp[4], tmp[4], ALU.mult)\
                    .then_inc(v_.done, v_.tick(f"kksq{f}"))
                eng.wait_ge(*at(f"sig{f}"))
                ts(tmp[2], tmp[2], -0.6065306597126334, None, ALU.mult)\
                    .then_inc(v_.done, v_.tick())
                ts(tmp[0], tmp[3], col("k_a", f), ka1[:, f:f + 1], ALU.mult, ALU.add)\
                    .then_inc(v_.done, v_.tick())
                eng.wait_ge(*v_.latest())
                for c in range(QT):
                    s_ = slice(c * P, (c + 1) * P)
                    eng.tensor_tensor_scan(tmp[6][:, s_], ones[:, :], tmp[2][:, s_], 0.0, ALU.mult, ALU.add)\
                        .then_inc(v_.done, v_.tick(f"cl{f}"))
                tt(k_, k_, tmp[0], ALU.mult)\
                    .then_inc(v_.done, v_.tick())
                eng.wait_ge(*v_.latest())
                cl = tmp[6][:, 0:T].rearrange("p (c n) -> p c n", c=QT)
                clm = tmp[7][:, 0:T].rearrange("p (c n) -> p c n", c=QT)
                tt(clm, cl, cl[:, :, 63:64].to_broadcast([P, QT, P]), ALU.subtract)\
                    .then_inc(v_.done, v_.tick())
                stt(out=sq[:, 1, :], in0=r_, scalar=col("r_k", f), in1=k_, op0=ALU.mult, op1=ALU.mult)\
                    .then_inc(v_.done, v_.tick(f"bon{f}"))
                eng.wait_ge(*v_.latest())
                tt(tmp[8][:, 0:T], tmp[7][:, 0:T], tmp[2][:, 0:T], ALU.subtract)\
                    .then_inc(v_.done, v_.tick(f"clm{f}"))
                eng.wait_ge(*at(f"kkn{f}"))
                ts(tmp[5], tmp[5], 1e-12, None, ALU.max)\
                    .then_inc(v_.done, v_.tick())
                eng.wait_ge(*v_.latest())
                eng.reciprocal(tmp[5], tmp[5])\
                    .then_inc(v_.done, v_.tick())
                eng.wait_ge(*v_.latest())
                tt(tmp[4], tmp[4], tmp[5], ALU.mult)\
                    .then_inc(v_.done, v_.tick())
                eng.wait_ge(*v_.latest())
                tt(tmp[5], tmp[4], tmp[3], ALU.mult)\
                    .then_inc(v_.done, v_.tick())
                eng.wait_ge(*at(f"E{f}"))
                eng.wait_ge(*v_.latest())
                stt(out=AR[:, f, :, 0:P], in0=tmp[4][:, 0:T].rearrange("p (c n) -> p c n", c=QT), scalar=-1.0, in1=tmp[8][:, 0:T].rearrange("p (c n) -> p c n", c=QT), op0=ALU.mult, op1=ALU.mult)\
                    .then_inc(v_.done, v_.tick())
                tt(AR[:, f, :, P:2 * P], r_[:, 0:T].rearrange("p (c n) -> p c n", c=QT), cl, ALU.mult)\
                    .then_inc(v_.done, v_.tick())
                tt(BH[:, f, :], tmp[5][:, 0:T], tmp[1][:, 0:T], ALU.mult)\
                    .then_inc(v_.done, v_.tick())
                tt(KH[:, f, :], k_[:, 0:T], tmp[1][:, 0:T], ALU.mult)\
                    .then_inc(v_.done, v_.tick(f"tmf{f}"))
                ts(dv[:, 1, f, :], tmp[4][:, T:NT], -1.0, None, ALU.mult)\
                    .then_inc(v_.done, v_.tick())
                cp(dv[:, 2, f, :], tmp[5][:, T:NT])\
                    .then_inc(v_.done, v_.tick())
                cp(dv[:, 3, f, :], k_[:, T:NT])\
                    .then_inc(v_.done, v_.tick())
                cp(dv[:, 4, f, :], r_[:, T:NT])\
                    .then_inc(v_.done, v_.tick())
                cp(dv[:, 5, f, :], vv[:, T:NT])\
                    .then_inc(v_.done, v_.tick(f"prep{f}"))
                if f == 3:
                    eng.wait_ge(*at("dvw3"))
                    points.new["dv"] = points.new["prep3"]
                eng.wait_ge(*at(f"tm{f}3"))
                eng.wait_ge(*v_.latest())
                for h, (lo, hi) in enumerate(HALFS):
                    eng.wait_ge(*at(f"bs{f}h{h}"))
                    tt(vv[:, lo:hi], bank(f"bs{f}h{h}")[:, 0:hi - lo], vv[:, lo:hi], ALU.mult)\
                        .then_inc(v_.done, v_.tick(("free", f"bs{f}h{h}")))
            for w in range(6):
                eng.wait_ge(*at(f"dv{w}"))
                cp(dvt[:, w, :], bank(f"dv{w}")[0:NB, :])\
                    .then_inc(v_.done, v_.tick(("free", f"dv{w}"), "dvt"))
            eng.memset(Hs, 0.0)\
                .then_inc(v_.done, v_.tick())
            eng.memset(Hm, 0.0)\
                .then_inc(v_.done, v_.tick("Hm0"))
            v_.end("prep")
            eng.wait_ge(*at("dv_stored"))
            eng.wait_ge(*at("end:prep:act"))
            eng.wait_ge(*at("end:prep:pe"))
            eng.wait_ge(*v_.latest())
            mask2 = us_ui[:, :, :].rearrange("p s n -> p (s n)").unsqueeze(1).to_broadcast([P, 2, 256])

            def four(m):
                return m.unsqueeze(1).to_broadcast([P, 4, P])

            for c in range(QT):
                if c:
                    eng.wait_ge(*at(f"y{c - 1}p"))
                for hg in range(2):
                    for hp in range(2):
                        h0 = hg * 4 + hp * 2
                        eng.wait_ge(*at(f"ln{c}{hg}{hp}"))
                        tt(LN[:, h0:h0 + 2, :], bank(f"ln{c}{hg}{hp}").rearrange("p (h n) -> p h n", h=2), mask2, ALU.mult)\
                            .then_inc(v_.done, v_.tick(("free", f"ln{c}{hg}{hp}")))
                    for hp in range(2):
                        h0 = hg * 4 + hp * 2
                        eng.wait_ge(*at(f"mq{c}{hg}{hp}"))
                        tt(MQ[:, h0:h0 + 2, :], bank(f"mq{c}{hg}{hp}").rearrange("p (h n) -> p h n", h=2), mask2, ALU.mult)\
                            .then_inc(v_.done, v_.tick(("free", f"mq{c}{hg}{hp}"), f"mqs{c}{hg}"))
                    t4 = Tsb[:, hg, :].rearrange("p (h n) -> p h n", h=4)
                    tt4 = TTsb[:, hg, :].rearrange("p (h n) -> p h n", h=4)
                    eng.wait_ge(*at(f"l{c}{hg}"))
                    tt(t4, bank(f"l{c}{hg}").rearrange("p (h n) -> p h n", h=4), four(level[:, 0, :]), ALU.mult)\
                        .then_inc(v_.done, v_.tick(("free", f"l{c}{hg}")))
                    eng.wait_ge(*v_.latest())
                    tt(tt4, LN[:, hg * 4:hg * 4 + 4, 0:P], four(level1T[:, :]), ALU.mult)\
                        .then_inc(v_.done, v_.tick())
                    eng.wait_ge(*v_.latest())
                    tt(t4, t4, four(ident[:, :]), ALU.add)\
                        .then_inc(v_.done, v_.tick(f"Ts{c}{hg}_1"))
                    tt(tt4, tt4, four(ident[:, :]), ALU.add)\
                        .then_inc(v_.done, v_.tick(f"TTs{c}{hg}_1"))
                for i, n in enumerate(LEVELS):
                    for hg in range(2):
                        eng.wait_ge(*at(f"X{c}{hg}_{n}"))
                        if i:
                            eng.wait_ge(*at(f"TT{c}{hg}_{n // 2}"))
                        tt(Xs[:, hg, :].rearrange("p (h n) -> p h n", h=4), bank(f"X{c}{hg}_{n}").rearrange("p (h n) -> p h n", h=4), four(level[:, 1 + i, :]), ALU.mult)\
                            .then_inc(v_.done, v_.tick(f"Xs{c}{hg}_{n}", ("free", f"X{c}{hg}_{n}")))
                eng.wait_ge(*at(f"mv{c}"))
                cp(MV, bank(f"mv{c}"))\
                    .then_inc(v_.done, v_.tick(f"mvs{c}", ("free", f"mv{c}")))
                eng.wait_ge(*at(f"us{c}"))
                eng.wait_ge(*at(f"sa{c}"))
                tt(SA, bank(f"sa{c}"), U, ALU.add)\
                    .then_inc(v_.done, v_.tick(f"sas{c}", ("free", f"sa{c}")))

                def per_key(x, i):
                    return x[:, :, i:i + 1].to_broadcast([P, 4, HD])

                tt(Hd, Hs, per_key(ec, c), ALU.mult)\
                    .then_inc(v_.done, v_.tick())
                eng.wait_ge(*at(f"H{c}"))
                eng.wait_ge(*v_.latest())
                tt(Hs, bank(f"H{c}")[:, 0:256].rearrange("p (f n) -> p f n", f=4), per_key(ecr, c), ALU.mult)\
                    .then_inc(v_.done, v_.tick(("free", f"H{c}")))
                eng.wait_ge(*v_.latest())
                tt(Hs, Hs, Hd, ALU.add)\
                    .then_inc(v_.done, v_.tick("Hend"))
                eng.wait_ge(*v_.latest())
                if c + 1 < QT:
                    eng.wait_ge(*at(f"y{c}p"))
                    tt(Hm, Hs, per_key(em, c + 1), ALU.mult)\
                        .then_inc(v_.done, v_.tick(f"Hm{c + 1}"))
                (kind, into), h = (("sa", sa), ("yd", yd))[c % 2], c // 2
                eng.wait_ge(*v_.latest())
                eng.wait_ge(*at(f"{kind}_in{h}"))
                eng.tensor_reduce(into[:, h * 16:(h + 1) * 16], S2, AX.X, ALU.add)\
                    .then_inc(v_.done, v_.tick(f"{kind}_sum{h}"))
            eng.wait_ge(*at("wk"))
            cp(wkt, bank("wk")[0:HD, :])\
                .then_inc(v_.done, v_.tick("wkt", ("free", "wk")))
            for f in range(4):
                y = oT[:, 4 + f, :]
                for h, (lo, hi) in enumerate(HALFS):
                    eng.wait_ge(*at(f"gm{f}h{h}"))
                    stt(out=y[:, lo:hi], in0=bank(f"gm{f}h{h}")[:, 0:hi - lo], scalar=-1.0 / HD, in1=y[:, lo:hi], op0=ALU.mult, op1=ALU.add)\
                        .then_inc(v_.done, v_.tick(("free", f"gm{f}h{h}")))
                eng.wait_ge(*v_.latest())
                if f >= 2:
                    eng.wait_ge(*at(f"gv{f - 2}h1"))
                tt(sq[:, f % 2, :], y, y, ALU.mult)\
                    .then_inc(v_.done, v_.tick(f"gsq{f}"))
                eng.wait_ge(*at(f"grt{f}"))
                eng.reciprocal(rstd[:, :], rstd[:, :])\
                    .then_inc(v_.done, v_.tick())
                eng.wait_ge(*v_.latest())
                tt(y, y, rstd[:, :], ALU.mult)\
                    .then_inc(v_.done, v_.tick(f"gn{f}"))
                eng.wait_ge(*v_.latest())
                ts(y, y, col("ln_w", f), col("ln_b", f), ALU.mult, ALU.add)\
                    .then_inc(v_.done, v_.tick())
                eng.wait_ge(*v_.latest())
                tt(y, y, XR[:, 8 + f, 1:1 + NT], ALU.add)\
                    .then_inc(v_.done, v_.tick())
                eng.wait_ge(*v_.latest())
                tt(y, y, gg[:, f, :], ALU.mult)\
                    .then_inc(v_.done, v_.tick())
            v_.end("rwkv")

            v_.stage("ffn")
            eng.wait_ge(*at("end:rwkv:pe"))
            eng.wait_ge(*at("end:rwkv:act"))
            eng.wait_ge(*at("end:rwkv:pool"))
            eng.wait_ge(*at("stored_rwkv"))
            eng.wait_ge(*v_.latest())
            for m in range(KD):
                for h, (lo, hi) in enumerate(HALFS):
                    eng.wait_ge(*at(f"wo{m}h{h}"))
                    tt(xT[:, m, lo:hi], bank(f"wo{m}h{h}")[:, 0:hi - lo], xT[:, m, lo:hi], ALU.add)\
                        .then_inc(v_.done, v_.tick(("free", f"wo{m}h{h}"), f"x1_{m}"))
            eng.wait_ge(*v_.latest())
            normalise("ffn", "norm_ffn", None)
            v_.stage("ffn")
            for m in range(FT):
                for h, (lo, hi) in enumerate(HALFS):
                    eng.wait_ge(*at(f"wu{m}h{h}"))
                    eng.wait_ge(*at(f"silu{m}h{h}"))
                    tt(actv[:, m, lo:hi], bank(f"wu{m}h{h}")[:, 0:hi - lo], silu[:, m % 2, lo:hi], ALU.mult)\
                        .then_inc(v_.done, v_.tick(("free", f"wu{m}h{h}"), f"actv{m}"))
            for m in range(KD):
                for h, (lo, hi) in enumerate(HALFS):
                    eng.wait_ge(*at(f"wd{m}h{h}"))
                    tt(xT[:, m, lo:hi], bank(f"wd{m}h{h}")[:, 0:hi - lo], xT[:, m, lo:hi], ALU.add)\
                        .then_inc(v_.done, v_.tick(("free", f"wd{m}h{h}"), f"x2_{m}"))
            eng.wait_ge(*v_.latest())
            normalise("ple", "norm_ple", None)
            v_.stage("ffn")
            for m in range(KD):
                s_ = silu[:, m % 2, :]
                eng.wait_ge(*at(f"pep{m}"))
                for h, (lo, hi) in enumerate(HALFS):
                    eng.wait_ge(*at(f"sg{m}h{h}"))
                    tt(s_[:, lo:hi], s_[:, lo:hi], pep[:, m, lo:hi], ALU.mult)\
                        .then_inc(v_.done, v_.tick())
                eng.wait_ge(*v_.latest())
                tt(xT[:, m, :], xT[:, m, :], s_, ALU.add)\
                    .then_inc(v_.done, v_.tick(f"xfin{m}"))
            for t in range(QT + 1):
                m = P if t < QT else NB
                eng.wait_ge(*at(f"out{t}0"))
                eng.wait_ge(*at(f"ya{t}"))
                cp(ot[0:m, t, 0:T], bank(f"out{t}0")[0:m, :])\
                    .then_inc(v_.done, v_.tick(("free", f"out{t}0"), f"y{t}"))

        return sems


_INS = ["x_prompt", "x_sample", "p_prompt", "p_sample", "cache_kv", "cache_win", "state_wkv", "state_shift",
        "page_table", "norm_mix", "w_in", "q_norm", "k_norm", "cmp_pe", "cmp_w1", "cmp_b1", "cmp_w2", "cmp_b2",
        "shift_mu", "w0", "w2", "a0", "a2", "g2", "k_k", "k_a", "r_k", "ln_w", "ln_b", "w_out", "norm_ffn", "w_gate",
        "w_up", "w_down", "norm_ple", "w_ple_gate", "w_ple"]
_OUTS = [("y_prompt", (1, T, D)), ("y_sample", (NB, 1, D)), ("kv_prompt", (1, 1, T, 4, G, HD)),
         ("kv_sample", (1, NB, 1, 4, G, HD)), ("win_prompt", (1, 1, T, 2, G, HD)),
         ("win_sample", (1, NB, PAST, 2, G, HD)), ("wkv_prompt", (1, 1, NH, HD, HD)),
         ("wkv_sample", (1, NB, NH, HD, HD)), ("shift_prompt", (1, 1, XRC)), ("shift_sample", (1, NB, XRC))]


def kernel(**inputs):
    import numpy as _np
    import concourse.bacc as _bacc
    from concourse import mybir as _mybir
    from concourse.bass_utils import run_bass_kernel_spmd as _run

    arrays = {n: _np.ascontiguousarray(inputs[n]) for n in _INS}
    points = Points()
    for _ in range(2):
        nc = _bacc.Bacc("TRN2", target_bir_lowering=False, num_devices=1, dynamic_dma_scratch_size=4096)
        a = {n: nc.dram_tensor(f"in_{n}", x.shape, _mybir.dt.from_np(x.dtype), kind="ExternalInput").ap()
             for n, x in arrays.items()}
        out = {n: nc.dram_tensor(f"out_{n}", shape, F32, kind="ExternalOutput").ap() for n, shape in _OUTS}
        build(nc, a, out, points)
        points = Points(points.new)
    r = _run(nc, [{f"in_{n}": x for n, x in arrays.items()}], core_ids=[0])
    return tuple(r.results[0][f"out_{n}"] for n, _ in _OUTS)
```

```python
from contextlib import ExitStack

import concourse.bass as bass
from concourse import mybir

F32 = mybir.dt.float32
F32R = mybir.dt.float32r
I32 = mybir.dt.int32
ALU = mybir.AluOpType
ACT = mybir.ActivationFunctionType
AX = mybir.AxisListType

P = 128
D = 1024
KD = D // P
T = 512
QT = T // P
NB = 8
NT = T + NB
HALF = NT // 2
HD = 64
NH = 8
G = 2
R = NH // G
PAST = 256
PAGE = 128
NPG = NB * PAST // PAGE
KV = 768
GATES = 3 * NH
XRC = 1792
XF = XRC // P
C_KV, C_GATE, C_XR = 512, 1280, 1304
STRIDE, BLOCK = 16, 32
NCP = (T - BLOCK) // STRIDE + 1
NCD = (PAST + 1 - BLOCK) // STRIDE + 1
FF = 2816
FT = FF // P
PLE = 256
PAIR_SEQ = NB * P + T // 2
XCMP = G * PAIR_SEQ + BLOCK // 2
NWIN = XCMP // 8 - 1
NEG = -1e30
EPS = 1e-6
GN_EPS = 64e-5
HALFS = ((0, HALF), (HALF, NT))
LEVELS = (2, 4, 8, 16, 32, 64)

ROWS = {}
for _name, _n in (("norm_mix", 8), ("norm_ffn", 8), ("norm_ple", 8), ("shift_mu", XF), ("w0", 4), ("a0", 4),
                  ("k_k", 4), ("k_a", 4), ("r_k", 4), ("ln_w", 4), ("ln_b", 4), ("q_norm", 1), ("k_norm", 3),
                  ("cmp_b1", 4), ("cmp_b2", 2)):
    ROWS[_name] = (sum(n for _, n in ROWS.values()), _n)
NROWS = sum(n for _, n in ROWS.values())


class Points:

    def __init__(self, known=None):
        self.known = known
        self.new = {}


class Steps:

    def __init__(self, name, points, sem):
        self.name, self.points, self.sem = name, points, sem
        self.count = {}
        self.key = None

    def stage(self, name):
        self.key = f"{self.name}_{name}"
        self.done = self.sem(self.key)
        self.count.setdefault(self.key, 0)

    def tick(self, *names):
        self.count[self.key] += 1
        for n in names:
            self.points.new[n] = (self.key, self.count[self.key])
        return 1

    def landed(self, key, *names):
        self.count[key] = self.count.get(key, 0) + 16
        for n in names:
            self.points.new[n] = (key, self.count[key])
        return 16

    def latest(self):
        return self.done, self.count[self.key]

    def end(self, phase):
        self.points.new[f"end:{phase}:{self.name}"] = (self.key, self.count[self.key])


def build(nc, a, out, points):
    ctx = ExitStack()
    with ctx:
        sems = {}

        def sem(name):
            if name not in sems:
                sems[name] = ctx.enter_context(nc.semaphore(name))
            return sems[name]

        start_of = {}

        def sb(name, shape, dt=F32):
            t = ctx.enter_context(nc.sbuf_tensor(name, shape, dt))
            n = 4
            for s in shape[1:]:
                n *= s
            start_of[name] = nc.sbuf_base - n
            return t

        def rounded(name, shape, within, column=0):
            return nc.alloc_sbuf_tensor_at(name, shape, F32R, offset=start_of[within] + 4 * column)

        xT = sb("xT", [P, KD, NT])
        hT = sb("hT", [P, KD, NT])
        oT = hT
        NSLOT = 3
        ring = sb("ring", [P, NSLOT, 8 * 256])
        XR = sb("XR", [P, XF, 1 + NT])
        par_rows = sb("par_rows", [P, P])
        par = sb("par", [P, NROWS])
        ident = sb("ident", [P, P])
        ones = sb("ones", [P, P])
        blk = sb("blk", [P, P])
        causal = sb("causal", [P, P])
        us_ui = sb("us_ui", [P, 2, P])
        level = sb("level", [P, 7, P])
        level1T = sb("level1T", [P, P])
        cmp_keep = sb("cmp_keep", [P, QT, NCP])
        cmp_add = sb("cmp_add", [P, QT, NCP])
        dec_add = sb("dec_add", [64, NB, 16])
        dec_own = sb("dec_own", [64, NB])
        eps = sb("eps", [P, 2])
        qgain = sb("qgain", [P, 1])
        ka1 = sb("ka1", [P, 4])
        rstd = sb("rstd", [P, NT])
        sq = sb("sq", [P, 2, NT])
        ARENA = 29952
        arena = sb("arena", [P, ARENA])

        class Place:

            def __init__(self, at=0):
                self.at = at

            def __call__(self, n, rows=P):
                self.at += n
                assert self.at <= ARENA, self.at
                return arena[0:rows, self.at - n:self.at]

            def skip(self, n):
                self.at += n
                assert self.at <= ARENA and n % 8 == 0, self.at
                return self.at - n

        new = Place()
        zkv = new(5 * KV).rearrange("p (t n) -> p t n", t=5)
        gate = new(5 * GATES).rearrange("p (t n) -> p t n", t=5)
        late = Place(new.at)
        csq = XR[:, 0:4, :].rearrange("p f n -> p (f n)")[:, 0:NPG * P].rearrange("p (t n) -> p t n", t=NPG)
        early = Place(new.at)
        xstage = Place(new.at)(5 * D).rearrange("p (t n) -> p t n", t=5)
        xcmp = new(2 * XCMP).rearrange("p (v n) -> p v n", v=2)
        pbuf = late(4 * T).rearrange("p (i n) -> p i n", i=4)
        ptb = late(2 * T).rearrange("p (i n) -> p i n", i=2)
        assert late.at <= new.at
        diag = new(4 * P).rearrange("p (i n) -> p i n", i=4)
        qT = new(R * NT).rearrange("p (r n) -> p r n", r=R)
        lr_w = Place(new.at)(T)
        kT = new(2 * T).rearrange("p (v n) -> p v n", v=2)
        over = Place(new.at)
        pairs = new(10 * 512).rearrange("p (s w a d) -> p s w a d", s=10, w=4, a=2)
        ptcb = Place(over.at)(2 * NH * P).rearrange("p (i h n) -> p i h n", i=2, h=NH)
        kTd = over(2 * NB * 257).rearrange("p (v b n) -> p v b n", v=2, b=NB)
        assert over.at <= new.at
        cache_at = new.at
        cache = new(2 * NPG * 256).rearrange("p (v g n) -> p v g n", v=2, g=NPG)
        kn = new(2 * QT * P).rearrange("p (v t n) -> p v t n", v=2, t=QT)
        dkn = new(256, NB)
        w2c = new(256).rearrange("p (v m d) -> p v m d", v=2, m=2)
        krs = new(16).rearrange("p (v t g) -> p v t g", v=2, t=QT)
        drs = new(4, NB)
        crs = new(32).rearrange("p (t g) -> p t g", g=G)
        pcm = new(NH * NCP).rearrange("p (h n) -> p h n", h=NH)
        st = new(96)
        stc = new(32)
        scol = new(16)
        sst = new(XRC, 9)
        att_end = new.at
        spare = oT[:, 4:8, :].rearrange("p f n -> p (f n)")
        gel = spare[:, 0:640].rearrange("p (m n) -> p m n", m=2)
        kc, kcn, vc = spare[:, 640:800], spare[:, 800:960], spare[:, 960:1120]
        vcd, vcp = spare[:, 1120:1248], spare[:, 1248:1376]
        qall = spare[:, 1376:1440]
        qb = spare[:, 1440:1952].rearrange("p (b n) -> p b n", b=NB)
        pcs = pbuf[0:64, 2, 0:P]

        tmp = [early(NT) for _ in range(9)]
        dvt = Place(early.at - 9 * NT)(6 * T, NB).rearrange("p (w n) -> p w n", w=6)
        factors = Place(cache_at)(4 * 2048).rearrange("p (f n) -> p f n", f=4)
        staged = Place(cache_at + 4096)(2 * 2048).rearrange("p (i n) -> p i n", i=2)

        def factors_of(t):
            return (t[:, :, 0:1024].rearrange("p f (c n) -> p f c n", c=QT), t[:, :, 1024:1536], t[:, :, 1536:2048])

        AR, BH, KH = factors_of(factors)
        ARs, BHs, KHs = factors_of(staged)
        em, ec, ecr = (sb(n, [P, 4, QT])[:, :, :] for n in ("em", "ec", "ecr"))
        dv = sb("dv", [P, 6, 4, NB])[:, :, :, :]
        xlast = sb("xlast", [P, XF, 9])

        new = Place()
        tm = new(4 * QT * T).rearrange("p (w c n) -> p w c n", w=4, c=QT)
        g2w = new(T)
        S = new(2048).rearrange("p (i j) -> p i j", i=32)
        ydt = new(T, NB)
        Hd = new(256).rearrange("p (f n) -> p f n", f=4)
        dvr = new(6 * HD).rearrange("p (w n) -> p w n", w=6)
        vrow, sa, yd = new(32), new(32), new(32)
        Tsb = new(2 * T).rearrange("p (g n) -> p g n", g=2)
        TTsb = new(2 * T).rearrange("p (g n) -> p g n", g=2)
        Xs = new(2 * T).rearrange("p (g n) -> p g n", g=2)
        U, ApT, SA, MV = new(T), new(T).rearrange("p (f n) -> p f n", f=4), new(T), new(T)
        assert new.at <= cache_at
        wkt = Tsb[0:HD, 0, :]
        new = Place(cache_at + 4 * 2048)
        S2 = new(1024).rearrange("p (i j) -> p i j", i=16)
        Hs = new(256).rearrange("p (f n) -> p f n", f=4)
        Hm = new(256).rearrange("p (f n) -> p f n", f=4)
        rwkv_end = new.at
        LN = XR[:, 0:4, :].rearrange("p f n -> p (f n)")[:, 0:2048].rearrange("p (h n) -> p h n", h=8)
        MQ = XR[:, 4:8, :].rearrange("p f n -> p (f n)")[:, 0:2048].rearrange("p (h n) -> p h n", h=8)
        shf = par_rows

        new = Place()
        act_hi, act_lo = (rounded(n, [P, FT, NT], "arena", new.skip(FT * NT)) for n in ("act_hi", "act_lo"))
        silu = new(2 * NT).rearrange("p (i n) -> p i n", i=2)
        act_f = new(2 * NT).rearrange("p (i n) -> p i n", i=2)
        x_hi = rounded("x_hi", [P, KD, NT], "arena", new.skip(KD * NT))
        x_lo = rounded("x_lo", [P, KD, NT], "hT")
        xr_flat = XR[:, :, :].rearrange("p f n -> p (f n)")
        w_hi = rounded("w_hi", [P, 2, 2048], "XR")
        w_lo = rounded("w_lo", [P, NSLOT, 2048], "ring")
        pst = xr_flat[:, 4096:4096 + 5 * PLE].rearrange("p (t n) -> p t n", t=5)
        pT = xr_flat[:, 5376:5376 + 2 * NT].rearrange("p (k n) -> p k n", k=2)
        new = Place()
        pep = new(KD * NT).rearrange("p (f n) -> p f n", f=KD)
        ot = new(5 * D).rearrange("p (t n) -> p t n", t=5)
        ssf = sb("ssf", [P, XF, NB])
        page_sb = sb("page_sb", [1, NPG], I32)

        psum = ctx.enter_context(nc.psum_tensor("psum", [P, 8, 512], F32))

        def col(name, i=0, lo=0, hi=P):
            c = ROWS[name][0] + i
            return par[lo:hi, c:c + 1]

        scratch = nc.dram_tensor("dec_scratch", (NB, NH, 6, HD), F32).ap()
        scratch_f = nc.dram_tensor("rwkv_factors", (P, 4, 2048), F32).ap()
        scratch_y = nc.dram_tensor("dec_scratch_y", (NB, T), F32).ap()

        chunks = [("xr", i) for i in range(7)] + [("kv", i) for i in range(3)] + [("gates", 0)]
        chunks += [("q", i) for i in range(2)] + [("w1", i) for i in range(4)]
        chunks += [("wo", i) for i in range(4)]
        for i in range(11):
            chunks += [("wg", i), ("wu", i)]
        chunks += [("wd", i, j) for i in range(4) for j in range(3)]
        chunks += [("wp", 0)] + [("wpg", i) for i in range(4)]
        XR_PAIRS = ((12, 13), (0, 4), (8, 1), (5, 9), (2, 6), (10, 3), (7, 11))
        slot_of = {c: i % NSLOT for i, c in enumerate(chunks)}

        def slot(c, n=256):
            return ring[:, slot_of[c], :].rearrange("p (k n) -> p k n", n=n)

        split_chunks = [c for c in chunks if c[0] in ("wo", "wg", "wu", "wd", "wpg")]

        def split_parts(c):
            n = (FT - 16) * 256 if c[0] == "wd" and c[2] == 2 else 2048
            return ring[:, slot_of[c], 0:n], w_hi[:, split_chunks.index(c) % 2, 0:n], w_lo[:, slot_of[c], 0:n]

        def split_before(c):
            i = split_chunks.index(c)
            return split_chunks[i - 2] if i >= 2 else None

        bank_user = {}
        turn = {"banks": list(range(8)), "next": 0}

        def bank(name):
            return psum[:, points.known[("bank", name)] if points.known else 0, :]

        def at(name):
            key, value = points.known[name] if points.known else ("pe_load", 0)
            return sem(key), value

        steps = {n: Steps(n, points, sem) for n in ("pe", "dve", "act", "pool", "sp")}
        block = ctx.enter_context(nc.Block())

        @block.sync
        def _(eng):
            sp = steps["sp"]

            def kp(w, c0, n, k0=0, kn=KD):
                return w[k0 * P:(k0 + kn) * P, c0:c0 + n].rearrange("(k p) n -> p k n", p=P)

            for i, c in enumerate(chunks):
                if i >= NSLOT:
                    eng.wait_ge(*at(("used", chunks[i - NSLOT])))
                if c == ("wo", 0):
                    eng.wait_ge(*at("od"))
                    eng.wait_ge(*at("stored_f2"))
                    eng.wait_ge(*at("stored_f3"))
                    for f in range(4):
                        eng.dma_start(factors[:, f, :], scratch_f[:, f, :])\
                            .then_inc(sem("load_f"), sp.landed("load_f", "factors"))
                dst, key, mark = slot(c), f"ring{i % NSLOT}", ("got", c)
                kind = c[0]
                if kind == "kv":
                    eng.dma_start(dst, kp(a["w_in"][0], C_KV + 256 * c[1], 256))\
                        .then_inc(sem(key), sp.landed(key, mark))
                elif kind == "gates":
                    eng.dma_start(dst[:, :, 0:GATES], kp(a["w_in"][0], C_GATE, GATES))\
                        .then_inc(sem(key), sp.landed(key, mark))
                elif kind == "q":
                    for j in range(2):
                        for g in range(G):
                            eng.dma_start(dst[:, :, j * P + g * HD:j * P + (g + 1) * HD], kp(a["w_in"][0], (g * R + 2 * c[1] + j) * HD, HD))\
                                .then_inc(sem(key), sp.landed(key, mark))
                elif kind == "xr":
                    for j, f in enumerate(XR_PAIRS[c[1]]):
                        eng.dma_start(dst[:, :, j * P:(j + 1) * P], kp(a["w_in"][0], C_XR + P * f, P))\
                            .then_inc(sem(key), sp.landed(key, mark))
                elif kind == "w1":
                    v, part = c[1] // 2, c[1] % 2
                    eng.dma_start(dst, kp(a["cmp_w1"][0, v], 0, 256, part * 8))\
                        .then_inc(sem(key), sp.landed(key, mark))
                elif kind == "wo":
                    for g in range(G):
                        src = a["w_out"][0, g * R * HD:(g + 1) * R * HD, 256 * c[1]:256 * c[1] + 256]
                        eng.dma_start(dst[g * HD:(g + 1) * HD, 0:4, :], src.rearrange("(r d) n -> d r n", d=HD))\
                            .then_inc(sem(key), sp.landed(key, mark))
                    eng.dma_start(dst[:, 4:8, :], kp(a["w_out"][0], 256 * c[1], 256, 4, 4))\
                        .then_inc(sem(key), sp.landed(key, mark))
                elif kind in ("wg", "wu"):
                    w = a["w_gate" if kind == "wg" else "w_up"][0]
                    eng.dma_start(dst, kp(w, 256 * c[1], 256))\
                        .then_inc(sem(key), sp.landed(key, mark))
                elif kind == "wd":
                    kn = min(8, FT - 8 * c[2])
                    eng.dma_start(dst[:, 0:kn, :], kp(a["w_down"][0], 256 * c[1], 256, 8 * c[2], kn))\
                        .then_inc(sem(key), sp.landed(key, mark))
                elif kind == "wp":
                    eng.dma_start(slot(c, D)[:, 0:2, :], kp(a["w_ple"][0], 0, D, 0, 2))\
                        .then_inc(sem(key), sp.landed(key, mark))
                else:
                    eng.dma_start(dst, kp(a["w_ple_gate"][0], 256 * c[1], 256))\
                        .then_inc(sem(key), sp.landed(key, mark))

        @block.gpsimd
        def _(eng):
            pl = steps["pool"]
            pl.stage("init")
            eng.memset(ident[:, :], 0.0)\
                .then_inc(pl.done, pl.tick())
            eng.memset(ones[:, :], 1.0)\
                .then_inc(pl.done, pl.tick())
            eng.memset(eps[:, 0:1], EPS)\
                .then_inc(pl.done, pl.tick())
            eng.memset(eps[:, 1:2], GN_EPS)\
                .then_inc(pl.done, pl.tick("eps"))
            eng.memset(par_rows[:, :], 0.0)\
                .then_inc(pl.done, pl.tick("par_zero"))
            eng.wait_ge(*pl.latest())
            eng.affine_select(out=ident[:, :], in_=ident[:, :], compare_op=ALU.not_equal, fill=1.0, base=0, pattern=[[-1, P]], channel_multiplier=1)\
                .then_inc(pl.done, pl.tick("ident"))
            eng.dma_start(page_sb[:, :], a["page_table"].rearrange("b n -> (b n)").rearrange("(o n) -> o n", o=1))\
                .then_inc(sem("load_page"), pl.landed("load_page", "page"))
            eng.dma_start(w2c, a["cmp_w2"][0].rearrange("v (m p) d -> p v m d", p=P))\
                .then_inc(sem("load_w2c"), pl.landed("load_w2c", "w2c"))
            eng.memset(blk[:, :], 1.0)\
                .then_inc(pl.done, pl.tick())
            eng.memset(causal[:, :], 0.0)\
                .then_inc(pl.done, pl.tick())
            eng.memset(us_ui[:, :, :], 1.0)\
                .then_inc(pl.done, pl.tick())
            eng.memset(level[:, :, :], 0.0)\
                .then_inc(pl.done, pl.tick())
            eng.memset(level1T[:, :], 0.0)\
                .then_inc(pl.done, pl.tick())
            eng.memset(cmp_keep[:, :, :], 1.0)\
                .then_inc(pl.done, pl.tick())
            eng.memset(dec_add[:, :, :], 0.0)\
                .then_inc(pl.done, pl.tick())
            eng.memset(dec_own[:, :], 1.0)\
                .then_inc(pl.done, pl.tick())
            eng.memset(XR[:, :, 0:1], 0.0)\
                .then_inc(pl.done, pl.tick())
            eng.wait_ge(*pl.latest())
            bv = blk[:, :].rearrange("p (s n) -> p s n", s=2)
            eng.affine_select(out=bv, in_=bv, compare_op=ALU.is_ge, fill=0.0, base=0, pattern=[[-HD, 2], [0, HD]], channel_multiplier=1)\
                .then_inc(pl.done, pl.tick())
            lv = {}
            for i, n in enumerate((1,) + LEVELS):
                lv[i] = level[:, i, :].rearrange("p (j s n) -> p j s n", s=2, n=n)
                eng.memset(lv[i][:, :, 0, :], 1.0)\
                    .then_inc(pl.done, pl.tick())
            lt = level1T[:, :].rearrange("p (j s) -> p j s", s=2)
            eng.memset(lt[:, :, 1:2], 1.0)\
                .then_inc(pl.done, pl.tick())
            eng.affine_select(out=causal[:, :], in_=causal[:, :], compare_op=ALU.is_ge, fill=NEG, base=0, pattern=[[-1, P]], channel_multiplier=1)\
                .then_inc(pl.done, pl.tick())
            eng.affine_select(out=us_ui[:, 0, :], in_=us_ui[:, 0, :], compare_op=ALU.is_gt, fill=0.0, base=0, pattern=[[1, P]], channel_multiplier=-1)\
                .then_inc(pl.done, pl.tick())
            eng.affine_select(out=us_ui[:, 1, :], in_=us_ui[:, 1, :], compare_op=ALU.is_ge, fill=0.0, base=0, pattern=[[1, P]], channel_multiplier=-1)\
                .then_inc(pl.done, pl.tick())
            eng.affine_select(out=cmp_keep[:, :, :], in_=cmp_keep[:, :, :], compare_op=ALU.is_ge, fill=0.0, base=-(BLOCK - 1), pattern=[[P, QT], [-STRIDE, NCP]], channel_multiplier=1)\
                .then_inc(pl.done, pl.tick())
            eng.affine_select(out=dec_add[:, :, :], in_=dec_add[:, :, :], compare_op=ALU.is_ge, fill=NEG, base=0, pattern=[[-NH, NB], [0, 16]], channel_multiplier=1)\
                .then_inc(pl.done, pl.tick())
            eng.affine_select(out=dec_own[:, :], in_=dec_own[:, :], compare_op=ALU.is_ge, fill=0.0, base=0, pattern=[[-NH, NB]], channel_multiplier=1)\
                .then_inc(pl.done, pl.tick())
            eng.wait_ge(*pl.latest())
            eng.affine_select(out=dec_add[:, :, :], in_=dec_add[:, :, :], compare_op=ALU.is_ge, fill=NEG, base=NH - 1, pattern=[[NH, NB], [0, 16]], channel_multiplier=-1)\
                .then_inc(pl.done, pl.tick())
            eng.affine_select(out=dec_own[:, :], in_=dec_own[:, :], compare_op=ALU.is_ge, fill=0.0, base=NH - 1, pattern=[[NH, NB]], channel_multiplier=-1)\
                .then_inc(pl.done, pl.tick())
            eng.affine_select(out=bv, in_=bv, compare_op=ALU.is_ge, fill=0.0, base=HD - 1, pattern=[[HD, 2], [0, HD]], channel_multiplier=-1)\
                .then_inc(pl.done, pl.tick())
            for i, n in enumerate((1,) + LEVELS):
                eng.affine_select(out=lv[i], in_=lv[i], compare_op=ALU.is_ge, fill=0.0, base=-n, pattern=[[-2 * n, P // (2 * n)], [0, 2], [0, n]], channel_multiplier=1)\
                    .then_inc(pl.done, pl.tick())
            eng.affine_select(out=lt, in_=lt, compare_op=ALU.is_equal, fill=0.0, base=0, pattern=[[-2, P // 2], [0, 2]], channel_multiplier=1)\
                .then_inc(pl.done, pl.tick())
            eng.tensor_scalar(cmp_add[:, :, :], cmp_keep[:, :, :], -NEG, NEG, ALU.mult, ALU.add)\
                .then_inc(pl.done, pl.tick())
            eng.wait_ge(*pl.latest())
            for i, n in enumerate((1,) + LEVELS):
                eng.affine_select(out=lv[i], in_=lv[i], compare_op=ALU.is_ge, fill=0.0, base=2 * n - 1, pattern=[[2 * n, P // (2 * n)], [0, 2], [0, n]], channel_multiplier=-1)\
                    .then_inc(pl.done, pl.tick())
            eng.affine_select(out=dec_add[:, :, :], in_=dec_add[:, :, :], compare_op=ALU.is_ge, fill=NEG, base=NCD - 1, pattern=[[0, NB], [-1, 16]], channel_multiplier=0)\
                .then_inc(pl.done, pl.tick("masks"))
            for half, w in ((0, "w2"), (1, "a2")):
                eng.dma_start(lr_w[half * HD:(half + 1) * HD, :], a[w][0])\
                    .then_inc(sem("load_lr"), pl.landed("load_lr", "lr_w"))
            pl.stage("att")
            eng.wait_ge(*at("page"))
            for i in range(NPG):
                pg = eng.value_load(page_sb[0:1, i:i + 1], min_val=0, max_val=a["cache_kv"].shape[1] - 1)
                src = a["cache_kv"][0, bass.ds(pg, 1)].rearrange("o (t a) v g d -> (o t) (v g) a d", a=2)
                s, h = i // 2, i % 2
                for par_ in range(2):
                    eng.dma_start(pairs[h * 64:(h + 1) * 64, s, :, par_, :], src[:, 0:4, par_, :])\
                        .then_inc(sem("load_pairs"), pl.landed("load_pairs"))
                src = a["cache_kv"][0, bass.ds(pg, 1)].rearrange("o t v g d -> (o t) (v g d)")
                eng.dma_start(cache[:, 0, i, :], src[:, 256:512])\
                    .then_inc(sem("load_cache0"), pl.landed("load_cache0", "cache0"))
            for b in range(NB):
                eng.dma_start(out["win_sample"][0, b, 0:PAST - 1].rearrange("t v g d -> t (v g d)"), a["cache_win"][0, b, 1:PAST].rearrange("t v g d -> t (v g d)"))\
                    .then_inc(sem("store_att"), pl.landed("store_att"))
            for f in [f for pair in XR_PAIRS for f in pair]:
                d = kn.rearrange("p v t n -> p (v t n)")[:, 0:NT]
                eng.wait_ge(*at(f"xr_s{f}"))
                eng.wait_ge(*pl.latest())
                eng.tensor_copy(xlast[:, f, :], XR[:, f, T:T + 9])\
                    .then_inc(pl.done, pl.tick("xlast"))
                eng.tensor_tensor(d[:, 0:T], XR[:, f, 0:T], XR[:, f, 1:1 + T], ALU.subtract)\
                    .then_inc(pl.done, pl.tick())
                eng.tensor_tensor(d[:, T:NT], ssf[:, f, :], XR[:, f, 1 + T:1 + NT], ALU.subtract)\
                    .then_inc(pl.done, pl.tick())
                eng.wait_ge(*pl.latest())
                eng.tensor_scalar(d, d, col("shift_mu", f), None, ALU.mult)\
                    .then_inc(pl.done, pl.tick())
                eng.wait_ge(*pl.latest())
                eng.tensor_tensor(XR[:, f, 1:1 + NT], XR[:, f, 1:1 + NT], d, ALU.add)\
                    .then_inc(pl.done, pl.tick(f"sh{f}"))
            def store_factors(f):
                eng.wait_ge(*at(f"prep{f}"))
                eng.dma_start(scratch_f[:, f, :], staged[:, f % 2, :])\
                    .then_inc(sem(f"store_f{f % 2}"), pl.landed(f"store_f{f % 2}", f"stored_f{f}"))

            eng.wait_ge(*at("par_t"))
            for v in range(2):
                eng.dma_start(shf[v * 16:(v + 1) * 16, :], a["cmp_pe"][0, v].rearrange("(l a) d -> l (a d)", a=2))\
                    .then_inc(sem("load_pe"), pl.landed("load_pe", "pe_rows"))
            store_factors(0)
            store_factors(1)
            eng.wait_ge(*at("zkv"))
            for t in range(QT):
                eng.dma_start(out["kv_prompt"][0, 0, t * P:(t + 1) * P].rearrange("t v g d -> t (v g d)"), zkv[:, t, 0:512])\
                    .then_inc(sem("store_kv"), pl.landed("store_kv", "kv_stored"))
            for t in range(QT):
                eng.dma_start(out["win_prompt"][0, 0, t * P:(t + 1) * P].rearrange("t v g d -> t (v g d)"), zkv[:, t, 512:768])\
                    .then_inc(sem("store_att"), pl.landed("store_att"))
            eng.dma_start(out["kv_sample"][0, :, 0].rearrange("b v g d -> b (v g d)"), zkv[0:NB, QT, 0:512])\
                .then_inc(sem("store_att"), pl.landed("store_att"))
            eng.dma_start(out["win_sample"][0, :, PAST - 1].rearrange("b v g d -> b (v g d)"), zkv[0:NB, QT, 512:768])\
                .then_inc(sem("store_att"), pl.landed("store_att"))
            eng.wait_ge(*at("kv_stored"))
            for h in range(2):
                src = out["kv_prompt"][0, 0, h * 256:(h + 1) * 256].rearrange("(t a) v g d -> t (v g) a d", a=2)
                for par_ in range(2):
                    eng.dma_start(pairs[:, NB + h, :, par_, :], src[:, 0:4, par_, :])\
                        .then_inc(sem("load_pairs"), pl.landed("load_pairs", "pairs"))
            store_factors(2)
            store_factors(3)
            eng.wait_ge(*at("dvt"))
            for b in range(NB):
                eng.dma_start(scratch[b].rearrange("h w d -> w h d").rearrange("(o w) h d -> o w h d", o=1), dvt[b:b + 1].rearrange("p w (h d) -> p w h d", h=NH))\
                    .then_inc(sem("store_dv"), pl.landed("store_dv", "dv_stored"))
            eng.wait_ge(*at("stored_f2"))
            eng.wait_ge(*at("stored_f3"))
            for i in range(NPG):
                s, h = i // 2, i % 2
                src = a["cache_win"][0, s, h * P:(h + 1) * P].rearrange("t v g d -> t (v g d)")
                eng.dma_start(cache[:, 1, i, :], src)\
                    .then_inc(sem("load_cache1"), pl.landed("load_cache1", "cache1"))
            eng.wait_ge(*at("gates"))
            for b in range(NB):
                eng.dma_start(scol[b * NH:(b + 1) * NH, 0:3], gate[b:b + 1, QT, :].rearrange("p (h n) -> p h n", n=3))\
                    .then_inc(sem("load_gd"), pl.landed("load_gd", "gd"))
            eng.wait_ge(*at("shift_rows"))
            eng.dma_start(out["shift_prompt"][0], sst[0:1, :])\
                .then_inc(sem("store_att"), pl.landed("store_att"))
            eng.dma_start(out["shift_sample"][0], sst[1:9, :])\
                .then_inc(sem("store_att"), pl.landed("store_att", "stored_att"))
            pl.stage("rwkv")
            eng.wait_ge(*at("end:att:pe"))
            eng.wait_ge(*at("end:att:dve"))
            eng.wait_ge(*at("end:att:act"))
            eng.wait_ge(*at("stored_att"))
            eng.dma_start(g2w, a["g2"][0])\
                .then_inc(sem("load_lr"), pl.landed("load_lr", "g2w"))
            eng.dma_start(S.rearrange("p i j -> p (i j)"), a["state_wkv"][0].rearrange("b h (s i) j -> (b h s) (i j)", s=2))\
                .then_inc(sem("load_S"), pl.landed("load_S", "S"))
            eng.wait_ge(*at("dv_stored"))
            for s in range(2):
                eng.dma_start(dvr[s:P:2, :, :], scratch.rearrange("b h w d -> (b h) w d"))\
                    .then_inc(sem("load_dv"), pl.landed("load_dv", "dvr"))
            for h in range(2):
                eng.dma_start(vrow[h:P:2, :], scratch[:, :, 5, h * 32:(h + 1) * 32].rearrange("b h i -> (b h) i"))\
                    .then_inc(sem("load_dv"), pl.landed("load_dv", "dvr"))
            eng.wait_ge(*at("dvr"))
            eng.wait_ge(*at("S"))

            def rows_of(v, h):
                return v[:, h * 16:(h + 1) * 16].unsqueeze(2).to_broadcast([P, 16, HD])

            def over_rows(w):
                return dvr[:, w, :].unsqueeze(1).to_broadcast([P, 16, HD])

            for h in range(2):
                Sh = S[:, h * 16:(h + 1) * 16, :]
                eng.tensor_tensor(S2, Sh, over_rows(1), ALU.mult)\
                    .then_inc(pl.done, pl.tick(f"sa_in{h}"))
                eng.wait_ge(*at(f"sa_sum{h}"))
                eng.tensor_tensor(Sh, Sh, over_rows(0), ALU.mult)\
                    .then_inc(pl.done, pl.tick())
                eng.tensor_tensor(S2, rows_of(sa, h), over_rows(2), ALU.mult)\
                    .then_inc(pl.done, pl.tick())
                eng.wait_ge(*pl.latest())
                eng.tensor_tensor(Sh, Sh, S2, ALU.add)\
                    .then_inc(pl.done, pl.tick())
                eng.wait_ge(*pl.latest())
                eng.tensor_tensor(S2, rows_of(vrow, h), over_rows(3), ALU.mult)\
                    .then_inc(pl.done, pl.tick())
                eng.wait_ge(*pl.latest())
                eng.tensor_tensor(Sh, Sh, S2, ALU.add)\
                    .then_inc(pl.done, pl.tick())
                eng.wait_ge(*pl.latest())
                eng.tensor_tensor(S2, Sh, over_rows(4), ALU.mult)\
                    .then_inc(pl.done, pl.tick(f"yd_in{h}"))
                eng.wait_ge(*at(f"yd_sum{h}"))
            eng.wait_ge(*pl.latest())
            eng.dma_start(out["wkv_sample"][0].rearrange("b h (s i) j -> (b h s) (i j)", s=2), S.rearrange("p i j -> p (i j)"))\
                .then_inc(sem("store_rwkv"), pl.landed("store_rwkv"))
            eng.dma_start(scratch_y.rearrange("b (q i) -> (b q) i", i=32), yd)\
                .then_inc(sem("store_y"), pl.landed("store_y", "y_stored"))
            eng.wait_ge(*at("y_stored"))
            eng.dma_start(ydt, scratch_y)\
                .then_inc(sem("load_y"), pl.landed("load_y", "ydt"))
            eng.wait_ge(*at("wkt"))
            eng.dma_start(out["wkv_prompt"][0, 0].rearrange("h i j -> i h j"), wkt.rearrange("p (h j) -> p h j", h=NH))\
                .then_inc(sem("store_rwkv"), pl.landed("store_rwkv", "stored_rwkv"))
            pl.end("rwkv")
            eng.wait_ge(*at("end:rwkv:pe"))
            eng.wait_ge(*at("end:rwkv:dve"))
            eng.wait_ge(*at("end:rwkv:act"))
            eng.wait_ge(*at("stored_rwkv"))
            eng.wait_ge(*at("ydt"))
            for t in range(QT):
                eng.dma_start(pst[:, t, :], a["p_prompt"][0, 0, t * P:(t + 1) * P, :])\
                    .then_inc(sem("load_p"), pl.landed("load_p", "p"))
            eng.dma_start(pst[0:NB, QT, :], a["p_sample"][0, :, 0, :])\
                .then_inc(sem("load_p"), pl.landed("load_p", "p"))
            for t in range(QT):
                eng.wait_ge(*at(f"y{t}"))
                eng.dma_start(out["y_prompt"][0, t * P:(t + 1) * P, :], ot[:, t, :])\
                    .then_inc(sem("store_end"), pl.landed("store_end"))
            eng.wait_ge(*at(f"y{QT}"))
            eng.dma_start(out["y_sample"][:, 0, :], ot[0:NB, QT, :])\
                .then_inc(sem("store_end"), pl.landed("store_end", "stored_all"))
            eng.wait_ge(*at("stored_all"))

        def place(h):
            return h // 4 * 4 + h % 2 * 2 + h // 2 % 2

        @block.tensor
        def _(eng):
            pe = steps["pe"]
            mm = eng.matmul

            def banks(b):
                turn["banks"], turn["next"] = list(b), 0

            def open_(name, fixed=None):
                which = fixed
                if which is None:
                    which = turn["banks"][turn["next"] % len(turn["banks"])]
                    turn["next"] += 1
                if which in bank_user:
                    eng.wait_ge(*at(("free", bank_user[which])))
                bank_user[which] = name
                points.new[("bank", name)] = which
                return psum[:, which, :]

            def turn_(dst, src, n=P):
                return mm(dst, src, ident[0:n, 0:n], is_transpose=True, start=True, stop=True)

            pe.stage("load")
            eng.wait_ge(*at("x"))
            eng.wait_ge(*at("ident"))
            for k in range(KD):
                ps = open_(f"x{k}")
                for t in range(QT):
                    turn_(ps[:, t * P:(t + 1) * P], xstage[:, t, k * P:(k + 1) * P])\
                        .then_inc(pe.done, pe.tick(*([f"x{k}"] if t == QT - 1 else ())))
            ps = open_("xd")
            for k in range(KD):
                turn_(ps[:, k * NB:(k + 1) * NB], xstage[0:NB, QT, k * P:(k + 1) * P], NB)\
                    .then_inc(pe.done, pe.tick(*(["xd"] if k == KD - 1 else ())))
            eng.wait_ge(*at("par"))
            ps = open_("par_t")
            turn_(ps[:, 0:P], par_rows[:, :], P)\
                .then_inc(pe.done, pe.tick("par_t"))
            eng.wait_ge(*at("ss"))
            ps = open_("ss_t")
            for f in range(XF):
                turn_(ps[:, f * NB:(f + 1) * NB], sst[0:NB, f * P:(f + 1) * P], NB)\
                    .then_inc(pe.done, pe.tick(*(["ss_t"] if f == XF - 1 else ())))

            def mean_square(which):
                pe.stage("norm")
                pss = [open_(f"{which}ms{h}") for h in range(2)]
                for k in range(KD):
                    eng.wait_ge(*at(f"{which}sq{k}"))
                    for h, (lo, hi) in enumerate(HALFS):
                        mm(pss[h][:, 0:hi - lo], ones[:, :], sq[:, k % 2, lo:hi], start=(k == 0), stop=(k == KD - 1))\
                            .then_inc(pe.done, pe.tick(f"{which}ms{h}" if k == KD - 1 else f"{which}sqd{k}"))

            def dense(group, c, j, rhs, nk=KD, k0=0, start=True, stop=True, pss=None, used=False):
                w = slot(c)
                pss = pss or [open_(f"{group}h{h}") for h in range(2)]
                for h, (lo, hi) in enumerate(HALFS):
                    for k in range(nk):
                        names = []
                        if stop and k == nk - 1:
                            names.append(f"{group}h{h}")
                        if used and k == nk - 1 and h == 1:
                            names.append(("used", c))
                        mm(pss[h][:, 0:hi - lo], w[:, k, j * P:(j + 1) * P], rhs[:, k0 + k, lo:hi], start=(start and k == 0), stop=(stop and k == nk - 1))\
                            .then_inc(pe.done, pe.tick(*names))

            def dense3(group, c, j, hi_x, lo_x, nk=KD, k0=0, start=True, stop=True, pss=None, used=False, wait=None):
                _, w1_, w2_ = split_parts(c)
                w1_, w2_ = (w.rearrange("p (k n) -> p k n", n=256) for w in (w1_, w2_))
                pss = pss or [open_(f"{group}h{h}") for h in range(2)]
                for h, (lo, hi) in enumerate(HALFS):
                    for k in range(nk):
                        if wait and h == 0:
                            eng.wait_ge(*at(f"{wait}{k}"))
                        for i, (w, x) in enumerate(((w1_, hi_x), (w1_, lo_x), (w2_, hi_x))):
                            last = k == nk - 1 and i == 2
                            names = []
                            if stop and last:
                                names.append(f"{group}h{h}")
                            if used and last and h == 1:
                                names.append(("used", c))
                            mm(pss[h][:, 0:hi - lo], w[:, k, j * P:(j + 1) * P], x[:, k0 + k, lo:hi], start=(start and k == 0 and i == 0), stop=(stop and last))\
                                .then_inc(pe.done, pe.tick(*names))

            mean_square("mix")
            pe.stage("proj")
            eng.wait_ge(*at("mixh"))

            def xr_chunk(c):
                eng.wait_ge(*at(("got", ("xr", c))))
                for j, f in enumerate(XR_PAIRS[c]):
                    dense(f"xr{f}", ("xr", c), j, hT, used=(j == 1))

            def kv_chunk(c):
                eng.wait_ge(*at(("got", ("kv", c))))
                w = slot(("kv", c))
                for t in range(QT + 1):
                    m = P if t < QT else NB
                    ps = open_(f"kv{c}_{t}")
                    for k in range(KD):
                        names = [f"kv{c}_{t}"] if k == KD - 1 else []
                        if k == KD - 1 and t == QT:
                            names.append(("used", ("kv", c)))
                        mm(ps[0:m, 0:256], hT[:, k, t * P:t * P + m], w[:, k, :], start=(k == 0), stop=(k == KD - 1))\
                            .then_inc(pe.done, pe.tick(*names))

            def gates_chunk():
                eng.wait_ge(*at(("got", ("gates", 0))))
                w = slot(("gates", 0))
                ps = open_("gates_p")
                for t in range(QT + 1):
                    m = P if t < QT else NB
                    for k in range(KD):
                        last = t == QT and k == KD - 1
                        mm(ps[0:m, t * GATES:(t + 1) * GATES], hT[:, k, t * P:t * P + m], w[:, k, 0:GATES], start=(k == 0), stop=(k == KD - 1))\
                            .then_inc(pe.done, pe.tick(*(["gates_p", ("used", ("gates", 0))] if last else [])))

            def q_chunk(c):
                eng.wait_ge(*at(("got", ("q", c))))
                for j in range(2):
                    dense(f"q{2 * c + j}", ("q", c), j, hT, used=(j == 1))

            def low_rank(f):
                if f == 0:
                    eng.wait_ge(*at("lr_w"))
                    eng.wait_ge(*at("lr_w_in"))
                for name, x0 in (("dec", 0), ("av", HD)):
                    for h, (lo, hi) in enumerate(HALFS):
                        ps = open_(f"{name}{f}h{h}")
                        mm(ps[:, 0:hi - lo], lr_w[x0:x0 + HD, f * P:(f + 1) * P], XR[x0:x0 + HD, 12, 1 + lo:1 + hi], start=True, stop=True)\
                            .then_inc(pe.done, pe.tick(f"{name}{f}h{h}"))

            def head_sums(name, i, f):
                eng.wait_ge(*at(f"{name}_in{f}"))
                for h, (lo, hi) in enumerate(HALFS):
                    ps = open_(f"{name}{f}h{h}")
                    mm(ps[:, 0:hi - lo], blk[:, :], sq[:, i, lo:hi], start=True, stop=True)\
                        .then_inc(pe.done, pe.tick(f"{name}{f}h{h}"))

            xr_chunk(0)
            xr_chunk(1)
            xr_chunk(2)
            low_rank(0)
            xr_chunk(3)
            eng.wait_ge(*at("masks"))
            head_sums("kks", 0, 0)
            xr_chunk(4)
            head_sums("bs", 1, 0)
            low_rank(1)
            xr_chunk(5)
            head_sums("kks", 0, 1)
            xr_chunk(6)
            head_sums("bs", 1, 1)
            low_rank(2)
            kv_chunk(0)
            head_sums("kks", 0, 2)
            kv_chunk(1)
            head_sums("bs", 1, 2)
            low_rank(3)
            kv_chunk(2)
            head_sums("kks", 0, 3)
            gates_chunk()
            q_chunk(0)
            head_sums("bs", 1, 3)
            q_chunk(1)
            eng.wait_ge(*at("prep3"))
            for w in range(6):
                ps = open_(f"dv{w}")
                for f in range(4):
                    turn_(ps[0:NB, f * P:(f + 1) * P], dv[:, w, f, :], P)\
                        .then_inc(pe.done, pe.tick(*([f"dv{w}"] if f == 3 else ())))
            pe.stage("att")
            eng.wait_ge(*at("masks"))
            for f in range(XF):
                if f % 4 == 0:
                    ps = open_(f"xrl{f // 4}")
                    eng.wait_ge(*at("xlast"))
                turn_(ps[0:9, (f % 4) * P:(f % 4 + 1) * P], xlast[:, f, :], P)\
                    .then_inc(pe.done, pe.tick(*([f"xrl{f // 4}"] if f % 4 == 3 or f == XF - 1 else ())))
            eng.wait_ge(*at("pairs"))
            for v in range(2):
                for g in range(G):
                    for s0 in (0, 4, 8):
                        n = min(4, 10 - s0)
                        ps = open_(f"pair{v}{g}{s0}")
                        for s in range(n):
                            turn_(ps[:, s * P:(s + 1) * P], pairs[:, s0 + s, 2 * v + g, :, :].rearrange("p a d -> p (a d)"), P)\
                                .then_inc(pe.done, pe.tick(*([f"pair{v}{g}{s0}", "pairs_turned"] if s == n - 1 else ())))
            eng.wait_ge(*at("pe_rows"))
            ps = open_("pe_t")
            turn_(ps[:, 0:32], shf[0:32, :], 32)\
                .then_inc(pe.done, pe.tick("pe_t"))
            def windows(v):
                pss = [open_(f"conv{v}{m}") for m in range(2)]
                xv = xcmp[:, v, :].rearrange("p (w i) -> p w i", i=8)
                for l in range(16):
                    c = ("w1", 2 * v + l // 8)
                    eng.wait_ge(*at(("got", c)))
                    for m in range(2):
                        names = [("used", c)] if l % 8 == 7 and m == 1 else []
                        if l == 15:
                            names.append(f"conv{v}{m}")
                        mm(pss[m][:, 0:NWIN], slot(c)[:, l % 8, m * P:(m + 1) * P], xv[:, l // 8:l // 8 + NWIN, l % 8], start=(l == 0), stop=(l == 15))\
                            .then_inc(pe.done, pe.tick(*names))

            def second_layer(v):
                eng.wait_ge(*at(f"gel{v}"))
                eng.wait_ge(*at("w2c"))
                ps = open_(f"cmp{v}")
                for g in range(G):
                    for m in range(2):
                        mm(ps[g * HD:(g + 1) * HD, 0:160], w2c[:, v, m, :], gel[:, m, g * 160:(g + 1) * 160], start=(m == 0), stop=(m == 1))\
                            .then_inc(pe.done, pe.tick(f"cmp{v}"))

            def decode_keys(v):
                for i0 in range(0, NPG, 4):
                    ps = open_(f"ck{v}_{i0}")
                    for i in range(4):
                        eng.wait_ge(*at(f"ckn{v}"))
                        turn_(ps[:, i * P:(i + 1) * P], cache[:, v, i0 + i, 0:P], P)\
                            .then_inc(pe.done, pe.tick(*([f"ck{v}_{i0}"] if i == 3 else ())))
                eng.wait_ge(*at(f"dkn{v}"))
                ps = open_(f"dk{v}")
                turn_(ps[:, 0:NB], dkn[:, v * P:(v + 1) * P], NB)\
                    .then_inc(pe.done, pe.tick(f"dk{v}"))

            def q_squares(r):
                eng.wait_ge(*at(f"qsq{r}"))
                for h, (lo, hi) in enumerate(HALFS):
                    ps = open_(f"qms{r}h{h}")
                    mm(ps[:, 0:hi - lo], blk[:, :], sq[:, r % 2, lo:hi], start=True, stop=True)\
                        .then_inc(pe.done, pe.tick(f"qms{r}h{h}"))

            q_squares(0)
            q_squares(1)
            eng.wait_ge(*at("xcmp"))
            windows(0)
            for v in range(2):
                eng.wait_ge(*at(f"kn{v}"))
                ps = open_(f"kT{v}")
                for t in range(QT):
                    turn_(ps[:, t * P:(t + 1) * P], kn[:, v, t, :], P)\
                        .then_inc(pe.done, pe.tick(*([f"kT{v}"] if t == QT - 1 else ())))
            q_squares(2)
            q_squares(3)
            windows(1)
            second_layer(0)
            decode_keys(0)
            second_layer(1)
            decode_keys(1)
            eng.wait_ge(*at("kcsq"))
            ps = open_("kcms")
            mm(ps[:, 0:160], blk[:, :], sq[:, 0, 0:160], start=True, stop=True)\
                .then_inc(pe.done, pe.tick("kcms"))
            eng.wait_ge(*at("vc"))
            ps = open_("vc_t")
            turn_(ps[:, 0:P], vc[:, 0:P])\
                .then_inc(pe.done, pe.tick())
            turn_(ps[0:NCP, P:2 * P], vc[:, P:P + NCP], P)\
                .then_inc(pe.done, pe.tick("vc_t"))
            eng.wait_ge(*at("qb"))
            for v in range(2):
                eng.wait_ge(*at(f"kTd{v}"))
                ps = open_(f"sd{v}")
                for b in range(NB):
                    mm(ps[0:64, 0:257], qb[:, b, :], kTd[:, v, b, :], start=(b == 0), stop=(b == NB - 1))\
                        .then_inc(pe.done, pe.tick(*([f"sd{v}"] if b == NB - 1 else [])))
            eng.wait_ge(*at("kcn"))
            ps = open_("sdc")
            mm(ps[0:64, 0:P], qall, kcn[:, 0:P], start=True, stop=True)\
                .then_inc(pe.done, pe.tick("sdc"))
            eng.wait_ge(*at("pdc"))
            ps = open_("ptc")
            mm(ps[:, 0:64], pcs[:, 0:P], diag[0:64, 2, 0:64], start=True, stop=True)\
                .then_inc(pe.done, pe.tick("ptc"))
            od = open_("od")
            eng.wait_ge(*at("ptcs"))
            eng.wait_ge(*at("vcd"))
            mm(od[:, 0:64], vcd, ptb[:, 0, 448:512], start=True, stop=True, skip_group_check=True)\
                .then_inc(pe.done, pe.tick())
            for v in range(2):
                eng.wait_ge(*at(f"pd{v}"))
                ps = open_(f"ptd{v}")
                for t in range(2):
                    mm(ps[:, t * 64:(t + 1) * 64], pbuf[0:64, v, t * P:(t + 1) * P], diag[0:64, v, 0:64], start=True, stop=True)\
                        .then_inc(pe.done, pe.tick())
                mm(ps[0:NB, 128:192], st[0:64, 64 + v * NB:64 + (v + 1) * NB], diag[0:64, v, 0:64], start=True, stop=True)\
                    .then_inc(pe.done, pe.tick(f"ptd{v}"))
                eng.wait_ge(*at(f"ptds{v}"))
                mm(od[:, 0:64], zkv[0:NB, QT, 384 + 256 * v:512 + 256 * v], ptb[0:NB, v, 128:192], start=False, stop=True, skip_group_check=True)\
                    .then_inc(pe.done, pe.tick())
                for b in range(NB):
                    for t in range(2):
                        last = v == 1 and b == NB - 1 and t == 1
                        mm(od[:, b * NH:(b + 1) * NH], cache[:, v, 2 * b + t, P:2 * P], ptb[:, v, t * 64 + b * NH:t * 64 + (b + 1) * NH], start=False, stop=True, skip_group_check=True)\
                            .then_inc(pe.done, pe.tick(*(["od"] if last else [])))
            banks(range(6))
            units = [(qt, r, g, v) for qt in range(QT) for r in range(R) for g in range(G) for v in range(2)]
            PER = len(units) // QT
            AHEAD = 3

            def scores(i):
                qt, r, g, v = units[i]
                n = (qt + 1) * P
                ps = open_(f"s{i}")
                mm(ps[:, 0:n], qT[g * HD:(g + 1) * HD, r, qt * P:(qt + 1) * P], kT[g * HD:(g + 1) * HD, v, 0:n], start=True, stop=True)\
                    .then_inc(pe.done, pe.tick(f"s{i}"))

            def block_scores(qt):
                ps = open_(f"sc{qt}")
                for g in range(G):
                    if g:
                        eng.wait_ge(*pe.latest())
                    for r in range(R):
                        h = g * R + r
                        mm(ps[:, h * NCP:(h + 1) * NCP], qT[g * HD:(g + 1) * HD, r, qt * P:(qt + 1) * P], kcn[g * HD:(g + 1) * HD, P:P + NCP], start=True, stop=True)\
                            .then_inc(pe.done, pe.tick(f"sc{qt}"))

            def block_turn(qt):
                eng.wait_ge(*at(f"pc{qt}"))
                for h2 in range(2):
                    ps = open_(f"ptc{qt}_{h2}")
                    for i in range(4):
                        turn_(ps[0:NCP, i * P:(i + 1) * P], pcm[:, h2 * 4 + i, :], P)\
                            .then_inc(pe.done, pe.tick(f"ptc{qt}_{h2}"))

            def turned(i):
                eng.wait_ge(*at(f"p{i}"))
                ps = open_(f"pt{i}")
                for j in range(units[i][0] + 1):
                    mm(ps[:, j * P:(j + 1) * P], pbuf[:, i % 4, j * P:(j + 1) * P], diag[:, i % 4, :], start=True, stop=True)\
                        .then_inc(pe.done, pe.tick(f"pt{i}"))

            def values(i):
                qt, r, g, v = units[i]
                if i % PER == 0:
                    open_(f"o{qt}", 6 + qt % 2)
                o = psum[g * HD:(g + 1) * HD, 6 + qt % 2, r * P:(r + 1) * P]
                if v == 0:
                    eng.wait_ge(*at(f"ptcs{qt}_{g}"))
                    mm(o, vcp[0:NCP, g * HD:(g + 1) * HD], ptcb[0:NCP, qt % 2, g * R + r, :], start=True, stop=True, skip_group_check=True)\
                        .then_inc(pe.done, pe.tick())
                eng.wait_ge(*at(f"pts{i}"))
                for j in range(qt + 1):
                    mm(o, zkv[:, j, 384 + 256 * v + g * HD:384 + 256 * v + (g + 1) * HD], ptb[:, i % 2, j * P:(j + 1) * P], start=False, stop=True, skip_group_check=True)\
                        .then_inc(pe.done, pe.tick(f"pv{i}", f"o{qt}"))

            eng.wait_ge(*at("kTs"))
            eng.wait_ge(*at("qTs"))
            block_scores(0)
            for i in range(AHEAD):
                scores(i)
            block_turn(0)
            for i in range(len(units)):
                qt, u = divmod(i, PER)
                if qt + 1 < QT and u == 8:
                    block_scores(qt + 1)
                if qt + 1 < QT and u == 12:
                    block_turn(qt + 1)
                if i + AHEAD < len(units):
                    scores(i + AHEAD)
                turned(i)
                if i:
                    values(i - 1)
            values(len(units) - 1)
            pe.end("att")

            pe.stage("rwkv")
            eng.wait_ge(*at("end:att:dve"))
            eng.wait_ge(*at("end:att:act"))
            eng.wait_ge(*at("stored_att"))
            banks(range(8))
            def rows_of_tokens(w, c):
                ps = open_(f"tm{w}{c}")
                for f in range(4):
                    s_ = slice(c * P, (c + 1) * P)
                    x = (AR[:, f, c, 0:P], BH[:, f, s_], KH[:, f, s_], XR[:, 8 + f, 1 + c * P:1 + (c + 1) * P])[w]
                    turn_(ps[:, f * P:(f + 1) * P], x, P)\
                        .then_inc(pe.done, pe.tick(*([f"tm{w}{c}"] if f == 3 else ())))

            for c in range(QT):
                rows_of_tokens(3, c)
            eng.wait_ge(*at("factors"))
            for w in range(3):
                rows_of_tokens(w, 0)
            eng.wait_ge(*at("Hm0"))
            banks(range(4))
            for c in range(QT):
                for hg in range(2):
                    for name, lhs in (("ln", BH), ("mq", KH)):
                        for i in range(2):
                            ps = open_(f"{name}{c}{hg}{i}")
                            lo = i * HD
                            for fp in range(2):
                                f = hg * 2 + fp
                                mm(ps[:, fp * 256:(fp + 1) * 256], lhs[lo:lo + HD, f, c * P:(c + 1) * P], AR[lo:lo + HD, f, c, :], start=True, stop=True)\
                                    .then_inc(pe.done, pe.tick(f"{name}{c}{hg}{i}"))
                    ps = open_(f"l{c}{hg}")
                    for i in range(2):
                        if i:
                            eng.wait_ge(*pe.latest())
                        lo = i * HD
                        for fp in range(2):
                            f = hg * 2 + fp
                            mm(ps[:, (i * 2 + fp) * P:(i * 2 + fp + 1) * P], AR[lo:lo + HD, f, c, 0:P], BH[lo:lo + HD, f, c * P:(c + 1) * P], start=True, stop=True)\
                                .then_inc(pe.done, pe.tick(f"l{c}{hg}"))
                Tb, TTb = {}, {}
                for hg in range(2):
                    Tb[hg] = open_(f"T{c}{hg}", 4 + hg)
                    TTb[hg] = open_(f"TT{c}{hg}", 6 + hg)
                    eng.wait_ge(*at(f"Ts{c}{hg}_1"))
                    mm(Tb[hg], ident[:, :], Tsb[:, hg, :], start=True, stop=True, skip_group_check=True)\
                        .then_inc(pe.done, pe.tick())
                    eng.wait_ge(*at(f"TTs{c}{hg}_1"))
                    mm(TTb[hg], ident[:, :], TTsb[:, hg, :], start=True, stop=True, skip_group_check=True)\
                        .then_inc(pe.done, pe.tick())
                for n in LEVELS:
                    if n in (8, 16, 32) and c + 1 < QT:
                        rows_of_tokens((8, 16, 32).index(n), c + 1)
                    for hg in range(2):
                        ps = open_(f"X{c}{hg}_{n}")
                        eng.wait_ge(*at(f"Ts{c}{hg}_{n // 2}"))
                        for i in range(4):
                            mm(ps[:, i * P:(i + 1) * P], LN[:, hg * 4 + i, 0:P], Tsb[:, hg, i * P:(i + 1) * P], start=True, stop=True)\
                                .then_inc(pe.done, pe.tick(f"X{c}{hg}_{n}"))
                    for hg in range(2):
                        eng.wait_ge(*at(f"Xs{c}{hg}_{n}"))
                        eng.wait_ge(*at(f"TTs{c}{hg}_{n // 2}"))
                        if n < 64:
                            for i in range(4):
                                s_ = slice(i * P, (i + 1) * P)
                                mm(Tb[hg][:, s_], TTsb[:, hg, s_], Xs[:, hg, s_], start=False, stop=True, skip_group_check=True)\
                                    .then_inc(pe.done, pe.tick(f"T{c}{hg}_{n}"))
                        for i in range(4):
                            s_ = slice(i * P, (i + 1) * P)
                            mm(TTb[hg][:, s_], Xs[:, hg, s_], TTsb[:, hg, s_], start=False, stop=True, skip_group_check=True)\
                                .then_inc(pe.done, pe.tick(f"TT{c}{hg}_{n}"))
                ps = open_(f"mv{c}")
                for h in range(NH):
                    mm(ps[:, h * HD:(h + 1) * HD], MQ[:, place(h), 0:P], tm[:, 3, c, h * HD:(h + 1) * HD], start=True, stop=True)\
                        .then_inc(pe.done, pe.tick(f"mv{c}"))
                ps = open_(f"ap{c}")
                eng.wait_ge(*at(f"TTs{c}0_64"))
                eng.wait_ge(*at(f"TTs{c}1_64"))
                for h in range(NH):
                    lo = (h % 2) * HD
                    mm(ps[lo:lo + HD, (h // 2) * P:(h // 2 + 1) * P], tm[:, 0, c, h * HD:(h + 1) * HD], TTsb[:, h // 4, (place(h) % 4) * P:(place(h) % 4 + 1) * P], start=True, stop=True)\
                        .then_inc(pe.done, pe.tick(f"ap{c}"))
                eng.wait_ge(*at(f"mvs{c}"))
                ps = open_(f"u{c}")
                for h in range(NH):
                    mm(ps[:, h * HD:(h + 1) * HD], TTsb[:, h // 4, (place(h) % 4) * P:(place(h) % 4 + 1) * P], MV[:, h * HD:(h + 1) * HD], start=True, stop=True)\
                        .then_inc(pe.done, pe.tick(f"u{c}"))
                eng.wait_ge(*at(f"aps{c}"))
                eng.wait_ge(*at(f"Hm{c}"))
                ps = open_(f"sa{c}")
                for h in (0, 2, 4, 6, 1, 3, 5, 7):
                    if h == 1:
                        eng.wait_ge(*pe.latest())
                    lo, f = (h % 2) * HD, h // 2
                    mm(ps[:, h * HD:(h + 1) * HD], ApT[lo:lo + HD, f, :], Hm[lo:lo + HD, f, :], start=True, stop=True)\
                        .then_inc(pe.done, pe.tick(f"sa{c}"))
                eng.wait_ge(*at(f"sas{c}"))
                ps = open_(f"H{c}")
                for h in range(NH):
                    lo, f = (h % 2) * HD, h // 2
                    o = ps[lo:lo + HD, f * HD:(f + 1) * HD]
                    mm(o, tm[:, 1, c, h * HD:(h + 1) * HD], SA[:, h * HD:(h + 1) * HD], start=True, stop=False)\
                        .then_inc(pe.done, pe.tick())
                    mm(o, tm[:, 2, c, h * HD:(h + 1) * HD], tm[:, 3, c, h * HD:(h + 1) * HD], start=False, stop=True)\
                        .then_inc(pe.done, pe.tick(f"H{c}"))
                ps = open_(f"y{c}p")
                for h in range(NH):
                    lo, f = (h % 2) * HD, h // 2
                    o = ps[lo:lo + HD, f * P:(f + 1) * P]
                    mm(o, Hm[lo:lo + HD, f, :], AR[lo:lo + HD, f, c, P:2 * P], start=True, stop=False)\
                        .then_inc(pe.done, pe.tick())
                    mm(o, SA[:, h * HD:(h + 1) * HD], LN[:, place(h), P:2 * P], start=False, stop=False)\
                        .then_inc(pe.done, pe.tick())
                    mm(o, tm[:, 3, c, h * HD:(h + 1) * HD], MQ[:, place(h), P:2 * P], start=False, stop=True)\
                        .then_inc(pe.done, pe.tick(f"y{c}p"))
            eng.wait_ge(*at("Hend"))
            ps = open_("wk")
            for f in range(4):
                turn_(ps[0:HD, f * P:(f + 1) * P], Hs[:, f, :], P)\
                    .then_inc(pe.done, pe.tick(*(["wk"] if f == 3 else ())))
            eng.wait_ge(*at("ydt"))
            ps = open_("yd")
            for f in range(4):
                turn_(ps[:, f * NB:(f + 1) * NB], ydt[:, f * P:(f + 1) * P], NB)\
                    .then_inc(pe.done, pe.tick(*(["yd"] if f == 3 else ())))
            banks(range(8))
            eng.wait_ge(*at("g2w"))
            for f in range(4):
                eng.wait_ge(*at(f"yall"))
                for h, (lo, hi) in enumerate(HALFS):
                    ps = open_(f"gm{f}h{h}")
                    mm(ps[:, 0:hi - lo], blk[:, :], oT[:, 4 + f, lo:hi], start=True, stop=True)\
                        .then_inc(pe.done, pe.tick(f"gm{f}h{h}"))
                eng.wait_ge(*at(f"gsq{f}"))
                for h, (lo, hi) in enumerate(HALFS):
                    ps = open_(f"gv{f}h{h}")
                    mm(ps[:, 0:hi - lo], blk[:, :], sq[:, f % 2, lo:hi], start=True, stop=True)\
                        .then_inc(pe.done, pe.tick(f"gv{f}h{h}"))
                for h, (lo, hi) in enumerate(HALFS):
                    ps = open_(f"gg{f}h{h}")
                    mm(ps[:, 0:hi - lo], g2w[:, f * P:(f + 1) * P], XR[:, 13, 1 + lo:1 + hi], start=True, stop=True)\
                        .then_inc(pe.done, pe.tick(f"gg{f}h{h}"))
            pe.end("rwkv")

            pe.stage("ffn")
            eng.wait_ge(*at("end:rwkv:dve"))
            eng.wait_ge(*at("end:rwkv:act"))
            eng.wait_ge(*at("end:rwkv:pool"))
            eng.wait_ge(*at("stored_rwkv"))
            for c in range(4):
                eng.wait_ge(*at(("lo", ("wo", c))))
                for j in range(2):
                    dense3(f"wo{2 * c + j}", ("wo", c), j, x_hi, x_lo, used=(j == 1), wait=None if c or j else "olo")
            mean_square("ffn")
            pe.stage("ffn")
            for c in range(11):
                for w in ("wg", "wu"):
                    eng.wait_ge(*at(("lo", (w, c))))
                    for j in range(2):
                        dense3(f"{w}{2 * c + j}", (w, c), j, x_hi, x_lo, used=(j == 1), wait="ffnlo" if w == "wg" and c + j == 0 else None)
            for c in range(4):
                pss = [[open_(f"wd{2 * c + j}h{h}") for h in range(2)] for j in range(2)]
                for i in range(3):
                    eng.wait_ge(*at(("lo", ("wd", c, i))))
                    eng.wait_ge(*at(f"act_lo{min(FT, 8 * i + 8) - 1}"))
                    for j in range(2):
                        dense3(f"wd{2 * c + j}", ("wd", c, i), j, act_hi, act_lo, min(8, FT - 8 * i), 8 * i, start=(i == 0),
                               stop=(i == 2), pss=pss[j], used=(j == 1))
            eng.wait_ge(*at("p"))
            for k in range(2):
                ps = open_(f"pe{k}")
                for t in range(QT):
                    turn_(ps[:, t * P:(t + 1) * P], pst[:, t, k * P:(k + 1) * P], P)\
                        .then_inc(pe.done, pe.tick(*([f"pe{k}"] if t == QT - 1 else ())))
            ps = open_("pd")
            for k in range(2):
                turn_(ps[:, k * NB:(k + 1) * NB], pst[0:NB, QT, k * P:(k + 1) * P], NB)\
                    .then_inc(pe.done, pe.tick("pd"))
            mean_square("ple")
            pe.stage("ffn")
            eng.wait_ge(*at("pTs"))
            eng.wait_ge(*at(("got", ("wp", 0))))
            w = slot(("wp", 0), D)
            for m in range(KD):
                for h, (lo, hi) in enumerate(HALFS):
                    ps = open_(f"wp{m}h{h}")
                    for k in range(2):
                        names = [f"wp{m}h{h}"] if k == 1 else []
                        if m == KD - 1 and h == 1 and k == 1:
                            names.append(("used", ("wp", 0)))
                        mm(ps[:, 0:hi - lo], w[:, k, m * P:(m + 1) * P], pT[:, k, lo:hi], start=(k == 0), stop=(k == 1))\
                            .then_inc(pe.done, pe.tick(*names))
            for c in range(4):
                eng.wait_ge(*at(("lo", ("wpg", c))))
                for j in range(2):
                    dense3(f"wpg{2 * c + j}", ("wpg", c), j, x_hi, x_lo, used=(j == 1), wait=None if c or j else "plelo")
            for t in range(QT + 1):
                m = P if t < QT else NB
                for k2 in range(2):
                    ps = open_(f"out{t}{k2}")
                    for k in range(4):
                        eng.wait_ge(*at(f"xfin{k2 * 4 + k}"))
                        turn_(ps[0:m, k * P:(k + 1) * P], xT[:, k2 * 4 + k, t * P:t * P + m], P)\
                            .then_inc(pe.done, pe.tick(*([f"out{t}{k2}"] if k == 3 else ())))


        @block.scalar
        def _(eng):
            ac = steps["act"]

            def squares(which, xs):
                ac.stage("norm")
                for k in range(KD):
                    eng.wait_ge(*at(xs(k)))
                    if k >= 2:
                        eng.wait_ge(*at(f"{which}sqd{k - 2}"))
                    eng.activation(sq[:, k % 2, :], xT[:, k, :], ACT.Square)\
                        .then_inc(ac.done, ac.tick(f"{which}sq{k}"))
                for h, (lo, hi) in enumerate(HALFS):
                    eng.wait_ge(*at(f"{which}ms{h}"))
                    eng.activation(rstd[:, lo:hi], bank(f"{which}ms{h}")[:, 0:hi - lo], ACT.Sqrt, scale=1.0 / D, bias=eps[:, 0:1])\
                        .then_inc(ac.done, ac.tick(f"{which}rt{h}", ("free", f"{which}ms{h}")))

            for t in range(QT):
                eng.dma_start(xstage[:, t, :], a["x_prompt"][0, t * P:(t + 1) * P, :])\
                    .then_inc(sem("load_x"), ac.landed("load_x"))
            eng.dma_start(xstage[0:NB, QT, :], a["x_sample"][:, 0, :])\
                .then_inc(sem("load_x"), ac.landed("load_x", "x"))
            eng.wait_ge(*at("par_zero"))
            for name, (r0, n) in ROWS.items():
                src = a[name][0]
                if name in ("q_norm", "cmp_b2", "k_norm"):
                    src = src.rearrange("(r d) -> r d", r=1) if name == "q_norm" else src
                    for g in range(G):
                        eng.dma_start(par_rows[r0:r0 + n, g * HD:(g + 1) * HD], src)\
                            .then_inc(sem("load_par"), ac.landed("load_par", "par"))
                    continue
                if name == "r_k":
                    src = src.rearrange("(f h) d -> f (h d)", h=2)
                elif name == "cmp_b1":
                    src = src.rearrange("v (m c) -> (v m) c", c=P)
                else:
                    src = src.rearrange("(f c) -> f c", c=P)
                eng.dma_start(par_rows[r0:r0 + n, :], src)\
                    .then_inc(sem("load_par"), ac.landed("load_par", "par"))
            eng.dma_start(sst[0:NB, :], a["state_shift"][0])\
                .then_inc(sem("load_ss"), ac.landed("load_ss", "ss"))
            eng.wait_ge(*at("eps"))
            squares("mix", lambda k: "xT")
            ac.stage("proj")
            def kv_rows(c):
                for t in range(QT + 1):
                    m = P if t < QT else NB
                    eng.wait_ge(*at(f"kv{c}_{t}"))
                    eng.activation(zkv[0:m, t, c * 256:(c + 1) * 256], bank(f"kv{c}_{t}")[0:m, 0:256], ACT.Copy)\
                        .then_inc(ac.done, ac.tick(("free", f"kv{c}_{t}"), "zkv"))

            def sigmoids(f):
                if f:
                    eng.wait_ge(*at(f"kk_a{f - 1}"))
                for name, i, bias in (("dec", 2, "w0"), ("av", 3, "a0")):
                    for h, (lo, hi) in enumerate(HALFS):
                        eng.wait_ge(*at(f"{name}{f}h{h}"))
                        eng.activation(tmp[i][:, lo:hi], bank(f"{name}{f}h{h}")[:, 0:hi - lo], ACT.Sigmoid, bias=col(bias, f))\
                            .then_inc(ac.done, ac.tick(("free", f"{name}{f}h{h}"), f"sig{f}"))

            def kk_norms(f):
                for h, (lo, hi) in enumerate(HALFS):
                    eng.wait_ge(*at(f"kks{f}h{h}"))
                    eng.activation(tmp[5][:, lo:hi], bank(f"kks{f}h{h}")[:, 0:hi - lo], ACT.Sqrt)\
                        .then_inc(ac.done, ac.tick(("free", f"kks{f}h{h}"), f"kkn{f}"))

            def decays(f):
                eng.wait_ge(*at(f"cl{f}"))
                cl = tmp[6][:, 0:T].rearrange("p (c n) -> p c n", c=QT)
                eng.activation(em[:, f, :], cl[:, :, 63], ACT.Exp)\
                    .then_inc(ac.done, ac.tick())
                eng.activation(ec[:, f, :], cl[:, :, 127], ACT.Exp)\
                    .then_inc(ac.done, ac.tick())
                eng.activation(dv[:, 0, f, :], tmp[2][:, T:NT], ACT.Exp)\
                    .then_inc(ac.done, ac.tick(f"dvw{f}"))
                eng.wait_ge(*at(f"clm{f}"))
                clm = tmp[7][:, 0:T].rearrange("p (c n) -> p c n", c=QT)
                eng.activation(ecr[:, f, :], clm[:, :, 127], ACT.Exp)\
                    .then_inc(ac.done, ac.tick())
                eng.activation(tmp[8][:, 0:T], tmp[8][:, 0:T], ACT.Exp)\
                    .then_inc(ac.done, ac.tick())
                eng.wait_ge(*ac.latest())
                eng.activation(tmp[6][:, 0:T], tmp[7][:, 0:T], ACT.Exp)\
                    .then_inc(ac.done, ac.tick())
                eng.activation(tmp[1][:, 0:T], tmp[7][:, 0:T], ACT.Exp, scale=-1.0)\
                    .then_inc(ac.done, ac.tick(f"E{f}"))

            eng.wait_ge(*at("sh12"))
            eng.activation(XR[0:HD, 12, 1:1 + NT], XR[0:HD, 12, 1:1 + NT], ACT.Tanh)\
                .then_inc(ac.done, ac.tick("lr_w_in"))
            eng.wait_ge(*at("sh13"))
            eng.activation(XR[:, 13, 1:1 + NT], XR[:, 13, 1:1 + NT], ACT.Sigmoid)\
                .then_inc(ac.done, ac.tick("lr_in"))
            for f in range(2):
                sigmoids(f)
                kk_norms(f)
                decays(f)
            sigmoids(2)
            kv_rows(0)
            kk_norms(2)
            decays(2)
            kv_rows(1)
            sigmoids(3)
            kk_norms(3)
            kv_rows(2)
            decays(3)
            eng.wait_ge(*at("gates_p"))
            ps = bank("gates_p")
            eng.activation(gate[:, 0:QT, :], ps[:, 0:QT * GATES].rearrange("p (t n) -> p t n", t=QT), ACT.Sigmoid)\
                .then_inc(ac.done, ac.tick())
            eng.activation(gate[0:NB, QT, :], ps[0:NB, QT * GATES:(QT + 1) * GATES], ACT.Sigmoid)\
                .then_inc(ac.done, ac.tick("gates", ("free", "gates_p")))
            for r in range(R):
                for h, (lo, hi) in enumerate(HALFS):
                    eng.wait_ge(*at(f"q{r}h{h}"))
                    eng.activation(qT[:, r, lo:hi], bank(f"q{r}h{h}")[:, 0:hi - lo], ACT.Copy)\
                        .then_inc(ac.done, ac.tick(("free", f"q{r}h{h}"), f"q_s{r}"))
            ac.stage("att")

            def q_squares(r):
                eng.wait_ge(*at(f"q_s{r}"))
                if r >= 2:
                    eng.wait_ge(*at(f"qms{r - 2}h1"))
                eng.activation(sq[:, r % 2, :], qT[:, r, :], ACT.Square)\
                    .then_inc(ac.done, ac.tick(f"qsq{r}"))

            def q_roots(r):
                for h, (lo, hi) in enumerate(HALFS):
                    eng.wait_ge(*at(f"qms{r}h{h}"))
                    if r:
                        eng.wait_ge(*at(f"q_n{r - 1}"))
                    eng.activation(rstd[:, lo:hi], bank(f"qms{r}h{h}")[:, 0:hi - lo], ACT.Sqrt, scale=1.0 / HD, bias=eps[:, 0:1])\
                        .then_inc(ac.done, ac.tick(f"qrt{r}", ("free", f"qms{r}h{h}")))

            q_squares(0)
            q_squares(1)
            eng.wait_ge(*at("kss"))
            eng.activation(krs, krs, ACT.Sqrt, scale=1.0 / HD, bias=eps[:, 0:1])\
                .then_inc(ac.done, ac.tick())
            eng.activation(drs, drs, ACT.Sqrt, scale=1.0 / HD, bias=eps[0:NB, 0:1])\
                .then_inc(ac.done, ac.tick("krt"))
            eng.wait_ge(*at("dv_stored"))
            for v in range(2):
                for g in range(G):
                    for s0 in (0, 4, 8):
                        n = min(4, 10 - s0) * P
                        eng.wait_ge(*at(f"pair{v}{g}{s0}"))
                        col0 = g * PAIR_SEQ + s0 * P
                        eng.activation(xcmp[:, v, col0:col0 + n], bank(f"pair{v}{g}{s0}")[:, 0:n], ACT.Copy)\
                            .then_inc(ac.done, ac.tick(("free", f"pair{v}{g}{s0}")))
            eng.wait_ge(*at("pe_t"))
            eng.activation(xcmp[:, :, G * PAIR_SEQ:XCMP], bank("pe_t")[:, 0:32].rearrange("p (v n) -> p v n", v=2), ACT.Copy)\
                .then_inc(ac.done, ac.tick(("free", "pe_t"), "xcmp"))
            for r in range(2):
                q_roots(r)
                q_squares(r + 2)
            for v in range(2):
                eng.wait_ge(*at(f"kT{v}"))
                eng.activation(kT[:, v, :], bank(f"kT{v}"), ACT.Copy, scale=col("k_norm", 1 + v))\
                    .then_inc(ac.done, ac.tick(("free", f"kT{v}"), "kTs"))
            q_roots(2)
            q_roots(3)
            for v in range(2):
                eng.wait_ge(*at(f"css{v}"))
                eng.activation(crs, crs, ACT.Sqrt, scale=1.0 / HD, bias=eps[:, 0:1])\
                    .then_inc(ac.done, ac.tick(f"crt{v}"))
                for m in range(2):
                    eng.wait_ge(*at(f"cb{v}{m}"))
                    if v:
                        eng.wait_ge(*at("cmp0"))
                    eng.activation(gel[:, m, :], bank(f"conv{v}{m}")[:, 0:320], ACT.Gelu_apprx_tanh, bias=stc[:, 2 * v + m:2 * v + m + 1])\
                        .then_inc(ac.done, ac.tick(f"gel{v}", ("free", f"conv{v}{m}")))
            for v in range(2):
                if v == 0:
                    eng.wait_ge(*at("pairs_turned"))
                for i0 in range(0, NPG, 4):
                    eng.wait_ge(*at(f"ck{v}_{i0}"))
                    eng.activation(kTd[:, v, i0 // 2:i0 // 2 + 2, 0:PAST], bank(f"ck{v}_{i0}").rearrange("p (b n) -> p b n", b=2), ACT.Copy, scale=col("k_norm", 1 + v))\
                        .then_inc(ac.done, ac.tick(("free", f"ck{v}_{i0}")))
                eng.wait_ge(*at(f"dk{v}"))
                eng.activation(kTd[:, v, :, PAST], bank(f"dk{v}")[:, 0:NB], ACT.Copy, scale=col("k_norm", 1 + v))\
                    .then_inc(ac.done, ac.tick(("free", f"dk{v}"), f"kTd{v}"))
            eng.wait_ge(*at("kcms"))
            eng.activation(kcn, bank("kcms")[:, 0:160], ACT.Sqrt, scale=1.0 / HD, bias=eps[:, 0:1])\
                .then_inc(ac.done, ac.tick("kcrt", ("free", "kcms")))
            for v in range(2):
                eng.wait_ge(*at(f"sdm{v}"))
                eng.activation(pbuf[0:64, v, 0:257], bank(f"sd{v}")[0:64, 0:257], ACT.Exp, bias=st[0:64, v:v + 1], accum_out=st[0:64, 4 + v:5 + v])\
                    .then_inc(ac.done, ac.tick(f"sde{v}", ("free", f"sd{v}")))
            eng.wait_ge(*at("sdm2"))
            eng.activation(pcs, pcs, ACT.Exp, bias=st[0:64, 2:3], accum_out=st[0:64, 6:7])\
                .then_inc(ac.done, ac.tick("sde2"))
            eng.wait_ge(*at("ptc"))
            eng.activation(ptb[:, 0, 448:512], bank("ptc")[:, 0:64], ACT.Copy)\
                .then_inc(ac.done, ac.tick(("free", "ptc"), "ptcs"))
            for v in range(2):
                eng.wait_ge(*at(f"ptd{v}"))
                eng.activation(ptb[:, v, 0:128], bank(f"ptd{v}")[:, 0:128], ACT.Copy)\
                    .then_inc(ac.done, ac.tick())
                eng.activation(ptb[0:NB, v, 128:192], bank(f"ptd{v}")[0:NB, 128:192], ACT.Copy)\
                    .then_inc(ac.done, ac.tick(("free", f"ptd{v}"), f"ptds{v}"))
            PER, AHEAD = 16, 3
            UNITS = QT * PER

            def exp_unit(i):
                n = (i // PER + 1) * P
                eng.wait_ge(*at(f"sm{i}"))
                eng.wait_ge(*at("od" if i < 4 else f"pt{i - 4}"))
                eng.activation(pbuf[:, i % 4, 0:n], bank(f"s{i}")[:, 0:n], ACT.Exp, bias=st[:, i % 4:i % 4 + 1], accum_out=st[:, 8 + i % 4:9 + i % 4])\
                    .then_inc(ac.done, ac.tick(f"se{i}", ("free", f"s{i}")))

            def evac_unit(i):
                n = (i // PER + 1) * P
                eng.wait_ge(*at(f"pt{i}"))
                eng.wait_ge(*at("od" if i < 2 else f"pv{i - 2}"))
                eng.activation(ptb[:, i % 2, 0:n], bank(f"pt{i}")[:, 0:n], ACT.Copy)\
                    .then_inc(ac.done, ac.tick(f"pts{i}", ("free", f"pt{i}")))

            def block_exp(qt):
                eng.wait_ge(*at(f"scm{qt}"))
                eng.activation(pcm, pcm, ACT.Exp)\
                    .then_inc(ac.done, ac.tick(f"sce{qt}"))

            def block_evac(qt):
                for h2 in range(2):
                    eng.wait_ge(*at(f"ptc{qt}_{h2}"))
                    eng.wait_ge(*at("od" if qt < 2 else f"o{qt - 2}"))
                    eng.activation(ptcb[0:NCP, qt % 2, h2 * 4:h2 * 4 + 4, :], bank(f"ptc{qt}_{h2}")[0:NCP, :].rearrange("p (h n) -> p h n", h=4), ACT.Copy)\
                        .then_inc(ac.done, ac.tick(("free", f"ptc{qt}_{h2}"), f"ptcs{qt}_{h2}"))

            block_exp(0)
            for i in range(AHEAD):
                exp_unit(i)
            block_evac(0)
            for i in range(UNITS):
                qt, u = divmod(i, PER)
                if qt + 1 < QT and u == 9:
                    block_exp(qt + 1)
                if qt + 1 < QT and u == 12:
                    block_evac(qt + 1)
                if i + AHEAD < UNITS:
                    exp_unit(i + AHEAD)
                evac_unit(i)
            ac.end("att")

            ac.stage("rwkv")
            eng.wait_ge(*at("end:att:pe"))
            eng.wait_ge(*at("end:att:dve"))
            eng.wait_ge(*at("stored_att"))

            def rows_of_tokens(w, c):
                eng.wait_ge(*at(f"tm{w}{c}"))
                eng.activation(tm[:, w, c, :], bank(f"tm{w}{c}"), ACT.Copy)\
                    .then_inc(ac.done, ac.tick(("free", f"tm{w}{c}"), f"tms{w}{c}"))

            for c in range(QT):
                rows_of_tokens(3, c)
            for w in range(3):
                rows_of_tokens(w, 0)
            for c in range(QT):
                for n in LEVELS:
                    if n in (8, 16, 32) and c + 1 < QT:
                        rows_of_tokens((8, 16, 32).index(n), c + 1)
                    for hg in range(2):
                        if n < 64:
                            eng.wait_ge(*at(f"T{c}{hg}_{n}"))
                            eng.activation(Tsb[:, hg, :], bank(f"T{c}{hg}"), ACT.Copy)\
                                .then_inc(ac.done, ac.tick(f"Ts{c}{hg}_{n}", *([("free", f"T{c}{hg}")] if n == 32 else [])))
                        eng.wait_ge(*at(f"TT{c}{hg}_{n}"))
                        eng.activation(TTsb[:, hg, :], bank(f"TT{c}{hg}"), ACT.Copy)\
                            .then_inc(ac.done, ac.tick(f"TTs{c}{hg}_{n}", *([("free", f"TT{c}{hg}")] if n == 64 else [])))
                eng.wait_ge(*at(f"ap{c}"))
                eng.activation(ApT.rearrange("p f n -> p (f n)"), bank(f"ap{c}"), ACT.Copy)\
                    .then_inc(ac.done, ac.tick(f"aps{c}", ("free", f"ap{c}")))
                eng.wait_ge(*at(f"u{c}"))
                eng.activation(U, bank(f"u{c}"), ACT.Copy)\
                    .then_inc(ac.done, ac.tick(f"us{c}", ("free", f"u{c}")))
                eng.wait_ge(*at(f"y{c}p"))
                eng.activation(oT[:, 4:8, c * P:(c + 1) * P], bank(f"y{c}p").rearrange("p (f n) -> p f n", f=4), ACT.Copy)\
                    .then_inc(ac.done, ac.tick(("free", f"y{c}p")))
            eng.wait_ge(*at("yd"))
            eng.activation(oT[:, 4:8, T:NT], bank("yd")[:, 0:4 * NB].rearrange("p (f b) -> p f b", f=4), ACT.Copy)\
                .then_inc(ac.done, ac.tick(("free", "yd"), "yall"))
            for f in range(4):
                if f:
                    eng.wait_ge(*at(f"gn{f - 1}"))
                for h, (lo, hi) in enumerate(HALFS):
                    eng.wait_ge(*at(f"gv{f}h{h}"))
                    eng.activation(rstd[:, lo:hi], bank(f"gv{f}h{h}")[:, 0:hi - lo], ACT.Sqrt, scale=1.0 / HD, bias=eps[:, 1:2])\
                        .then_inc(ac.done, ac.tick(f"grt{f}", ("free", f"gv{f}h{h}")))
            ac.end("rwkv")

            def hi_of_chunk(c):
                f, high, _ = split_parts(c)
                eng.wait_ge(*at(("got", c)))
                if split_before(c):
                    eng.wait_ge(*at(("used", split_before(c))))
                eng.activation(high, f, ACT.Copy)\
                    .then_inc(ac.done, ac.tick(("hi", c)))

            def hi_of_input(which, ready):
                for k in range(KD):
                    eng.wait_ge(*at(ready(k)))
                    eng.activation(x_hi[:, k, :], hT[:, k, :], ACT.Copy)\
                        .then_inc(ac.done, ac.tick(f"{which}hi{k}"))

            ac.stage("ffn")
            eng.wait_ge(*at("end:rwkv:dve"))
            eng.wait_ge(*at("end:rwkv:pe"))
            eng.wait_ge(*at("end:rwkv:pool"))
            eng.wait_ge(*at("stored_rwkv"))
            hi_of_chunk(("wo", 0))
            hi_of_input("o", lambda k: "end:rwkv:dve")
            for c in (1, 2, 3):
                hi_of_chunk(("wo", c))
            squares("ffn", lambda k: f"x1_{k}")
            ac.stage("ffn")
            hi_of_chunk(("wg", 0))
            hi_of_input("ffn", lambda k: f"ffnh{k}")
            hi_of_chunk(("wu", 0))
            for c in range(11):
                for m in (2 * c, 2 * c + 1):
                    if m >= 2:
                        eng.wait_ge(*at(f"act_f{m - 2}"))
                    for h, (lo, hi) in enumerate(HALFS):
                        eng.wait_ge(*at(f"wg{m}h{h}"))
                        eng.activation(silu[:, m % 2, lo:hi], bank(f"wg{m}h{h}")[:, 0:hi - lo], ACT.Silu)\
                            .then_inc(ac.done, ac.tick(f"silu{m}h{h}", ("free", f"wg{m}h{h}")))
                hi_of_chunk(("wg", c + 1) if c < 10 else ("wd", 0, 0))
                for m in (2 * c, 2 * c + 1):
                    eng.wait_ge(*at(f"act_f{m}"))
                    eng.activation(act_hi[:, m, :], act_f[:, m % 2, :], ACT.Copy)\
                        .then_inc(ac.done, ac.tick(f"act_hi{m}"))
                hi_of_chunk(("wu", c + 1) if c < 10 else ("wd", 0, 1))
            for i in range(2, 12):
                hi_of_chunk(("wd", i // 3, i % 3))
            for k in range(2):
                eng.wait_ge(*at(f"pe{k}"))
                eng.activation(pT[:, k, 0:T], bank(f"pe{k}"), ACT.Copy)\
                    .then_inc(ac.done, ac.tick(("free", f"pe{k}")))
            eng.wait_ge(*at("pd"))
            eng.activation(pT[:, :, T:NT], bank("pd")[:, 0:2 * NB].rearrange("p (k b) -> p k b", k=2), ACT.Copy)\
                .then_inc(ac.done, ac.tick(("free", "pd"), "pTs"))
            squares("ple", lambda k: f"x2_{k}")
            ac.stage("ffn")
            hi_of_chunk(("wpg", 0))
            hi_of_input("ple", lambda k: f"pleh{k}")
            for m in range(KD):
                for h, (lo, hi) in enumerate(HALFS):
                    eng.wait_ge(*at(f"wp{m}h{h}"))
                    eng.activation(pep[:, m, lo:hi], bank(f"wp{m}h{h}")[:, 0:hi - lo], ACT.Copy)\
                        .then_inc(ac.done, ac.tick(f"pep{m}", ("free", f"wp{m}h{h}")))
            hi_of_chunk(("wpg", 1))
            for m in range(KD):
                if m >= 2:
                    eng.wait_ge(*at(f"xfin{m - 2}"))
                for h, (lo, hi) in enumerate(HALFS):
                    eng.wait_ge(*at(f"wpg{m}h{h}"))
                    eng.activation(silu[:, m % 2, lo:hi], bank(f"wpg{m}h{h}")[:, 0:hi - lo], ACT.Sigmoid)\
                        .then_inc(ac.done, ac.tick(f"sg{m}h{h}", ("free", f"wpg{m}h{h}")))
                if m in (1, 3):
                    hi_of_chunk(("wpg", m // 2 + 2))
            for t in range(QT + 1):
                m = P if t < QT else NB
                eng.wait_ge(*at(f"out{t}1"))
                eng.activation(ot[0:m, t, T:2 * T], bank(f"out{t}1")[0:m, :], ACT.Copy)\
                    .then_inc(ac.done, ac.tick(("free", f"out{t}1"), f"ya{t}"))

        @block.vector
        def _(eng):
            v_ = steps["dve"]
            tt, ts, stt, cp = eng.tensor_tensor, eng.tensor_scalar, eng.scalar_tensor_tensor, eng.tensor_copy

            def normalise(which, gain):
                v_.stage("norm")
                for h, (lo, hi) in enumerate(HALFS):
                    eng.wait_ge(*at(f"{which}rt{h}"))
                    eng.reciprocal(rstd[:, lo:hi], rstd[:, lo:hi])\
                        .then_inc(v_.done, v_.tick())
                eng.wait_ge(*v_.latest())
                for k in range(KD):
                    stt(out=hT[:, k, :], in0=xT[:, k, :], scalar=col(gain, k), in1=rstd[:, :], op0=ALU.mult, op1=ALU.mult)\
                        .then_inc(v_.done, v_.tick(f"{which}h", f"{which}h{k}"))

            v_.stage("load")
            for k in range(KD):
                eng.wait_ge(*at(f"x{k}"))
                cp(xT[:, k, 0:T], bank(f"x{k}"))\
                    .then_inc(v_.done, v_.tick(("free", f"x{k}")))
            eng.wait_ge(*at("xd"))
            cp(xT[:, :, T:NT], bank("xd")[:, 0:KD * NB].rearrange("p (k b) -> p k b", k=KD))\
                .then_inc(v_.done, v_.tick(("free", "xd"), "xT"))
            eng.wait_ge(*at("par_t"))
            cp(par[:, :], bank("par_t")[:, 0:NROWS])\
                .then_inc(v_.done, v_.tick(("free", "par_t")))
            eng.wait_ge(*at("ss_t"))
            cp(ssf[:, :, :], bank("ss_t")[:, 0:XF * NB].rearrange("p (f b) -> p f b", f=XF))\
                .then_inc(v_.done, v_.tick(("free", "ss_t")))
            eng.wait_ge(*v_.latest())
            ts(qgain[:, :], col("q_norm"), HD ** -0.5, None, ALU.mult)\
                .then_inc(v_.done, v_.tick())
            c0 = ROWS["k_a"][0]
            ts(ka1[:, :], par[:, c0:c0 + 4], -1.0, 1.0, ALU.mult, ALU.add)\
                .then_inc(v_.done, v_.tick())
            eng.wait_ge(*v_.latest())
            normalise("mix", "norm_mix")
            v_.stage("proj")
            def keys_normal(f):
                k_ = XR[:, 4 + f, 1:1 + NT]
                eng.wait_ge(*at(f"sh{4 + f}"))
                eng.wait_ge(*v_.latest())
                ts(tmp[4], k_, col("k_k", f), None, ALU.mult)\
                    .then_inc(v_.done, v_.tick())
                eng.wait_ge(*v_.latest())
                tt(sq[:, 0, :], tmp[4], tmp[4], ALU.mult)\
                    .then_inc(v_.done, v_.tick(f"kks_in{f}"))

            def log_decays(f):
                r_, k_ = XR[:, f, 1:1 + NT], XR[:, 4 + f, 1:1 + NT]
                eng.wait_ge(*at(f"sh{f}"))
                eng.wait_ge(*v_.latest())
                eng.wait_ge(*at(f"sig{f}"))
                ts(tmp[2], tmp[2], -0.6065306597126334, None, ALU.mult)\
                    .then_inc(v_.done, v_.tick())
                ts(tmp[0], tmp[3], col("k_a", f), ka1[:, f:f + 1], ALU.mult, ALU.add)\
                    .then_inc(v_.done, v_.tick())
                eng.wait_ge(*v_.latest())
                for c in range(QT):
                    s_ = slice(c * P, (c + 1) * P)
                    eng.tensor_tensor_scan(tmp[6][:, s_], ones[:, :], tmp[2][:, s_], 0.0, ALU.mult, ALU.add)\
                        .then_inc(v_.done, v_.tick(f"cl{f}"))
                tt(k_, k_, tmp[0], ALU.mult)\
                    .then_inc(v_.done, v_.tick())
                eng.wait_ge(*v_.latest())
                cl = tmp[6][:, 0:T].rearrange("p (c n) -> p c n", c=QT)
                clm = tmp[7][:, 0:T].rearrange("p (c n) -> p c n", c=QT)
                tt(clm, cl, cl[:, :, 63:64].to_broadcast([P, QT, P]), ALU.subtract)\
                    .then_inc(v_.done, v_.tick())
                stt(out=sq[:, 1, :], in0=r_, scalar=col("r_k", f), in1=k_, op0=ALU.mult, op1=ALU.mult)\
                    .then_inc(v_.done, v_.tick(f"bs_in{f}"))
                eng.wait_ge(*v_.latest())
                tt(tmp[8][:, 0:T], tmp[7][:, 0:T], tmp[2][:, 0:T], ALU.subtract)\
                    .then_inc(v_.done, v_.tick(f"clm{f}"))

            def kk_and_a(f):
                eng.wait_ge(*at(f"kkn{f}"))
                ts(tmp[5], tmp[5], 1e-12, None, ALU.max)\
                    .then_inc(v_.done, v_.tick())
                eng.wait_ge(*v_.latest())
                eng.reciprocal(tmp[5], tmp[5])\
                    .then_inc(v_.done, v_.tick())
                eng.wait_ge(*v_.latest())
                tt(tmp[4], tmp[4], tmp[5], ALU.mult)\
                    .then_inc(v_.done, v_.tick())
                eng.wait_ge(*v_.latest())
                tt(tmp[5], tmp[4], tmp[3], ALU.mult)\
                    .then_inc(v_.done, v_.tick(f"kk_a{f}"))

            def factors_made(f):
                r_, k_, vv = XR[:, f, 1:1 + NT], XR[:, 4 + f, 1:1 + NT], XR[:, 8 + f, 1:1 + NT]
                cl = tmp[6][:, 0:T].rearrange("p (c n) -> p c n", c=QT)
                eng.wait_ge(*at(f"sh{8 + f}"))
                if f >= 2:
                    eng.wait_ge(*at(f"stored_f{f - 2}"))
                eng.wait_ge(*at(f"E{f}"))
                eng.wait_ge(*v_.latest())
                stt(out=ARs[:, f % 2, :, 0:P], in0=tmp[4][:, 0:T].rearrange("p (c n) -> p c n", c=QT), scalar=-1.0, in1=tmp[8][:, 0:T].rearrange("p (c n) -> p c n", c=QT), op0=ALU.mult, op1=ALU.mult)\
                    .then_inc(v_.done, v_.tick())
                tt(ARs[:, f % 2, :, P:2 * P], r_[:, 0:T].rearrange("p (c n) -> p c n", c=QT), cl, ALU.mult)\
                    .then_inc(v_.done, v_.tick())
                tt(BHs[:, f % 2, :], tmp[5][:, 0:T], tmp[1][:, 0:T], ALU.mult)\
                    .then_inc(v_.done, v_.tick())
                tt(KHs[:, f % 2, :], k_[:, 0:T], tmp[1][:, 0:T], ALU.mult)\
                    .then_inc(v_.done, v_.tick(f"tmf{f}"))
                ts(dv[:, 1, f, :], tmp[4][:, T:NT], -1.0, None, ALU.mult)\
                    .then_inc(v_.done, v_.tick())
                cp(dv[:, 2, f, :], tmp[5][:, T:NT])\
                    .then_inc(v_.done, v_.tick())
                cp(dv[:, 3, f, :], k_[:, T:NT])\
                    .then_inc(v_.done, v_.tick())
                cp(dv[:, 4, f, :], r_[:, T:NT])\
                    .then_inc(v_.done, v_.tick())
                cp(dv[:, 5, f, :], vv[:, T:NT])\
                    .then_inc(v_.done, v_.tick(f"prep{f}"))

            def bonus(f):
                eng.wait_ge(*v_.latest())
                for h, (lo, hi) in enumerate(HALFS):
                    eng.wait_ge(*at(f"bs{f}h{h}"))
                    tt(XR[:, 4 + f, 1 + lo:1 + hi], bank(f"bs{f}h{h}")[:, 0:hi - lo], XR[:, 8 + f, 1 + lo:1 + hi], ALU.mult)\
                        .then_inc(v_.done, v_.tick(("free", f"bs{f}h{h}"), f"bonus{f}"))

            def xr_tiles(c):
                for f in XR_PAIRS[c]:
                    for h, (lo, hi) in enumerate(HALFS):
                        eng.wait_ge(*at(f"xr{f}h{h}"))
                        cp(XR[:, f, 1 + lo:1 + hi], bank(f"xr{f}h{h}")[:, 0:hi - lo])\
                            .then_inc(v_.done, v_.tick(("free", f"xr{f}h{h}"), f"xr_s{f}"))

            xr_tiles(0)
            xr_tiles(1)
            xr_tiles(2)
            keys_normal(0)
            xr_tiles(3)
            log_decays(0)
            kk_and_a(0)
            xr_tiles(4)
            factors_made(0)
            bonus(0)
            keys_normal(1)
            xr_tiles(5)
            log_decays(1)
            kk_and_a(1)
            xr_tiles(6)
            factors_made(1)
            bonus(1)
            for f in (2, 3):
                keys_normal(f)
                log_decays(f)
                kk_and_a(f)
                factors_made(f)
                bonus(f)
            eng.wait_ge(*v_.latest())
            for w in range(6):
                eng.wait_ge(*at(f"dv{w}"))
                cp(dvt[:, w, :], bank(f"dv{w}")[0:NB, :])\
                    .then_inc(v_.done, v_.tick(("free", f"dv{w}"), "dvt"))
            v_.stage("att")
            eng.wait_ge(*at("masks"))
            for i in range(4):
                n = min(4, XF - 4 * i) * P
                eng.wait_ge(*at(f"xrl{i}"))
                cp(sst[:, i * 512:i * 512 + n], bank(f"xrl{i}")[0:9, 0:n])\
                    .then_inc(v_.done, v_.tick(("free", f"xrl{i}"), "shift_rows"))
            eng.wait_ge(*at("zkv"))
            eng.wait_ge(*at("sh11"))
            for v in range(2):
                k_ = zkv[:, 0:QT, 256 + 256 * v:384 + 256 * v]
                tt(kn[:, v, :, :], k_, k_, ALU.mult)\
                    .then_inc(v_.done, v_.tick())
                k_ = zkv[0:NB, QT, 256 + 256 * v:384 + 256 * v]
                tt(dkn[:, v * P:(v + 1) * P], k_, k_, ALU.mult)\
                    .then_inc(v_.done, v_.tick())
            eng.wait_ge(*v_.latest())
            eng.tensor_reduce(krs.rearrange("p v t g -> p (v t g)"), kn.rearrange("p v t (g d) -> p (v t g) d", d=HD), AX.X, ALU.add)\
                .then_inc(v_.done, v_.tick())
            eng.tensor_reduce(drs, dkn.rearrange("p (j d) -> p j d", d=HD), AX.X, ALU.add)\
                .then_inc(v_.done, v_.tick("kss"))
            eng.wait_ge(*at("krt"))
            eng.reciprocal(krs, krs)\
                .then_inc(v_.done, v_.tick())
            eng.reciprocal(drs, drs)\
                .then_inc(v_.done, v_.tick())
            eng.wait_ge(*v_.latest())
            for v in range(2):
                tt(kn[:, v, :, :].rearrange("p t (g d) -> p t g d", d=HD), zkv[:, 0:QT, 256 + 256 * v:384 + 256 * v].rearrange("p t (g d) -> p t g d", d=HD), krs[:, v, :, :].unsqueeze(3).to_broadcast([P, QT, G, HD]), ALU.mult)\
                    .then_inc(v_.done, v_.tick(f"kn{v}"))
                tt(dkn[:, v * P:(v + 1) * P].rearrange("p (g d) -> p g d", d=HD), zkv[0:NB, QT, 256 + 256 * v:384 + 256 * v].rearrange("p (g d) -> p g d", d=HD), drs[:, 2 * v:2 * v + 2].unsqueeze(2).to_broadcast([NB, G, HD]), ALU.mult)\
                    .then_inc(v_.done, v_.tick(f"dkn{v}"))
            for r in range(R):
                eng.wait_ge(*at(f"qrt{r}"))
                eng.reciprocal(rstd[:, :], rstd[:, :])\
                    .then_inc(v_.done, v_.tick())
                eng.wait_ge(*v_.latest())
                stt(out=qT[:, r, :], in0=qT[:, r, :], scalar=qgain[:, 0:1], in1=rstd[:, :], op0=ALU.mult, op1=ALU.mult)\
                    .then_inc(v_.done, v_.tick(f"q_n{r}", "qTs"))
            eng.memset(qall, 0.0)\
                .then_inc(v_.done, v_.tick())
            eng.memset(qb, 0.0)\
                .then_inc(v_.done, v_.tick())
            eng.wait_ge(*v_.latest())
            for g in range(G):
                lo, hi = g * HD, (g + 1) * HD
                cp(qall[lo:hi, :].rearrange("p (b h) -> p b h", h=NH)[:, :, g * R:(g + 1) * R], qT[lo:hi, :, T:NT].rearrange("p r b -> p b r"))\
                    .then_inc(v_.done, v_.tick())
            eng.wait_ge(*v_.latest())
            for b in range(NB):
                cp(qb[:, b, b * NH:(b + 1) * NH], qall[:, b * NH:(b + 1) * NH])\
                    .then_inc(v_.done, v_.tick("qb"))
            for v in range(2):
                eng.wait_ge(*at(f"cache{v}"))
                if v:
                    eng.wait_ge(*at(f"crt{v - 1}"))
                tt(csq, cache[:, v, :, 0:P], cache[:, v, :, 0:P], ALU.mult)\
                    .then_inc(v_.done, v_.tick())
                eng.wait_ge(*v_.latest())
                eng.tensor_reduce(crs, csq.rearrange("p t (g d) -> p (t g) d", d=HD).rearrange("p (t g) d -> p t g d", g=G), AX.X, ALU.add)\
                    .then_inc(v_.done, v_.tick(f"css{v}"))
                eng.wait_ge(*at(f"crt{v}"))
                eng.reciprocal(crs, crs)\
                    .then_inc(v_.done, v_.tick())
                eng.wait_ge(*v_.latest())
                k_ = cache[:, v, :, 0:P].rearrange("p t (g d) -> p t g d", d=HD)
                tt(k_, k_, crs.unsqueeze(3).to_broadcast([P, NPG, G, HD]), ALU.mult)\
                    .then_inc(v_.done, v_.tick(f"ckn{v}"))
                eng.wait_ge(*v_.latest())
                for m in range(2):
                    eng.wait_ge(*at(f"conv{v}{m}"))
                    tt(stc[:, 2 * v + m:2 * v + m + 1], bank(f"conv{v}{m}")[:, 320:321], col("cmp_b1", 2 * v + m), ALU.add)\
                        .then_inc(v_.done, v_.tick(f"cb{v}{m}"))
            for v in range(2):
                eng.wait_ge(*at(f"cmp{v}"))
                ts([kc, vc][v], bank(f"cmp{v}")[:, 0:160], col("cmp_b2", v), None, ALU.add)\
                    .then_inc(v_.done, v_.tick(("free", f"cmp{v}"), *(["vc"] if v else [])))
            eng.wait_ge(*v_.latest())
            eng.wait_ge(*at("qms2h1"))
            eng.wait_ge(*at("qms3h1"))
            tt(sq[:, 0, 0:160], kc, kc, ALU.mult)\
                .then_inc(v_.done, v_.tick("kcsq"))
            eng.wait_ge(*at("kcrt"))
            eng.reciprocal(kcn, kcn)\
                .then_inc(v_.done, v_.tick())
            eng.wait_ge(*v_.latest())
            stt(out=kcn, in0=kc, scalar=col("k_norm", 0), in1=kcn, op0=ALU.mult, op1=ALU.mult)\
                .then_inc(v_.done, v_.tick("kcn"))
            eng.wait_ge(*at("vc_t"))
            cp(vcd, bank("vc_t")[:, 0:P])\
                .then_inc(v_.done, v_.tick())
            cp(vcp[0:NCP, :], bank("vc_t")[0:NCP, P:2 * P])\
                .then_inc(v_.done, v_.tick("vcd", ("free", "vc_t")))
            for v in range(2):
                eng.wait_ge(*at(f"sd{v}"))
                eng.tensor_reduce(st[0:64, v:v + 1], bank(f"sd{v}")[0:64, 0:257], AX.X, ALU.max, negate=True)\
                    .then_inc(v_.done, v_.tick(f"sdm{v}"))
            eng.wait_ge(*at("sdc"))
            tt(pcs, bank("sdc")[0:64, 0:P], dec_add[:, :, :].rearrange("p b n -> p (b n)"), ALU.add)\
                .then_inc(v_.done, v_.tick(("free", "sdc")))
            eng.wait_ge(*v_.latest())
            eng.tensor_reduce(st[0:64, 2:3], pcs, AX.X, ALU.max, negate=True)\
                .then_inc(v_.done, v_.tick("sdm2"))
            eng.wait_ge(*at("sde0"))
            eng.wait_ge(*at("sde1"))
            eng.wait_ge(*at("sde2"))
            eng.wait_ge(*at("gd"))
            eng.reciprocal(st[0:64, 8:11], st[0:64, 4:7])\
                .then_inc(v_.done, v_.tick())
            eng.wait_ge(*v_.latest())
            for i, br in enumerate((1, 2, 0)):
                tt(st[0:64, 12 + i:13 + i], st[0:64, 8 + i:9 + i], scol[0:64, br:br + 1], ALU.mult)\
                    .then_inc(v_.done, v_.tick())
            eng.wait_ge(*v_.latest())
            ts(diag[0:64, 2, 0:64], ident[0:64, 0:64], st[0:64, 14:15], None, ALU.mult)\
                .then_inc(v_.done, v_.tick("pdc"))
            for v in range(2):
                ts(diag[0:64, v, 0:64], ident[0:64, 0:64], st[0:64, 12 + v:13 + v], None, ALU.mult)\
                    .then_inc(v_.done, v_.tick())
                ts(st[0:64, 64 + v * NB:64 + (v + 1) * NB], dec_own[:, :], pbuf[0:64, v, 256:257], None, ALU.mult)\
                    .then_inc(v_.done, v_.tick(f"pd{v}"))
            eng.wait_ge(*at("od"))
            for g in range(G):
                lo, hi = g * HD, (g + 1) * HD
                cp(oT[lo:hi, 0:R, T:NT], bank("od")[lo:hi, 0:64].rearrange("p (b g r) -> p g r b", g=G, r=R)[:, g])\
                    .then_inc(v_.done, v_.tick(("free", "od")))
            eng.wait_ge(*v_.latest())

            PER, AHEAD = 16, 3
            UNITS = QT * PER

            def max_unit(i):
                qt = i // PER
                eng.wait_ge(*at(f"s{i}"))
                if i >= 4:
                    eng.wait_ge(*at(f"se{i - 4}"))
                ps = bank(f"s{i}")
                tt(ps[:, qt * P:(qt + 1) * P], ps[:, qt * P:(qt + 1) * P], causal[:, :], ALU.add)\
                    .then_inc(v_.done, v_.tick())
                eng.wait_ge(*v_.latest())
                eng.tensor_reduce(st[:, i % 4:i % 4 + 1], ps[:, 0:(qt + 1) * P], AX.X, ALU.max, negate=True)\
                    .then_inc(v_.done, v_.tick(f"sm{i}"))

            def scale_unit(i):
                qt, u = divmod(i, PER)
                r, g, v = u // 4, u // 2 % 2, u % 2
                h = g * R + r
                eng.wait_ge(*at(f"se{i}"))
                eng.reciprocal(st[:, 16 + i % 4:17 + i % 4], st[:, 8 + i % 4:9 + i % 4])\
                    .then_inc(v_.done, v_.tick())
                if i >= 4:
                    eng.wait_ge(*at(f"pt{i - 4}"))
                eng.wait_ge(*v_.latest())
                ts(diag[:, i % 4, :], ident[:, :], st[:, 16 + i % 4:17 + i % 4], gate[:, qt, 3 * h + 1 + v:3 * h + 2 + v], ALU.mult, ALU.mult)\
                    .then_inc(v_.done, v_.tick(f"p{i}"))

            def block_max(qt):
                eng.wait_ge(*at(f"sc{qt}"))
                if qt:
                    eng.wait_ge(*at(f"ptc{qt - 1}_1"))
                tt(pcm, bank(f"sc{qt}")[:, 0:NH * NCP].rearrange("p (h n) -> p h n", h=NH), cmp_add[:, qt, :].unsqueeze(1).to_broadcast([P, NH, NCP]), ALU.add)\
                    .then_inc(v_.done, v_.tick(("free", f"sc{qt}")))
                eng.wait_ge(*v_.latest())
                eng.tensor_reduce(stc[:, 8:16], pcm, AX.X, ALU.max)\
                    .then_inc(v_.done, v_.tick())
                eng.wait_ge(*v_.latest())
                tt(pcm, pcm, stc[:, 8:16].unsqueeze(2).to_broadcast([P, NH, NCP]), ALU.subtract)\
                    .then_inc(v_.done, v_.tick(f"scm{qt}"))

            def block_scale(qt):
                eng.wait_ge(*at(f"sce{qt}"))
                tt(pcm, pcm, cmp_keep[:, qt, :].unsqueeze(1).to_broadcast([P, NH, NCP]), ALU.mult)\
                    .then_inc(v_.done, v_.tick())
                eng.wait_ge(*v_.latest())
                eng.tensor_reduce(stc[:, 16:24], pcm, AX.X, ALU.add)\
                    .then_inc(v_.done, v_.tick())
                eng.wait_ge(*v_.latest())
                ts(stc[:, 16:24], stc[:, 16:24], 1e-30, None, ALU.max)\
                    .then_inc(v_.done, v_.tick())
                eng.wait_ge(*v_.latest())
                eng.reciprocal(stc[:, 16:24], stc[:, 16:24])\
                    .then_inc(v_.done, v_.tick())
                eng.wait_ge(*v_.latest())
                tt(stc[:, 16:24], stc[:, 16:24], gate[:, qt, :].rearrange("p (h n) -> p h n", n=3)[:, :, 0], ALU.mult)\
                    .then_inc(v_.done, v_.tick())
                eng.wait_ge(*v_.latest())
                tt(pcm, pcm, stc[:, 16:24].unsqueeze(2).to_broadcast([P, NH, NCP]), ALU.mult)\
                    .then_inc(v_.done, v_.tick(f"pc{qt}"))

            def mixed(qt):
                eng.wait_ge(*at(f"o{qt}"))
                cp(oT[:, 0:R, qt * P:(qt + 1) * P], bank(f"o{qt}").rearrange("p (r n) -> p r n", r=R))\
                    .then_inc(v_.done, v_.tick(("free", f"o{qt}")))

            block_max(0)
            for i in range(AHEAD):
                max_unit(i)
            block_scale(0)
            for i in range(UNITS):
                qt, u = divmod(i, PER)
                if qt + 1 < QT and u == 8:
                    block_max(qt + 1)
                if qt + 1 < QT and u == 10:
                    block_scale(qt + 1)
                scale_unit(i)
                if i + AHEAD < UNITS:
                    max_unit(i + AHEAD)
                if qt and u == 2:
                    mixed(qt - 1)
            mixed(QT - 1)
            v_.end("att")

            v_.stage("rwkv")
            eng.wait_ge(*at("end:att:pe"))
            eng.wait_ge(*at("end:att:act"))
            eng.wait_ge(*at("stored_att"))
            for f in range(4):
                eng.wait_ge(*at("tms33"))
                cp(XR[:, 8 + f, 1:1 + NT], XR[:, 4 + f, 1:1 + NT])\
                    .then_inc(v_.done, v_.tick())
            eng.memset(Hs, 0.0)\
                .then_inc(v_.done, v_.tick())
            eng.memset(Hm, 0.0)\
                .then_inc(v_.done, v_.tick("Hm0"))
            v_.end("prep")
            eng.wait_ge(*v_.latest())
            mask2 = us_ui[:, :, :].rearrange("p s n -> p (s n)").unsqueeze(1).to_broadcast([P, 2, 256])

            def four(m):
                return m.unsqueeze(1).to_broadcast([P, 4, P])

            for c in range(QT):
                if c:
                    eng.wait_ge(*at(f"y{c - 1}p"))
                for hg in range(2):
                    for hp in range(2):
                        h0 = hg * 4 + hp * 2
                        eng.wait_ge(*at(f"ln{c}{hg}{hp}"))
                        tt(LN[:, h0:h0 + 2, :], bank(f"ln{c}{hg}{hp}").rearrange("p (h n) -> p h n", h=2), mask2, ALU.mult)\
                            .then_inc(v_.done, v_.tick(("free", f"ln{c}{hg}{hp}")))
                    for hp in range(2):
                        h0 = hg * 4 + hp * 2
                        eng.wait_ge(*at(f"mq{c}{hg}{hp}"))
                        tt(MQ[:, h0:h0 + 2, :], bank(f"mq{c}{hg}{hp}").rearrange("p (h n) -> p h n", h=2), mask2, ALU.mult)\
                            .then_inc(v_.done, v_.tick(("free", f"mq{c}{hg}{hp}"), f"mqs{c}{hg}"))
                    t4 = Tsb[:, hg, :].rearrange("p (h n) -> p h n", h=4)
                    tt4 = TTsb[:, hg, :].rearrange("p (h n) -> p h n", h=4)
                    eng.wait_ge(*at(f"l{c}{hg}"))
                    tt(t4, bank(f"l{c}{hg}").rearrange("p (h n) -> p h n", h=4), four(level[:, 0, :]), ALU.mult)\
                        .then_inc(v_.done, v_.tick(("free", f"l{c}{hg}")))
                    eng.wait_ge(*v_.latest())
                    tt(tt4, LN[:, hg * 4:hg * 4 + 4, 0:P], four(level1T[:, :]), ALU.mult)\
                        .then_inc(v_.done, v_.tick())
                    eng.wait_ge(*v_.latest())
                    tt(t4, t4, four(ident[:, :]), ALU.add)\
                        .then_inc(v_.done, v_.tick(f"Ts{c}{hg}_1"))
                    tt(tt4, tt4, four(ident[:, :]), ALU.add)\
                        .then_inc(v_.done, v_.tick(f"TTs{c}{hg}_1"))
                for i, n in enumerate(LEVELS):
                    for hg in range(2):
                        eng.wait_ge(*at(f"X{c}{hg}_{n}"))
                        if i:
                            eng.wait_ge(*at(f"TT{c}{hg}_{n // 2}"))
                        tt(Xs[:, hg, :].rearrange("p (h n) -> p h n", h=4), bank(f"X{c}{hg}_{n}").rearrange("p (h n) -> p h n", h=4), four(level[:, 1 + i, :]), ALU.mult)\
                            .then_inc(v_.done, v_.tick(f"Xs{c}{hg}_{n}", ("free", f"X{c}{hg}_{n}")))
                eng.wait_ge(*at(f"mv{c}"))
                cp(MV, bank(f"mv{c}"))\
                    .then_inc(v_.done, v_.tick(f"mvs{c}", ("free", f"mv{c}")))
                eng.wait_ge(*at(f"us{c}"))
                eng.wait_ge(*at(f"sa{c}"))
                tt(SA, bank(f"sa{c}"), U, ALU.add)\
                    .then_inc(v_.done, v_.tick(f"sas{c}", ("free", f"sa{c}")))

                def per_key(x, i):
                    return x[:, :, i:i + 1].to_broadcast([P, 4, HD])

                tt(Hd, Hs, per_key(ec, c), ALU.mult)\
                    .then_inc(v_.done, v_.tick())
                eng.wait_ge(*at(f"H{c}"))
                eng.wait_ge(*v_.latest())
                tt(Hs, bank(f"H{c}")[:, 0:256].rearrange("p (f n) -> p f n", f=4), per_key(ecr, c), ALU.mult)\
                    .then_inc(v_.done, v_.tick(("free", f"H{c}")))
                eng.wait_ge(*v_.latest())
                tt(Hs, Hs, Hd, ALU.add)\
                    .then_inc(v_.done, v_.tick("Hend"))
                eng.wait_ge(*v_.latest())
                if c + 1 < QT:
                    eng.wait_ge(*at(f"y{c}p"))
                    tt(Hm, Hs, per_key(em, c + 1), ALU.mult)\
                        .then_inc(v_.done, v_.tick(f"Hm{c + 1}"))
                (kind, into), h = (("sa", sa), ("yd", yd))[c % 2], c // 2
                eng.wait_ge(*v_.latest())
                eng.wait_ge(*at(f"{kind}_in{h}"))
                eng.tensor_reduce(into[:, h * 16:(h + 1) * 16], S2, AX.X, ALU.add)\
                    .then_inc(v_.done, v_.tick(f"{kind}_sum{h}"))
            eng.wait_ge(*at("wk"))
            cp(wkt, bank("wk")[0:HD, :])\
                .then_inc(v_.done, v_.tick("wkt", ("free", "wk")))
            for f in range(4):
                y = oT[:, 4 + f, :]
                for h, (lo, hi) in enumerate(HALFS):
                    eng.wait_ge(*at(f"gm{f}h{h}"))
                    stt(out=y[:, lo:hi], in0=bank(f"gm{f}h{h}")[:, 0:hi - lo], scalar=-1.0 / HD, in1=y[:, lo:hi], op0=ALU.mult, op1=ALU.add)\
                        .then_inc(v_.done, v_.tick(("free", f"gm{f}h{h}")))
                eng.wait_ge(*v_.latest())
                if f >= 2:
                    eng.wait_ge(*at(f"gv{f - 2}h1"))
                tt(sq[:, f % 2, :], y, y, ALU.mult)\
                    .then_inc(v_.done, v_.tick(f"gsq{f}"))
                eng.wait_ge(*at(f"grt{f}"))
                eng.reciprocal(rstd[:, :], rstd[:, :])\
                    .then_inc(v_.done, v_.tick())
                eng.wait_ge(*v_.latest())
                tt(y, y, rstd[:, :], ALU.mult)\
                    .then_inc(v_.done, v_.tick(f"gn{f}"))
                eng.wait_ge(*v_.latest())
                ts(y, y, col("ln_w", f), col("ln_b", f), ALU.mult, ALU.add)\
                    .then_inc(v_.done, v_.tick())
                eng.wait_ge(*v_.latest())
                tt(y, y, XR[:, 8 + f, 1:1 + NT], ALU.add)\
                    .then_inc(v_.done, v_.tick())
                eng.wait_ge(*v_.latest())
                for h, (lo, hi) in enumerate(HALFS):
                    eng.wait_ge(*at(f"gg{f}h{h}"))
                    tt(y[:, lo:hi], bank(f"gg{f}h{h}")[:, 0:hi - lo], y[:, lo:hi], ALU.mult)\
                        .then_inc(v_.done, v_.tick(("free", f"gg{f}h{h}")))
            v_.end("rwkv")

            v_.stage("ffn")
            eng.wait_ge(*at("end:rwkv:pe"))
            eng.wait_ge(*at("end:rwkv:act"))
            eng.wait_ge(*at("end:rwkv:pool"))
            eng.wait_ge(*at("stored_rwkv"))
            eng.wait_ge(*v_.latest())
            def lo_of_chunk(c):
                f, high, rest = split_parts(c)
                eng.wait_ge(*at(("hi", c)))
                tt(rest, f, high.bitcast(F32), ALU.subtract)\
                    .then_inc(v_.done, v_.tick(("lo", c)))

            def lo_of_input(which):
                for k in range(KD):
                    eng.wait_ge(*at(f"{which}hi{k}"))
                    tt(x_lo[:, k, :], hT[:, k, :], x_hi[:, k, :].bitcast(F32), ALU.subtract)\
                        .then_inc(v_.done, v_.tick(f"{which}lo{k}"))

            lo_of_chunk(("wo", 0))
            lo_of_input("o")
            lo_of_chunk(("wo", 1))
            for m in range(KD):
                for h, (lo, hi) in enumerate(HALFS):
                    eng.wait_ge(*at(f"wo{m}h{h}"))
                    tt(xT[:, m, lo:hi], bank(f"wo{m}h{h}")[:, 0:hi - lo], xT[:, m, lo:hi], ALU.add)\
                        .then_inc(v_.done, v_.tick(("free", f"wo{m}h{h}"), f"x1_{m}"))
                if m in (1, 3):
                    lo_of_chunk(("wo", m // 2 + 2))
            eng.wait_ge(*v_.latest())
            normalise("ffn", "norm_ffn")
            v_.stage("ffn")
            lo_of_chunk(("wg", 0))
            lo_of_input("ffn")
            lo_of_chunk(("wu", 0))
            for c in range(11):
                lo_of_chunk(("wg", c + 1) if c < 10 else ("wd", 0, 0))
                for m in (2 * c, 2 * c + 1):
                    if m >= 2:
                        eng.wait_ge(*at(f"act_lo{m - 2}"))
                    for h, (lo, hi) in enumerate(HALFS):
                        eng.wait_ge(*at(f"wu{m}h{h}"))
                        eng.wait_ge(*at(f"silu{m}h{h}"))
                        tt(act_f[:, m % 2, lo:hi], bank(f"wu{m}h{h}")[:, 0:hi - lo], silu[:, m % 2, lo:hi], ALU.mult)\
                            .then_inc(v_.done, v_.tick(("free", f"wu{m}h{h}"), f"act_f{m}"))
                for m in (2 * c, 2 * c + 1):
                    eng.wait_ge(*at(f"act_hi{m}"))
                    tt(act_lo[:, m, :], act_f[:, m % 2, :], act_hi[:, m, :].bitcast(F32), ALU.subtract)\
                        .then_inc(v_.done, v_.tick(f"act_lo{m}"))
                lo_of_chunk(("wu", c + 1) if c < 10 else ("wd", 0, 1))
            lo_of_chunk(("wd", 0, 2))
            for c in range(4):
                if c < 3:
                    lo_of_chunk(("wd", c + 1, 0))
                for m in (2 * c, 2 * c + 1):
                    for h, (lo, hi) in enumerate(HALFS):
                        eng.wait_ge(*at(f"wd{m}h{h}"))
                        tt(xT[:, m, lo:hi], bank(f"wd{m}h{h}")[:, 0:hi - lo], xT[:, m, lo:hi], ALU.add)\
                            .then_inc(v_.done, v_.tick(("free", f"wd{m}h{h}"), f"x2_{m}"))
                if c < 3:
                    lo_of_chunk(("wd", c + 1, 1))
                    lo_of_chunk(("wd", c + 1, 2))
            eng.wait_ge(*v_.latest())
            normalise("ple", "norm_ple")
            v_.stage("ffn")
            lo_of_chunk(("wpg", 0))
            lo_of_input("ple")
            lo_of_chunk(("wpg", 1))
            for m in range(KD):
                s_ = silu[:, m % 2, :]
                eng.wait_ge(*at(f"pep{m}"))
                for h, (lo, hi) in enumerate(HALFS):
                    eng.wait_ge(*at(f"sg{m}h{h}"))
                    tt(s_[:, lo:hi], s_[:, lo:hi], pep[:, m, lo:hi], ALU.mult)\
                        .then_inc(v_.done, v_.tick())
                eng.wait_ge(*v_.latest())
                tt(xT[:, m, :], xT[:, m, :], s_, ALU.add)\
                    .then_inc(v_.done, v_.tick(f"xfin{m}"))
                if m in (1, 3):
                    lo_of_chunk(("wpg", m // 2 + 2))
            for t in range(QT + 1):
                m = P if t < QT else NB
                eng.wait_ge(*at(f"out{t}0"))
                eng.wait_ge(*at(f"ya{t}"))
                cp(ot[0:m, t, 0:T], bank(f"out{t}0")[0:m, :])\
                    .then_inc(v_.done, v_.tick(("free", f"out{t}0"), f"y{t}"))

        return sems


_INS = ["x_prompt", "x_sample", "p_prompt", "p_sample", "cache_kv", "cache_win", "state_wkv", "state_shift",
        "page_table", "norm_mix", "w_in", "q_norm", "k_norm", "cmp_pe", "cmp_w1", "cmp_b1", "cmp_w2", "cmp_b2",
        "shift_mu", "w0", "w2", "a0", "a2", "g2", "k_k", "k_a", "r_k", "ln_w", "ln_b", "w_out", "norm_ffn", "w_gate",
        "w_up", "w_down", "norm_ple", "w_ple_gate", "w_ple"]
_OUTS = [("y_prompt", (1, T, D)), ("y_sample", (NB, 1, D)), ("kv_prompt", (1, 1, T, 4, G, HD)),
         ("kv_sample", (1, NB, 1, 4, G, HD)), ("win_prompt", (1, 1, T, 2, G, HD)),
         ("win_sample", (1, NB, PAST, 2, G, HD)), ("wkv_prompt", (1, 1, NH, HD, HD)),
         ("wkv_sample", (1, NB, NH, HD, HD)), ("shift_prompt", (1, 1, XRC)), ("shift_sample", (1, NB, XRC))]


def kernel(**inputs):
    import numpy as _np
    import concourse.bacc as _bacc
    from concourse import mybir as _mybir
    from concourse.bass_utils import run_bass_kernel_spmd as _run

    arrays = {n: _np.ascontiguousarray(inputs[n]) for n in _INS}
    points = Points()
    for _ in range(2):
        nc = _bacc.Bacc("TRN2", target_bir_lowering=False, num_devices=1, dynamic_dma_scratch_size=4096)
        a = {n: nc.dram_tensor(f"in_{n}", x.shape, _mybir.dt.from_np(x.dtype), kind="ExternalInput").ap()
             for n, x in arrays.items()}
        out = {n: nc.dram_tensor(f"out_{n}", shape, F32, kind="ExternalOutput").ap() for n, shape in _OUTS}
        build(nc, a, out, points)
        points = Points(points.new)
    r = _run(nc, [{f"in_{n}": x for n, x in arrays.items()}], core_ids=[0])
    return tuple(r.results[0][f"out_{n}"] for n, _ in _OUTS)
```

```python
from contextlib import ExitStack

import concourse.bass as bass
from concourse import mybir

F32 = mybir.dt.float32
F32R = mybir.dt.float32r
I32 = mybir.dt.int32
ALU = mybir.AluOpType
ACT = mybir.ActivationFunctionType
AX = mybir.AxisListType

P = 128
D = 1024
KD = D // P
T = 512
QT = T // P
NB = 8
NT = T + NB
HALF = NT // 2
HD = 64
NH = 8
G = 2
R = NH // G
PAST = 256
PAGE = 128
NPG = NB * PAST // PAGE
KV = 768
GATES = 3 * NH
XRC = 1792
XF = XRC // P
C_KV, C_GATE, C_XR = 512, 1280, 1304
STRIDE, BLOCK = 16, 32
NCP = (T - BLOCK) // STRIDE + 1
NCD = (PAST + 1 - BLOCK) // STRIDE + 1
FF = 2816
FT = FF // P
PLE = 256
PAIR_SEQ = NB * P + T // 2
XCMP = G * PAIR_SEQ + BLOCK // 2
NWIN = XCMP // 8 - 1
NEG = -1e30
EPS = 1e-6
GN_EPS = 64e-5
HALFS = ((0, HALF), (HALF, NT))
LEVELS = (2, 4, 8, 16, 32, 64)

ROWS = {}
for _name, _n in (("norm_mix", 8), ("norm_ffn", 8), ("norm_ple", 8), ("shift_mu", XF), ("w0", 4), ("a0", 4),
                  ("k_k", 4), ("k_a", 4), ("r_k", 4), ("ln_w", 4), ("ln_b", 4), ("q_norm", 1), ("k_norm", 3),
                  ("cmp_b1", 4), ("cmp_b2", 2)):
    ROWS[_name] = (sum(n for _, n in ROWS.values()), _n)
NROWS = sum(n for _, n in ROWS.values())


class Points:

    def __init__(self, known=None):
        self.known = known
        self.new = {}


class Steps:

    def __init__(self, name, points, sem):
        self.name, self.points, self.sem = name, points, sem
        self.count = {}
        self.key = None

    def stage(self, name):
        self.key = f"{self.name}_{name}"
        self.done = self.sem(self.key)
        self.count.setdefault(self.key, 0)

    def tick(self, *names):
        self.count[self.key] += 1
        for n in names:
            self.points.new[n] = (self.key, self.count[self.key])
        return 1

    def landed(self, key, *names):
        self.count[key] = self.count.get(key, 0) + 16
        for n in names:
            self.points.new[n] = (key, self.count[key])
        return 16

    def latest(self):
        return self.done, self.count[self.key]

    def end(self, phase):
        self.points.new[f"end:{phase}:{self.name}"] = (self.key, self.count[self.key])


def build(nc, a, out, points):
    ctx = ExitStack()
    with ctx:
        sems = {}

        def sem(name):
            if name not in sems:
                sems[name] = ctx.enter_context(nc.semaphore(name))
            return sems[name]

        start_of = {}

        def sb(name, shape, dt=F32):
            t = ctx.enter_context(nc.sbuf_tensor(name, shape, dt))
            n = 4
            for s in shape[1:]:
                n *= s
            start_of[name] = nc.sbuf_base - n
            return t

        def rounded(name, shape, within, column=0):
            return nc.alloc_sbuf_tensor_at(name, shape, F32R, offset=start_of[within] + 4 * column)

        xT = sb("xT", [P, KD, NT])
        hT = sb("hT", [P, KD, NT])
        oT = hT
        NSLOT = 3
        ring = sb("ring", [P, NSLOT, 8 * 256])
        XR = sb("XR", [P, XF, 1 + NT])
        xr_flat = XR[:, :, :].rearrange("p f n -> p (f n)")
        par_rows = sb("par_rows", [P, P])
        par = sb("par", [P, NROWS])
        ident = sb("ident", [P, P])
        ones = sb("ones", [P, P])
        blk = sb("blk", [P, P])
        causal = sb("causal", [P, P])
        us_ui = sb("us_ui", [P, 2, P])
        level = sb("level", [P, 7, P])
        level1T = sb("level1T", [P, P])
        cmp_keep = sb("cmp_keep", [P, QT, NCP])
        cmp_add = sb("cmp_add", [P, QT, NCP])
        dec_add = sb("dec_add", [64, NB, 16])
        dec_own = sb("dec_own", [64, NB])
        eps = sb("eps", [P, 2])
        qgain = sb("qgain", [P, 1])
        ka1 = sb("ka1", [P, 4])
        rstd = sb("rstd", [P, NT])
        sq = sb("sq", [P, 2, NT])
        ARENA = 29952
        arena = sb("arena", [P, ARENA])

        class Place:

            def __init__(self, at=0):
                self.at = at

            def __call__(self, n, rows=P):
                self.at += n
                assert self.at <= ARENA, self.at
                return arena[0:rows, self.at - n:self.at]

            def skip(self, n):
                self.at += n
                assert self.at <= ARENA and n % 8 == 0, self.at
                return self.at - n

        new = Place()
        zkv = new(5 * KV).rearrange("p (t n) -> p t n", t=5)
        gate = new(5 * GATES).rearrange("p (t n) -> p t n", t=5)
        late = Place(new.at)
        csq = XR[:, 0:4, :].rearrange("p f n -> p (f n)")[:, 0:NPG * P].rearrange("p (t n) -> p t n", t=NPG)
        early = Place(new.at)
        xstage = Place(new.at)(5 * D).rearrange("p (t n) -> p t n", t=5)
        xcmp = new(2 * XCMP).rearrange("p (v n) -> p v n", v=2)
        pbuf = late(4 * T).rearrange("p (i n) -> p i n", i=4)
        ptb = late(2 * T).rearrange("p (i n) -> p i n", i=2)
        assert late.at <= new.at
        diag = new(4 * P).rearrange("p (i n) -> p i n", i=4)
        qT = new(R * NT).rearrange("p (r n) -> p r n", r=R)
        qT_end = new.at
        lr_w = Place(new.at)(T)
        kT = new(2 * T).rearrange("p (v n) -> p v n", v=2)
        over = Place(new.at)
        pairs = new(10 * 512).rearrange("p (s w a d) -> p s w a d", s=10, w=4, a=2)
        ptcb = Place(over.at)(2 * NH * P).rearrange("p (i h n) -> p i h n", i=2, h=NH)
        kTd = over(2 * NB * 257).rearrange("p (v b n) -> p v b n", v=2, b=NB)
        assert over.at <= new.at
        cache_at = new.at
        cache = new(2 * NPG * 256).rearrange("p (v g n) -> p v g n", v=2, g=NPG)
        kn = new(2 * QT * P).rearrange("p (v t n) -> p v t n", v=2, t=QT)
        kn_end = new.at
        dkn = new(256, NB)
        w2c = new(256).rearrange("p (v m d) -> p v m d", v=2, m=2)
        krs = new(16).rearrange("p (v t g) -> p v t g", v=2, t=QT)
        drs = new(4, NB)
        crs = new(32).rearrange("p (t g) -> p t g", g=G)
        pcm = new(NH * NCP).rearrange("p (h n) -> p h n", h=NH)
        st = new(96)
        stc = new(32)
        scol = new(16)
        sst = new(XRC, 9)
        spare = oT[:, 4:8, :].rearrange("p f n -> p (f n)")
        gel = spare[:, 0:640].rearrange("p (m n) -> p m n", m=2)
        kc, kcn, vc = spare[:, 640:800], spare[:, 800:960], spare[:, 960:1120]
        vcd, vcp = spare[:, 1120:1248], spare[:, 1248:1376]
        qall = spare[:, 1376:1440]
        qb = spare[:, 1440:1952].rearrange("p (b n) -> p b n", b=NB)
        pcs = pbuf[0:64, 2, 0:P]

        tmp = [early(NT) for _ in range(9)]
        dvt = hT[0:NB, :, :].rearrange("p f n -> p (f n)")[:, 0:6 * T].rearrange("p (w n) -> p w n", w=6)
        factors = Place(cache_at)(4 * 2048).rearrange("p (f n) -> p f n", f=4)
        early_x_hi = rounded("early_x_hi", [P, KD, NT], "arena", cache_at)
        staged = Place(cache_at + KD * NT)(2048)
        early_w_hi = (rounded("early_w_hi0", [P, 2048], "arena", early.at),
                      rounded("early_w_hi1", [P, 2048], "arena", cache_at + KD * NT + 2048))
        shift_d = Place(cache_at + KD * NT + 4096)(NT)
        assert early.at % 8 == 0 and early.at + 2048 <= qT_end and cache_at + KD * NT + 4096 + NT <= kn_end

        def factors_of(t):
            return (t[:, :, 0:1024].rearrange("p f (c n) -> p f c n", c=QT), t[:, :, 1024:1536], t[:, :, 1536:2048])

        AR, BH, KH = factors_of(factors)
        ARs, BHs, KHs = factors_of(staged.unsqueeze(1))
        em, ec, ecr = (sb(n, [P, 4, QT])[:, :, :] for n in ("em", "ec", "ecr"))
        dv = sb("dv", [P, 6, 4, NB])[:, :, :, :]
        xlast = sb("xlast", [P, XF, 9])

        grstd = (rstd[:, :], XR[:, 12, 0:NT])

        new = Place()
        tm = new(3 * 2 * T).rearrange("p (w c n) -> p w c n", w=3, c=2)
        tmv = new(QT * T).rearrange("p (c n) -> p c n", c=QT)
        g2w = new(T)
        S = new(2048).rearrange("p (i j) -> p i j", i=32)
        ydt = new(T, NB)
        Hd = new(256).rearrange("p (f n) -> p f n", f=4)
        dvr = new(6 * HD).rearrange("p (w n) -> p w n", w=6)
        vrow, sa, yd = new(32), new(32), new(32)
        Tsb = new(2 * T).rearrange("p (g n) -> p g n", g=2)
        TTsb = new(2 * T).rearrange("p (g n) -> p g n", g=2)
        Xs = new(2 * T).rearrange("p (g n) -> p g n", g=2)
        U, ApT, SA, MV = new(T), new(T).rearrange("p (f n) -> p f n", f=4), new(T), new(T)
        ln_odd = new(2048).rearrange("p (h n) -> p h n", h=8)
        assert new.at <= cache_at
        wkt = Tsb[0:HD, 0, :]
        new = Place(cache_at + 4 * 2048)
        S2 = new(1024).rearrange("p (i j) -> p i j", i=16)
        Hs = new(256).rearrange("p (f n) -> p f n", f=4)
        Hm = new(256).rearrange("p (f n) -> p f n", f=4)
        mq_odd = new(2048).rearrange("p (h n) -> p h n", h=8)
        LNs = (xr_flat[:, 0:2048].rearrange("p (h n) -> p h n", h=8), ln_odd)
        MQs = (xr_flat[:, 4 * (NT + 1):4 * (NT + 1) + 2048].rearrange("p (h n) -> p h n", h=8), mq_odd)
        shf = par_rows

        new = Place()
        act_hi, act_lo = (rounded(n, [P, FT, NT], "arena", new.skip(FT * NT)) for n in ("act_hi", "act_lo"))
        silu = new(2 * NT).rearrange("p (i n) -> p i n", i=2)
        act_f = new(2 * NT).rearrange("p (i n) -> p i n", i=2)
        x_hi = rounded("x_hi", [P, KD, NT], "arena", new.skip(KD * NT))
        x_lo = rounded("x_lo", [P, KD, NT], "hT")
        w_hi = rounded("w_hi", [P, 2, 2048], "XR")
        w_lo = rounded("w_lo", [P, NSLOT, 2048], "ring")
        pst = xr_flat[:, 4096:4096 + 5 * PLE].rearrange("p (t n) -> p t n", t=5)
        pT = xr_flat[:, 5376:5376 + 2 * NT].rearrange("p (k n) -> p k n", k=2)
        new = Place()
        pep = new(KD * NT).rearrange("p (f n) -> p f n", f=KD)
        ot = new(5 * D).rearrange("p (t n) -> p t n", t=5)
        ssf = sb("ssf", [P, XF, NB])
        page_sb = sb("page_sb", [1, NPG], I32)

        psum = ctx.enter_context(nc.psum_tensor("psum", [P, 8, 512], F32))

        def col(name, i=0, lo=0, hi=P):
            c = ROWS[name][0] + i
            return par[lo:hi, c:c + 1]

        scratch = nc.dram_tensor("dec_scratch", (NB, NH, 6, HD), F32).ap()
        scratch_f = nc.dram_tensor("rwkv_factors", (P, 4, 2048), F32).ap()
        scratch_y = nc.dram_tensor("dec_scratch_y", (NB, T), F32).ap()

        chunks = [("xr", i) for i in range(7)] + [("kv", i) for i in range(3)] + [("gates", 0)]
        chunks += [("q", i) for i in range(2)] + [("w1", i) for i in range(4)]
        chunks += [("wo", i) for i in range(4)]
        for i in range(11):
            chunks += [("wg", i), ("wu", i)]
        chunks += [("wd", i, j) for i in range(4) for j in range(3)]
        chunks += [("wp", 0)] + [("wpg", i) for i in range(4)]
        XR_PAIRS = ((12, 13), (0, 4), (8, 1), (5, 9), (2, 6), (10, 3), (7, 11))
        slot_of = {c: i % NSLOT for i, c in enumerate(chunks)}

        def slot(c, n=256):
            return ring[:, slot_of[c], :].rearrange("p (k n) -> p k n", n=n)

        early_chunks = [c for c in chunks if c[0] in ("xr", "kv", "q")]
        split_chunks = [c for c in chunks if c[0] in ("wo", "wg", "wu", "wd", "wpg")]

        def split_parts(c):
            if c in early_chunks:
                return ring[:, slot_of[c], :], early_w_hi[early_chunks.index(c) % 2][:, :], w_lo[:, slot_of[c], :]
            n = (FT - 16) * 256 if c[0] == "wd" and c[2] == 2 else 2048
            return ring[:, slot_of[c], 0:n], w_hi[:, split_chunks.index(c) % 2, 0:n], w_lo[:, slot_of[c], 0:n]

        def split_before(c):
            of = early_chunks if c in early_chunks else split_chunks
            i = of.index(c)
            return of[i - 2] if i >= 2 else None

        bank_user = {}
        turn = {"banks": list(range(8)), "next": 0}

        def bank(name):
            return psum[:, points.known[("bank", name)] if points.known else 0, :]

        def at(name):
            key, value = points.known[name] if points.known else ("pe_load", 0)
            return sem(key), value

        steps = {n: Steps(n, points, sem) for n in ("pe", "dve", "act", "pool", "sp")}
        block = ctx.enter_context(nc.Block())

        @block.sync
        def _(eng):
            sp = steps["sp"]

            def kp(w, c0, n, k0=0, kn=KD):
                return w[k0 * P:(k0 + kn) * P, c0:c0 + n].rearrange("(k p) n -> p k n", p=P)

            eng.wait_ge(*at("x"))
            for i, c in enumerate(chunks):
                if i >= NSLOT:
                    eng.wait_ge(*at(("used", chunks[i - NSLOT])))
                if c == ("wo", 0):
                    eng.wait_ge(*at("od"))
                    eng.wait_ge(*at("stored_f3"))
                    for f in range(4):
                        eng.dma_start(factors[:, f, :], scratch_f[:, f, :])\
                            .then_inc(sem("load_f"), sp.landed("load_f", "factors"))
                dst, key, mark = slot(c), f"ring{i % NSLOT}", ("got", c)
                kind = c[0]
                if kind == "kv":
                    eng.dma_start(dst, kp(a["w_in"][0], C_KV + 256 * c[1], 256))\
                        .then_inc(sem(key), sp.landed(key, mark))
                elif kind == "gates":
                    eng.dma_start(dst[:, :, 0:GATES], kp(a["w_in"][0], C_GATE, GATES))\
                        .then_inc(sem(key), sp.landed(key, mark))
                elif kind == "q":
                    for j in range(2):
                        for g in range(G):
                            eng.dma_start(dst[:, :, j * P + g * HD:j * P + (g + 1) * HD], kp(a["w_in"][0], (g * R + 2 * c[1] + j) * HD, HD))\
                                .then_inc(sem(key), sp.landed(key, mark))
                elif kind == "xr":
                    for j, f in enumerate(XR_PAIRS[c[1]]):
                        eng.dma_start(dst[:, :, j * P:(j + 1) * P], kp(a["w_in"][0], C_XR + P * f, P))\
                            .then_inc(sem(key), sp.landed(key, mark))
                elif kind == "w1":
                    v, part = c[1] // 2, c[1] % 2
                    eng.dma_start(dst, kp(a["cmp_w1"][0, v], 0, 256, part * 8))\
                        .then_inc(sem(key), sp.landed(key, mark))
                elif kind == "wo":
                    for g in range(G):
                        src = a["w_out"][0, g * R * HD:(g + 1) * R * HD, 256 * c[1]:256 * c[1] + 256]
                        eng.dma_start(dst[g * HD:(g + 1) * HD, 0:4, :], src.rearrange("(r d) n -> d r n", d=HD))\
                            .then_inc(sem(key), sp.landed(key, mark))
                    eng.dma_start(dst[:, 4:8, :], kp(a["w_out"][0], 256 * c[1], 256, 4, 4))\
                        .then_inc(sem(key), sp.landed(key, mark))
                elif kind in ("wg", "wu"):
                    w = a["w_gate" if kind == "wg" else "w_up"][0]
                    eng.dma_start(dst, kp(w, 256 * c[1], 256))\
                        .then_inc(sem(key), sp.landed(key, mark))
                elif kind == "wd":
                    kn = min(8, FT - 8 * c[2])
                    eng.dma_start(dst[:, 0:kn, :], kp(a["w_down"][0], 256 * c[1], 256, 8 * c[2], kn))\
                        .then_inc(sem(key), sp.landed(key, mark))
                elif kind == "wp":
                    eng.dma_start(slot(c, D)[:, 0:2, :], kp(a["w_ple"][0], 0, D, 0, 2))\
                        .then_inc(sem(key), sp.landed(key, mark))
                else:
                    eng.dma_start(dst, kp(a["w_ple_gate"][0], 256 * c[1], 256))\
                        .then_inc(sem(key), sp.landed(key, mark))

        @block.gpsimd
        def _(eng):
            pl = steps["pool"]
            pl.stage("init")
            eng.memset(ident[:, :], 0.0)\
                .then_inc(pl.done, pl.tick())
            eng.memset(ones[:, :], 1.0)\
                .then_inc(pl.done, pl.tick())
            eng.memset(eps[:, 0:1], EPS)\
                .then_inc(pl.done, pl.tick())
            eng.memset(eps[:, 1:2], GN_EPS)\
                .then_inc(pl.done, pl.tick("eps"))
            eng.memset(par_rows[:, :], 0.0)\
                .then_inc(pl.done, pl.tick("par_zero"))
            eng.wait_ge(*pl.latest())
            eng.affine_select(out=ident[:, :], in_=ident[:, :], compare_op=ALU.not_equal, fill=1.0, base=0, pattern=[[-1, P]], channel_multiplier=1)\
                .then_inc(pl.done, pl.tick("ident"))
            eng.dma_start(page_sb[:, :], a["page_table"].rearrange("b n -> (b n)").rearrange("(o n) -> o n", o=1))\
                .then_inc(sem("load_page"), pl.landed("load_page", "page"))
            eng.dma_start(w2c, a["cmp_w2"][0].rearrange("v (m p) d -> p v m d", p=P))\
                .then_inc(sem("load_w2c"), pl.landed("load_w2c", "w2c"))
            eng.memset(blk[:, :], 1.0)\
                .then_inc(pl.done, pl.tick())
            eng.memset(causal[:, :], 0.0)\
                .then_inc(pl.done, pl.tick())
            eng.memset(us_ui[:, :, :], 1.0)\
                .then_inc(pl.done, pl.tick())
            eng.memset(level[:, :, :], 0.0)\
                .then_inc(pl.done, pl.tick())
            eng.memset(level1T[:, :], 0.0)\
                .then_inc(pl.done, pl.tick())
            eng.memset(cmp_keep[:, :, :], 1.0)\
                .then_inc(pl.done, pl.tick())
            eng.memset(dec_add[:, :, :], 0.0)\
                .then_inc(pl.done, pl.tick())
            eng.memset(dec_own[:, :], 1.0)\
                .then_inc(pl.done, pl.tick())
            eng.memset(XR[:, :, 0:1], 0.0)\
                .then_inc(pl.done, pl.tick())
            eng.wait_ge(*pl.latest())
            bv = blk[:, :].rearrange("p (s n) -> p s n", s=2)
            eng.affine_select(out=bv, in_=bv, compare_op=ALU.is_ge, fill=0.0, base=0, pattern=[[-HD, 2], [0, HD]], channel_multiplier=1)\
                .then_inc(pl.done, pl.tick())
            lv = {}
            for i, n in enumerate((1,) + LEVELS):
                lv[i] = level[:, i, :].rearrange("p (j s n) -> p j s n", s=2, n=n)
                eng.memset(lv[i][:, :, 0, :], 1.0)\
                    .then_inc(pl.done, pl.tick())
            lt = level1T[:, :].rearrange("p (j s) -> p j s", s=2)
            eng.memset(lt[:, :, 1:2], 1.0)\
                .then_inc(pl.done, pl.tick())
            eng.affine_select(out=causal[:, :], in_=causal[:, :], compare_op=ALU.is_ge, fill=NEG, base=0, pattern=[[-1, P]], channel_multiplier=1)\
                .then_inc(pl.done, pl.tick())
            eng.affine_select(out=us_ui[:, 0, :], in_=us_ui[:, 0, :], compare_op=ALU.is_gt, fill=0.0, base=0, pattern=[[1, P]], channel_multiplier=-1)\
                .then_inc(pl.done, pl.tick())
            eng.affine_select(out=us_ui[:, 1, :], in_=us_ui[:, 1, :], compare_op=ALU.is_ge, fill=0.0, base=0, pattern=[[1, P]], channel_multiplier=-1)\
                .then_inc(pl.done, pl.tick())
            eng.affine_select(out=cmp_keep[:, :, :], in_=cmp_keep[:, :, :], compare_op=ALU.is_ge, fill=0.0, base=-(BLOCK - 1), pattern=[[P, QT], [-STRIDE, NCP]], channel_multiplier=1)\
                .then_inc(pl.done, pl.tick())
            eng.affine_select(out=dec_add[:, :, :], in_=dec_add[:, :, :], compare_op=ALU.is_ge, fill=NEG, base=0, pattern=[[-NH, NB], [0, 16]], channel_multiplier=1)\
                .then_inc(pl.done, pl.tick())
            eng.affine_select(out=dec_own[:, :], in_=dec_own[:, :], compare_op=ALU.is_ge, fill=0.0, base=0, pattern=[[-NH, NB]], channel_multiplier=1)\
                .then_inc(pl.done, pl.tick())
            eng.wait_ge(*pl.latest())
            eng.affine_select(out=dec_add[:, :, :], in_=dec_add[:, :, :], compare_op=ALU.is_ge, fill=NEG, base=NH - 1, pattern=[[NH, NB], [0, 16]], channel_multiplier=-1)\
                .then_inc(pl.done, pl.tick())
            eng.affine_select(out=dec_own[:, :], in_=dec_own[:, :], compare_op=ALU.is_ge, fill=0.0, base=NH - 1, pattern=[[NH, NB]], channel_multiplier=-1)\
                .then_inc(pl.done, pl.tick())
            eng.affine_select(out=bv, in_=bv, compare_op=ALU.is_ge, fill=0.0, base=HD - 1, pattern=[[HD, 2], [0, HD]], channel_multiplier=-1)\
                .then_inc(pl.done, pl.tick())
            for i, n in enumerate((1,) + LEVELS):
                eng.affine_select(out=lv[i], in_=lv[i], compare_op=ALU.is_ge, fill=0.0, base=-n, pattern=[[-2 * n, P // (2 * n)], [0, 2], [0, n]], channel_multiplier=1)\
                    .then_inc(pl.done, pl.tick())
            eng.affine_select(out=lt, in_=lt, compare_op=ALU.is_equal, fill=0.0, base=0, pattern=[[-2, P // 2], [0, 2]], channel_multiplier=1)\
                .then_inc(pl.done, pl.tick())
            eng.tensor_scalar(cmp_add[:, :, :], cmp_keep[:, :, :], -NEG, NEG, ALU.mult, ALU.add)\
                .then_inc(pl.done, pl.tick())
            eng.wait_ge(*pl.latest())
            for i, n in enumerate((1,) + LEVELS):
                eng.affine_select(out=lv[i], in_=lv[i], compare_op=ALU.is_ge, fill=0.0, base=2 * n - 1, pattern=[[2 * n, P // (2 * n)], [0, 2], [0, n]], channel_multiplier=-1)\
                    .then_inc(pl.done, pl.tick())
            eng.affine_select(out=dec_add[:, :, :], in_=dec_add[:, :, :], compare_op=ALU.is_ge, fill=NEG, base=NCD - 1, pattern=[[0, NB], [-1, 16]], channel_multiplier=0)\
                .then_inc(pl.done, pl.tick("masks"))
            for half, w in ((0, "w2"), (1, "a2")):
                eng.dma_start(lr_w[half * HD:(half + 1) * HD, :], a[w][0])\
                    .then_inc(sem("load_lr"), pl.landed("load_lr", "lr_w"))
            pl.stage("att")
            eng.wait_ge(*at("page"))
            for i in range(NPG):
                pg = eng.value_load(page_sb[0:1, i:i + 1], min_val=0, max_val=a["cache_kv"].shape[1] - 1)
                src = a["cache_kv"][0, bass.ds(pg, 1)].rearrange("o (t a) v g d -> (o t) (v g) a d", a=2)
                s, h = i // 2, i % 2
                for par_ in range(2):
                    eng.dma_start(pairs[h * 64:(h + 1) * 64, s, :, par_, :], src[:, 0:4, par_, :])\
                        .then_inc(sem("load_pairs"), pl.landed("load_pairs"))
            for f in [f for pair in XR_PAIRS for f in pair]:
                d = shift_d
                eng.wait_ge(*at(f"xr_s{f}"))
                eng.wait_ge(*pl.latest())
                eng.tensor_copy(xlast[:, f, :], XR[:, f, T:T + 9])\
                    .then_inc(pl.done, pl.tick("xlast"))
                eng.tensor_tensor(d[:, 0:T], XR[:, f, 0:T], XR[:, f, 1:1 + T], ALU.subtract)\
                    .then_inc(pl.done, pl.tick())
                eng.tensor_tensor(d[:, T:NT], ssf[:, f, :], XR[:, f, 1 + T:1 + NT], ALU.subtract)\
                    .then_inc(pl.done, pl.tick())
                eng.wait_ge(*pl.latest())
                eng.tensor_scalar(d, d, col("shift_mu", f), None, ALU.mult)\
                    .then_inc(pl.done, pl.tick())
                eng.wait_ge(*pl.latest())
                eng.tensor_tensor(XR[:, f, 1:1 + NT], XR[:, f, 1:1 + NT], d, ALU.add)\
                    .then_inc(pl.done, pl.tick(f"sh{f}"))
            eng.wait_ge(*at("par_t"))
            for v in range(2):
                eng.dma_start(shf[v * 16:(v + 1) * 16, :], a["cmp_pe"][0, v].rearrange("(l a) d -> l (a d)", a=2))\
                    .then_inc(sem("load_pe"), pl.landed("load_pe", "pe_rows"))
            for b in range(NB):
                eng.dma_start(out["win_sample"][0, b, 0:PAST - 1].rearrange("t v g d -> t (v g d)"), a["cache_win"][0, b, 1:PAST].rearrange("t v g d -> t (v g d)"))\
                    .then_inc(sem("store_att"), pl.landed("store_att"))
            eng.wait_ge(*at("zkv"))
            for t in range(QT):
                eng.dma_start(out["kv_prompt"][0, 0, t * P:(t + 1) * P].rearrange("t v g d -> t (v g d)"), zkv[:, t, 0:512])\
                    .then_inc(sem("store_kv"), pl.landed("store_kv", "kv_stored"))
            for t in range(QT):
                eng.dma_start(out["win_prompt"][0, 0, t * P:(t + 1) * P].rearrange("t v g d -> t (v g d)"), zkv[:, t, 512:768])\
                    .then_inc(sem("store_att"), pl.landed("store_att"))
            eng.dma_start(out["kv_sample"][0, :, 0].rearrange("b v g d -> b (v g d)"), zkv[0:NB, QT, 0:512])\
                .then_inc(sem("store_att"), pl.landed("store_att"))
            eng.dma_start(out["win_sample"][0, :, PAST - 1].rearrange("b v g d -> b (v g d)"), zkv[0:NB, QT, 512:768])\
                .then_inc(sem("store_att"), pl.landed("store_att"))
            eng.wait_ge(*at("kv_stored"))
            for h in range(2):
                src = out["kv_prompt"][0, 0, h * 256:(h + 1) * 256].rearrange("(t a) v g d -> t (v g) a d", a=2)
                for par_ in range(2):
                    eng.dma_start(pairs[:, NB + h, :, par_, :], src[:, 0:4, par_, :])\
                        .then_inc(sem("load_pairs"), pl.landed("load_pairs", "pairs"))
            eng.wait_ge(*at("stored_f3"))
            eng.wait_ge(*at(("used", ("q", 1))))
            for i in range(NPG):
                pg = eng.value_load(page_sb[0:1, i:i + 1], min_val=0, max_val=a["cache_kv"].shape[1] - 1)
                src = a["cache_kv"][0, bass.ds(pg, 1)].rearrange("o t v g d -> (o t) (v g d)")
                eng.dma_start(cache[:, 0, i, :], src[:, 256:512])\
                    .then_inc(sem("load_cache0"), pl.landed("load_cache0", "cache0"))
            eng.wait_ge(*at("dvt"))
            for b in range(NB):
                eng.dma_start(scratch[b].rearrange("h w d -> w h d").rearrange("(o w) h d -> o w h d", o=1), dvt[b:b + 1].rearrange("p w (h d) -> p w h d", h=NH))\
                    .then_inc(sem("store_dv"), pl.landed("store_dv", "dv_stored"))
            for i in range(NPG):
                s, h = i // 2, i % 2
                src = a["cache_win"][0, s, h * P:(h + 1) * P].rearrange("t v g d -> t (v g d)")
                eng.dma_start(cache[:, 1, i, :], src)\
                    .then_inc(sem("load_cache1"), pl.landed("load_cache1", "cache1"))
            eng.wait_ge(*at("gates"))
            for b in range(NB):
                eng.dma_start(scol[b * NH:(b + 1) * NH, 0:3], gate[b:b + 1, QT, :].rearrange("p (h n) -> p h n", n=3))\
                    .then_inc(sem("load_gd"), pl.landed("load_gd", "gd"))
            eng.wait_ge(*at("shift_rows"))
            eng.dma_start(out["shift_prompt"][0], sst[0:1, :])\
                .then_inc(sem("store_att"), pl.landed("store_att"))
            eng.dma_start(out["shift_sample"][0], sst[1:9, :])\
                .then_inc(sem("store_att"), pl.landed("store_att", "stored_att"))
            pl.stage("rwkv")
            eng.wait_ge(*at("end:att:pe"))
            eng.wait_ge(*at("end:att:dve"))
            eng.wait_ge(*at("end:att:act"))
            eng.wait_ge(*at("stored_att"))
            eng.dma_start(g2w, a["g2"][0])\
                .then_inc(sem("load_lr"), pl.landed("load_lr", "g2w"))
            eng.dma_start(S.rearrange("p i j -> p (i j)"), a["state_wkv"][0].rearrange("b h (s i) j -> (b h s) (i j)", s=2))\
                .then_inc(sem("load_S"), pl.landed("load_S", "S"))
            eng.wait_ge(*at("dv_stored"))
            for s in range(2):
                eng.dma_start(dvr[s:P:2, :, :], scratch.rearrange("b h w d -> (b h) w d"))\
                    .then_inc(sem("load_dv"), pl.landed("load_dv", "dvr"))
            for h in range(2):
                eng.dma_start(vrow[h:P:2, :], scratch[:, :, 5, h * 32:(h + 1) * 32].rearrange("b h i -> (b h) i"))\
                    .then_inc(sem("load_dv"), pl.landed("load_dv", "dvr"))
            eng.wait_ge(*at("dvr"))
            eng.wait_ge(*at("S"))

            def rows_of(v, h):
                return v[:, h * 16:(h + 1) * 16].unsqueeze(2).to_broadcast([P, 16, HD])

            def over_rows(w):
                return dvr[:, w, :].unsqueeze(1).to_broadcast([P, 16, HD])

            for h in range(2):
                Sh = S[:, h * 16:(h + 1) * 16, :]
                eng.tensor_tensor(S2, Sh, over_rows(1), ALU.mult)\
                    .then_inc(pl.done, pl.tick(f"sa_in{h}"))
                eng.wait_ge(*at(f"sa_sum{h}"))
                eng.tensor_tensor(Sh, Sh, over_rows(0), ALU.mult)\
                    .then_inc(pl.done, pl.tick())
                eng.tensor_tensor(S2, rows_of(sa, h), over_rows(2), ALU.mult)\
                    .then_inc(pl.done, pl.tick())
                eng.wait_ge(*pl.latest())
                eng.tensor_tensor(Sh, Sh, S2, ALU.add)\
                    .then_inc(pl.done, pl.tick())
                eng.wait_ge(*pl.latest())
                eng.tensor_tensor(S2, rows_of(vrow, h), over_rows(3), ALU.mult)\
                    .then_inc(pl.done, pl.tick())
                eng.wait_ge(*pl.latest())
                eng.tensor_tensor(Sh, Sh, S2, ALU.add)\
                    .then_inc(pl.done, pl.tick())
                eng.wait_ge(*pl.latest())
                eng.tensor_tensor(S2, Sh, over_rows(4), ALU.mult)\
                    .then_inc(pl.done, pl.tick(f"yd_in{h}"))
                eng.wait_ge(*at(f"yd_sum{h}"))
            eng.wait_ge(*pl.latest())
            eng.dma_start(out["wkv_sample"][0].rearrange("b h (s i) j -> (b h s) (i j)", s=2), S.rearrange("p i j -> p (i j)"))\
                .then_inc(sem("store_rwkv"), pl.landed("store_rwkv"))
            eng.dma_start(scratch_y.rearrange("b (q i) -> (b q) i", i=32), yd)\
                .then_inc(sem("store_y"), pl.landed("store_y", "y_stored"))
            eng.wait_ge(*at("y_stored"))
            eng.dma_start(ydt, scratch_y)\
                .then_inc(sem("load_y"), pl.landed("load_y", "ydt"))
            eng.wait_ge(*at("wkt"))
            eng.dma_start(out["wkv_prompt"][0, 0].rearrange("h i j -> i h j"), wkt.rearrange("p (h j) -> p h j", h=NH))\
                .then_inc(sem("store_rwkv"), pl.landed("store_rwkv", "stored_rwkv"))
            pl.end("rwkv")
            eng.wait_ge(*at("end:rwkv:pe"))
            eng.wait_ge(*at("end:rwkv:dve"))
            eng.wait_ge(*at("end:rwkv:act"))
            eng.wait_ge(*at("stored_rwkv"))
            eng.wait_ge(*at("ydt"))
            for t in range(QT):
                eng.dma_start(pst[:, t, :], a["p_prompt"][0, 0, t * P:(t + 1) * P, :])\
                    .then_inc(sem("load_p"), pl.landed("load_p", "p"))
            eng.dma_start(pst[0:NB, QT, :], a["p_sample"][0, :, 0, :])\
                .then_inc(sem("load_p"), pl.landed("load_p", "p"))
            for t in range(QT):
                eng.wait_ge(*at(f"y{t}"))
                eng.dma_start(out["y_prompt"][0, t * P:(t + 1) * P, :], ot[:, t, :])\
                    .then_inc(sem("store_end"), pl.landed("store_end"))
            eng.wait_ge(*at(f"y{QT}"))
            eng.dma_start(out["y_sample"][:, 0, :], ot[0:NB, QT, :])\
                .then_inc(sem("store_end"), pl.landed("store_end", "stored_all"))
            eng.wait_ge(*at("stored_all"))

        UNITS_OF = {2: (0, 1), 4: (2, 3), 8: (4,), 16: (5,), 32: (6,), 64: (7,)}

        def side(x, n, which):
            return x.rearrange("p (m s n) -> p m s n", s=2, n=n)[:, :, which, :]

        def place(h):
            return h // 4 * 4 + h % 2 * 2 + h // 2 % 2

        @block.tensor
        def _(eng):
            pe = steps["pe"]
            mm = eng.matmul

            def banks(b):
                turn["banks"], turn["next"] = list(b), 0

            def open_(name, fixed=None):
                which = fixed
                if which is None:
                    which = turn["banks"][turn["next"] % len(turn["banks"])]
                    turn["next"] += 1
                if which in bank_user:
                    eng.wait_ge(*at(("free", bank_user[which])))
                bank_user[which] = name
                points.new[("bank", name)] = which
                return psum[:, which, :]

            def turn_(dst, src, n=P):
                return mm(dst, src, ident[0:n, 0:n], is_transpose=True, start=True, stop=True)

            pe.stage("load")
            eng.wait_ge(*at("x"))
            eng.wait_ge(*at("ident"))
            for k in range(KD):
                ps = open_(f"x{k}")
                for t in range(QT):
                    turn_(ps[:, t * P:(t + 1) * P], xstage[:, t, k * P:(k + 1) * P])\
                        .then_inc(pe.done, pe.tick(*([f"x{k}"] if t == QT - 1 else ())))
            ps = open_("xd")
            for k in range(KD):
                turn_(ps[:, k * NB:(k + 1) * NB], xstage[0:NB, QT, k * P:(k + 1) * P], NB)\
                    .then_inc(pe.done, pe.tick(*(["xd"] if k == KD - 1 else ())))
            eng.wait_ge(*at("par"))
            ps = open_("par_t")
            turn_(ps[:, 0:P], par_rows[:, :], P)\
                .then_inc(pe.done, pe.tick("par_t"))
            eng.wait_ge(*at("ss"))
            ps = open_("ss_t")
            for f in range(XF):
                turn_(ps[:, f * NB:(f + 1) * NB], sst[0:NB, f * P:(f + 1) * P], NB)\
                    .then_inc(pe.done, pe.tick(*(["ss_t"] if f == XF - 1 else ())))

            def mean_square(which):
                pe.stage("norm")
                pss = [open_(f"{which}ms{h}") for h in range(2)]
                for k in range(KD):
                    eng.wait_ge(*at(f"{which}sq{k}"))
                    for h, (lo, hi) in enumerate(HALFS):
                        mm(pss[h][:, 0:hi - lo], ones[:, :], sq[:, k % 2, lo:hi], start=(k == 0), stop=(k == KD - 1))\
                            .then_inc(pe.done, pe.tick(f"{which}ms{h}" if k == KD - 1 else f"{which}sqd{k}"))

            def dense(group, c, j, hi_x, lo_x, nk=KD, k0=0, start=True, stop=True, pss=None, used=False, wait=None, halves=(0, 1)):
                _, w1_, w2_ = split_parts(c)
                w1_, w2_ = (w.rearrange("p (k n) -> p k n", n=256) for w in (w1_, w2_))
                pss = pss or [open_(f"{group}h{h}") for h in range(2)]
                for h in halves:
                    lo, hi = HALFS[h]
                    for k in range(nk):
                        if wait:
                            eng.wait_ge(*at(f"{wait}{k}" if wait == "olo" else f"{wait}{k}h{h}"))
                        for i, (w, x) in enumerate(((w1_, hi_x), (w1_, lo_x), (w2_, hi_x))):
                            last = k == nk - 1 and i == 2
                            names = []
                            if stop and last:
                                names.append(f"{group}h{h}")
                            if used and last and h == halves[-1]:
                                names.append(("used", c))
                            mm(pss[h][:, 0:hi - lo], w[:, k, j * P:(j + 1) * P], x[:, k0 + k, lo:hi], start=(start and k == 0 and i == 0), stop=(stop and last))\
                                .then_inc(pe.done, pe.tick(*names))

            def first_dense(groups, c, hi_x, which):
                eng.wait_ge(*at(("lo", c)))
                pss = [[open_(f"{g}h{h}") for h in range(2)] for g in groups]
                for h in range(2):
                    for j, g in enumerate(groups):
                        dense(g, c, j, hi_x, x_lo, pss=pss[j], used=(j == 1 and h == 1), wait=f"{which}lo" if j == 0 else None, halves=(h,))

            mean_square("mix")
            pe.stage("proj")

            def xr_chunk(c):
                eng.wait_ge(*at(("lo", ("xr", c))))
                for j, f in enumerate(XR_PAIRS[c]):
                    dense(f"xr{f}", ("xr", c), j, early_x_hi, x_lo, used=(j == 1))

            def kv_chunk(c):
                eng.wait_ge(*at(("lo", ("kv", c))))
                _, w1_, w2_ = split_parts(("kv", c))
                w1_, w2_ = (w.rearrange("p (k n) -> p k n", n=256) for w in (w1_, w2_))
                for t in range(QT + 1):
                    m = P if t < QT else NB
                    ps = open_(f"kv{c}_{t}")
                    for k in range(KD):
                        for i, (x, w) in enumerate(((early_x_hi, w1_), (early_x_hi, w2_), (x_lo, w1_))):
                            last = k == KD - 1 and i == 2
                            names = [f"kv{c}_{t}"] if last else []
                            if last and t == QT:
                                names.append(("used", ("kv", c)))
                            mm(ps[0:m, 0:256], x[:, k, t * P:t * P + m], w[:, k, :], start=(k == 0 and i == 0), stop=last)\
                                .then_inc(pe.done, pe.tick(*names))

            def gates_chunk():
                eng.wait_ge(*at(("got", ("gates", 0))))
                w = slot(("gates", 0))
                ps = open_("gates_p")
                for t in range(QT + 1):
                    m = P if t < QT else NB
                    for k in range(KD):
                        for i, x in enumerate((early_x_hi, x_lo)):
                            last = t == QT and k == KD - 1 and i == 1
                            mm(ps[0:m, t * GATES:(t + 1) * GATES], x[:, k, t * P:t * P + m].bitcast(F32), w[:, k, 0:GATES], start=(k == 0 and i == 0), stop=(k == KD - 1 and i == 1))\
                                .then_inc(pe.done, pe.tick(*(["gates_p", ("used", ("gates", 0))] if last else [])))

            def q_chunk(c):
                eng.wait_ge(*at(("lo", ("q", c))))
                for j in range(2):
                    dense(f"q{2 * c + j}", ("q", c), j, early_x_hi, x_lo, used=(j == 1))

            def low_rank(f):
                if f == 0:
                    eng.wait_ge(*at("lr_w"))
                    eng.wait_ge(*at("lr_w_in"))
                for name, x0 in (("dec", 0), ("av", HD)):
                    for h, (lo, hi) in enumerate(HALFS):
                        ps = open_(f"{name}{f}h{h}")
                        mm(ps[:, 0:hi - lo], lr_w[x0:x0 + HD, f * P:(f + 1) * P], XR[x0:x0 + HD, 12, 1 + lo:1 + hi], start=True, stop=True)\
                            .then_inc(pe.done, pe.tick(f"{name}{f}h{h}"))

            def head_sums(name, i, f):
                eng.wait_ge(*at(f"{name}_in{f}"))
                for h, (lo, hi) in enumerate(HALFS):
                    ps = open_(f"{name}{f}h{h}")
                    mm(ps[:, 0:hi - lo], blk[:, :], sq[:, i, lo:hi], start=True, stop=True)\
                        .then_inc(pe.done, pe.tick(f"{name}{f}h{h}"))

            first_dense([f"xr{f}" for f in XR_PAIRS[0]], ("xr", 0), early_x_hi, "mix")
            xr_chunk(1)
            xr_chunk(2)
            low_rank(0)
            xr_chunk(3)
            eng.wait_ge(*at("masks"))
            head_sums("kks", 0, 0)
            xr_chunk(4)
            head_sums("bs", 1, 0)
            low_rank(1)
            xr_chunk(5)
            head_sums("kks", 0, 1)
            xr_chunk(6)
            head_sums("bs", 1, 1)
            low_rank(2)
            kv_chunk(0)
            head_sums("kks", 0, 2)
            kv_chunk(1)
            head_sums("bs", 1, 2)
            low_rank(3)
            kv_chunk(2)
            head_sums("kks", 0, 3)
            gates_chunk()
            q_chunk(0)
            head_sums("bs", 1, 3)
            q_chunk(1)
            eng.wait_ge(*at("prep3"))
            for w in range(6):
                ps = open_(f"dv{w}")
                for f in range(4):
                    turn_(ps[0:NB, f * P:(f + 1) * P], dv[:, w, f, :], P)\
                        .then_inc(pe.done, pe.tick(*([f"dv{w}"] if f == 3 else ())))
            pe.stage("att")
            banks(range(4))
            eng.wait_ge(*at("masks"))
            for f in range(XF):
                if f % 4 == 0:
                    ps = open_(f"xrl{f // 4}")
                    eng.wait_ge(*at("xlast"))
                turn_(ps[0:9, (f % 4) * P:(f % 4 + 1) * P], xlast[:, f, :], P)\
                    .then_inc(pe.done, pe.tick(*([f"xrl{f // 4}"] if f % 4 == 3 or f == XF - 1 else ())))
            eng.wait_ge(*at("pairs"))
            for v in range(2):
                for g in range(G):
                    for s0 in (0, 4, 8):
                        n = min(4, 10 - s0)
                        ps = open_(f"pair{v}{g}{s0}")
                        for s in range(n):
                            turn_(ps[:, s * P:(s + 1) * P], pairs[:, s0 + s, 2 * v + g, :, :].rearrange("p a d -> p (a d)"), P)\
                                .then_inc(pe.done, pe.tick(*([f"pair{v}{g}{s0}", "pairs_turned"] if s == n - 1 else ())))
            eng.wait_ge(*at("pe_rows"))
            ps = open_("pe_t")
            turn_(ps[:, 0:32], shf[0:32, :], 32)\
                .then_inc(pe.done, pe.tick("pe_t"))
            def windows(v):
                pss = [open_(f"conv{v}{m}", 4 + 2 * v + m) for m in range(2)]
                xv = xcmp[:, v, :].rearrange("p (w i) -> p w i", i=8)
                for l in range(16):
                    c = ("w1", 2 * v + l // 8)
                    eng.wait_ge(*at(("got", c)))
                    for m in range(2):
                        names = [("used", c)] if l % 8 == 7 and m == 1 else []
                        if l == 15:
                            names.append(f"conv{v}{m}")
                        mm(pss[m][:, 0:NWIN], slot(c)[:, l % 8, m * P:(m + 1) * P], xv[:, l // 8:l // 8 + NWIN, l % 8], start=(l == 0), stop=(l == 15))\
                            .then_inc(pe.done, pe.tick(*names))

            def second_layer(v):
                eng.wait_ge(*at(f"gel{v}"))
                eng.wait_ge(*at("w2c"))
                ps = open_(f"cmp{v}")
                for g in range(G):
                    for m in range(2):
                        mm(ps[g * HD:(g + 1) * HD, 0:160], w2c[:, v, m, :], gel[:, m, g * 160:(g + 1) * 160], start=(m == 0), stop=(m == 1))\
                            .then_inc(pe.done, pe.tick(f"cmp{v}"))

            def decode_keys(v):
                for i0 in range(0, NPG, 4):
                    ps = open_(f"ck{v}_{i0}")
                    for i in range(4):
                        eng.wait_ge(*at(f"ckn{v}"))
                        turn_(ps[:, i * P:(i + 1) * P], cache[:, v, i0 + i, 0:P], P)\
                            .then_inc(pe.done, pe.tick(*([f"ck{v}_{i0}"] if i == 3 else ())))
                eng.wait_ge(*at(f"dkn{v}"))
                ps = open_(f"dk{v}")
                turn_(ps[:, 0:NB], dkn[:, v * P:(v + 1) * P], NB)\
                    .then_inc(pe.done, pe.tick(f"dk{v}"))

            def q_squares(r):
                eng.wait_ge(*at(f"qsq{r}"))
                for h, (lo, hi) in enumerate(HALFS):
                    ps = open_(f"qms{r}h{h}")
                    mm(ps[:, 0:hi - lo], blk[:, :], sq[:, r % 2, lo:hi], start=True, stop=True)\
                        .then_inc(pe.done, pe.tick(f"qms{r}h{h}"))

            q_squares(0)
            q_squares(1)
            eng.wait_ge(*at("xcmp"))
            windows(0)
            for v in range(2):
                eng.wait_ge(*at(f"kn{v}"))
                ps = open_(f"kT{v}")
                for t in range(QT):
                    turn_(ps[:, t * P:(t + 1) * P], kn[:, v, t, :], P)\
                        .then_inc(pe.done, pe.tick(*([f"kT{v}"] if t == QT - 1 else ())))
            q_squares(2)
            q_squares(3)
            windows(1)
            second_layer(0)
            decode_keys(0)
            second_layer(1)
            decode_keys(1)
            banks(range(8))
            eng.wait_ge(*at("kcsq"))
            ps = open_("kcms")
            mm(ps[:, 0:160], blk[:, :], sq[:, 0, 0:160], start=True, stop=True)\
                .then_inc(pe.done, pe.tick("kcms"))
            eng.wait_ge(*at("vc"))
            ps = open_("vc_t")
            turn_(ps[:, 0:P], vc[:, 0:P])\
                .then_inc(pe.done, pe.tick())
            turn_(ps[0:NCP, P:2 * P], vc[:, P:P + NCP], P)\
                .then_inc(pe.done, pe.tick("vc_t"))
            eng.wait_ge(*at("qb"))
            for v in range(2):
                eng.wait_ge(*at(f"kTd{v}"))
                ps = open_(f"sd{v}")
                for b in range(NB):
                    mm(ps[0:64, 0:257], qb[:, b, :], kTd[:, v, b, :], start=(b == 0), stop=(b == NB - 1))\
                        .then_inc(pe.done, pe.tick(*([f"sd{v}"] if b == NB - 1 else [])))
            eng.wait_ge(*at("kcn"))
            ps = open_("sdc")
            mm(ps[0:64, 0:P], qall, kcn[:, 0:P], start=True, stop=True)\
                .then_inc(pe.done, pe.tick("sdc"))
            eng.wait_ge(*at("pdc"))
            ps = open_("ptc")
            mm(ps[:, 0:64], pcs[:, 0:P], diag[0:64, 2, 0:64], start=True, stop=True)\
                .then_inc(pe.done, pe.tick("ptc"))
            od = open_("od")
            eng.wait_ge(*at("ptcs"))
            eng.wait_ge(*at("vcd"))
            mm(od[:, 0:64], vcd, ptb[:, 0, 448:512], start=True, stop=True, skip_group_check=True)\
                .then_inc(pe.done, pe.tick())
            for v in range(2):
                eng.wait_ge(*at(f"pd{v}"))
                ps = open_(f"ptd{v}")
                for t in range(2):
                    mm(ps[:, t * 64:(t + 1) * 64], pbuf[0:64, v, t * P:(t + 1) * P], diag[0:64, v, 0:64], start=True, stop=True)\
                        .then_inc(pe.done, pe.tick())
                mm(ps[0:NB, 128:192], st[0:64, 64 + v * NB:64 + (v + 1) * NB], diag[0:64, v, 0:64], start=True, stop=True)\
                    .then_inc(pe.done, pe.tick(f"ptd{v}"))
                eng.wait_ge(*at(f"ptds{v}"))
                mm(od[:, 0:64], zkv[0:NB, QT, 384 + 256 * v:512 + 256 * v], ptb[0:NB, v, 128:192], start=False, stop=True, skip_group_check=True)\
                    .then_inc(pe.done, pe.tick())
                for b in range(NB):
                    for t in range(2):
                        last = v == 1 and b == NB - 1 and t == 1
                        mm(od[:, b * NH:(b + 1) * NH], cache[:, v, 2 * b + t, P:2 * P], ptb[:, v, t * 64 + b * NH:t * 64 + (b + 1) * NH], start=False, stop=True, skip_group_check=True)\
                            .then_inc(pe.done, pe.tick(*(["od"] if last else [])))
            banks(range(6))
            units = [(qt, r, g, v) for qt in range(QT) for r in range(R) for g in range(G) for v in range(2)]
            PER = len(units) // QT
            AHEAD = 3

            def scores(i):
                qt, r, g, v = units[i]
                n = (qt + 1) * P
                ps = open_(f"s{i}")
                mm(ps[:, 0:n], qT[g * HD:(g + 1) * HD, r, qt * P:(qt + 1) * P], kT[g * HD:(g + 1) * HD, v, 0:n], start=True, stop=True)\
                    .then_inc(pe.done, pe.tick(f"s{i}"))

            def block_scores(qt):
                ps = open_(f"sc{qt}")
                for g in range(G):
                    if g:
                        eng.wait_ge(*pe.latest())
                    for r in range(R):
                        h = g * R + r
                        mm(ps[:, h * NCP:(h + 1) * NCP], qT[g * HD:(g + 1) * HD, r, qt * P:(qt + 1) * P], kcn[g * HD:(g + 1) * HD, P:P + NCP], start=True, stop=True)\
                            .then_inc(pe.done, pe.tick(f"sc{qt}"))

            def block_turn(qt):
                eng.wait_ge(*at(f"pc{qt}"))
                for h2 in range(2):
                    ps = open_(f"ptc{qt}_{h2}")
                    for i in range(4):
                        turn_(ps[0:NCP, i * P:(i + 1) * P], pcm[:, h2 * 4 + i, :], P)\
                            .then_inc(pe.done, pe.tick(f"ptc{qt}_{h2}"))

            def turned(i):
                eng.wait_ge(*at(f"p{i}"))
                ps = open_(f"pt{i}")
                for j in range(units[i][0] + 1):
                    turn_(ps[:, j * P:(j + 1) * P], pbuf[:, i % 4, j * P:(j + 1) * P], P)\
                        .then_inc(pe.done, pe.tick(f"pt{i}"))

            def values(i):
                qt, r, g, v = units[i]
                if i % PER == 0:
                    open_(f"o{qt}", 6 + qt % 2)
                o = psum[g * HD:(g + 1) * HD, 6 + qt % 2, r * P:(r + 1) * P]
                if v == 0:
                    eng.wait_ge(*at(f"ptcs{qt}_{g}"))
                    mm(o, vcp[0:NCP, g * HD:(g + 1) * HD], ptcb[0:NCP, qt % 2, g * R + r, :], start=True, stop=True, skip_group_check=True)\
                        .then_inc(pe.done, pe.tick())
                eng.wait_ge(*at(f"pts{i}"))
                for j in range(qt + 1):
                    mm(o, zkv[:, j, 384 + 256 * v + g * HD:384 + 256 * v + (g + 1) * HD], ptb[:, i % 2, j * P:(j + 1) * P], start=False, stop=True, skip_group_check=True)\
                        .then_inc(pe.done, pe.tick(f"pv{i}", f"o{qt}"))

            eng.wait_ge(*at("kTs"))
            eng.wait_ge(*at("qTs"))
            block_scores(0)
            for i in range(AHEAD):
                scores(i)
            block_turn(0)
            for i in range(len(units)):
                qt, u = divmod(i, PER)
                if qt + 1 < QT and u == 8:
                    block_scores(qt + 1)
                if qt + 1 < QT and u == 12:
                    block_turn(qt + 1)
                if i + AHEAD < len(units):
                    scores(i + AHEAD)
                turned(i)
                if i:
                    values(i - 1)
            values(len(units) - 1)
            pe.end("att")

            pe.stage("rwkv")
            eng.wait_ge(*at("end:att:dve"))
            eng.wait_ge(*at("end:att:act"))
            eng.wait_ge(*at("stored_att"))
            banks(range(8))
            def rows_of_tokens(w, c):
                ps = open_(f"tm{w}{c}")
                for f in range(4):
                    s_ = slice(c * P, (c + 1) * P)
                    x = (AR[:, f, c, 0:P], BH[:, f, s_], KH[:, f, s_], XR[:, 8 + f, 1 + c * P:1 + (c + 1) * P])[w]
                    turn_(ps[:, f * P:(f + 1) * P], x, P)\
                        .then_inc(pe.done, pe.tick(*([f"tm{w}{c}"] if f == 3 else ())))

            for c in range(QT):
                rows_of_tokens(3, c)
            eng.wait_ge(*at("factors"))
            for w in range(3):
                rows_of_tokens(w, 0)
            eng.wait_ge(*at("Hm0"))
            banks(range(4))
            UNITS = [(hg, name, i) for hg in range(2) for name in ("ln", "mq") for i in range(2)]

            def chunk_products(c, unit):
                hg, name, i = UNITS[unit]
                ps = open_(f"{name}{c}{hg}{i}")
                lo = i * HD
                for fp in range(2):
                    f = hg * 2 + fp
                    mm(ps[:, fp * 256:(fp + 1) * 256], (BH if name == "ln" else KH)[lo:lo + HD, f, c * P:(c + 1) * P], AR[lo:lo + HD, f, c, :], start=True, stop=True)\
                        .then_inc(pe.done, pe.tick(f"{name}{c}{hg}{i}"))

            def chunk_l(c):
                for hg in range(2):
                    ps = open_(f"l{c}{hg}")
                    for i in range(2):
                        if i:
                            eng.wait_ge(*pe.latest())
                        lo = i * HD
                        for fp in range(2):
                            f = hg * 2 + fp
                            mm(ps[:, (i * 2 + fp) * P:(i * 2 + fp + 1) * P], AR[lo:lo + HD, f, c, 0:P], BH[lo:lo + HD, f, c * P:(c + 1) * P], start=True, stop=True)\
                                .then_inc(pe.done, pe.tick(f"l{c}{hg}"))

            for unit in range(8):
                chunk_products(0, unit)
            chunk_l(0)
            for c in range(QT):
                LN, MQ = LNs[c % 2], MQs[c % 2]
                Tb, TTb = {}, {}
                for n in LEVELS:
                    if n in (8, 16, 32) and c + 1 < QT:
                        rows_of_tokens((8, 16, 32).index(n), c + 1)
                    for hg in range(2):
                        ps = open_(f"X{c}{hg}_{n}")
                        eng.wait_ge(*at(f"Ts{c}{hg}_{n // 2}"))
                        for i in range(4):
                            mm(side(ps[:, i * P:(i + 1) * P], n, 0), LN[:, hg * 4 + i, 0:P], side(Tsb[:, hg, i * P:(i + 1) * P], n, 0), start=True, stop=True)\
                                .then_inc(pe.done, pe.tick(f"X{c}{hg}_{n}"))
                    if c + 1 < QT:
                        for unit in UNITS_OF[n]:
                            chunk_products(c + 1, unit)
                    for hg in range(2):
                        if n == LEVELS[0]:
                            Tb[hg] = open_(f"T{c}{hg}", 4 + hg)
                            TTb[hg] = open_(f"TT{c}{hg}", 6 + hg)
                        eng.wait_ge(*at(f"Xs{c}{hg}_{n}"))
                        eng.wait_ge(*at(f"TTs{c}{hg}_{n // 2}"))
                        if n < 64:
                            for i in range(4):
                                s_ = slice(i * P, (i + 1) * P)
                                out_, x = Tb[hg][:, s_], Xs[:, hg, s_]
                                if n > LEVELS[0]:
                                    out_, x = side(out_, n, 0), side(x, n, 0)
                                mm(out_, TTsb[:, hg, s_], x, start=(n == LEVELS[0] and i == 0), stop=True, skip_group_check=True)\
                                    .then_inc(pe.done, pe.tick(f"T{c}{hg}_{n}"))
                        for i in range(4):
                            s_ = slice(i * P, (i + 1) * P)
                            out_, x = TTb[hg][:, s_], TTsb[:, hg, s_]
                            if n > LEVELS[0]:
                                out_, x = side(out_, n, 1), side(x, n, 1)
                            mm(out_, Xs[:, hg, s_], x, start=(n == LEVELS[0] and i == 0), stop=True, skip_group_check=True)\
                                .then_inc(pe.done, pe.tick(f"TT{c}{hg}_{n}"))
                if c + 1 < QT:
                    chunk_l(c + 1)
                ps = open_(f"mv{c}")
                for h in range(NH):
                    mm(ps[:, h * HD:(h + 1) * HD], MQ[:, place(h), 0:P], tmv[:, c, h * HD:(h + 1) * HD], start=True, stop=True)\
                        .then_inc(pe.done, pe.tick(f"mv{c}"))
                ps = open_(f"ap{c}")
                eng.wait_ge(*at(f"TTs{c}0_64"))
                eng.wait_ge(*at(f"TTs{c}1_64"))
                for h in range(NH):
                    lo = (h % 2) * HD
                    mm(ps[lo:lo + HD, (h // 2) * P:(h // 2 + 1) * P], tm[:, 0, c % 2, h * HD:(h + 1) * HD], TTsb[:, h // 4, (place(h) % 4) * P:(place(h) % 4 + 1) * P], start=True, stop=True)\
                        .then_inc(pe.done, pe.tick(f"ap{c}"))
                eng.wait_ge(*at(f"mvs{c}"))
                ps = open_(f"u{c}")
                for h in range(NH):
                    mm(ps[:, h * HD:(h + 1) * HD], TTsb[:, h // 4, (place(h) % 4) * P:(place(h) % 4 + 1) * P], MV[:, h * HD:(h + 1) * HD], start=True, stop=True)\
                        .then_inc(pe.done, pe.tick(f"u{c}"))
                eng.wait_ge(*at(f"aps{c}"))
                eng.wait_ge(*at(f"Hm{c}"))
                ps = open_(f"sa{c}")
                for h in (0, 2, 4, 6, 1, 3, 5, 7):
                    if h == 1:
                        eng.wait_ge(*pe.latest())
                    lo, f = (h % 2) * HD, h // 2
                    mm(ps[:, h * HD:(h + 1) * HD], ApT[lo:lo + HD, f, :], Hm[lo:lo + HD, f, :], start=True, stop=True)\
                        .then_inc(pe.done, pe.tick(f"sa{c}"))
                eng.wait_ge(*at(f"sas{c}"))
                ps = open_(f"H{c}")
                for h in range(NH):
                    lo, f = (h % 2) * HD, h // 2
                    o = ps[lo:lo + HD, f * HD:(f + 1) * HD]
                    mm(o, tm[:, 1, c % 2, h * HD:(h + 1) * HD], SA[:, h * HD:(h + 1) * HD], start=True, stop=False)\
                        .then_inc(pe.done, pe.tick())
                    mm(o, tm[:, 2, c % 2, h * HD:(h + 1) * HD], tmv[:, c, h * HD:(h + 1) * HD], start=False, stop=True)\
                        .then_inc(pe.done, pe.tick(f"H{c}"))
                ps = open_(f"y{c}p")
                for h in range(NH):
                    lo, f = (h % 2) * HD, h // 2
                    o = ps[lo:lo + HD, f * P:(f + 1) * P]
                    mm(o, Hm[lo:lo + HD, f, :], AR[lo:lo + HD, f, c, P:2 * P], start=True, stop=False)\
                        .then_inc(pe.done, pe.tick())
                    mm(o, SA[:, h * HD:(h + 1) * HD], LN[:, place(h), P:2 * P], start=False, stop=False)\
                        .then_inc(pe.done, pe.tick())
                    mm(o, tmv[:, c, h * HD:(h + 1) * HD], MQ[:, place(h), P:2 * P], start=False, stop=True)\
                        .then_inc(pe.done, pe.tick(f"y{c}p"))
            eng.wait_ge(*at("Hend"))
            ps = open_("wk")
            for f in range(4):
                turn_(ps[0:HD, f * P:(f + 1) * P], Hs[:, f, :], P)\
                    .then_inc(pe.done, pe.tick(*(["wk"] if f == 3 else ())))
            eng.wait_ge(*at("ydt"))
            ps = open_("yd")
            for f in range(4):
                turn_(ps[:, f * NB:(f + 1) * NB], ydt[:, f * P:(f + 1) * P], NB)\
                    .then_inc(pe.done, pe.tick(*(["yd"] if f == 3 else ())))
            banks(range(8))
            eng.wait_ge(*at("g2w"))
            eng.wait_ge(*at("yall"))
            for f in range(5):
                if f < 4:
                    for h, (lo, hi) in enumerate(HALFS):
                        ps = open_(f"gm{f}h{h}")
                        mm(ps[:, 0:hi - lo], blk[:, :], oT[:, 4 + f, lo:hi], start=True, stop=True)\
                            .then_inc(pe.done, pe.tick(f"gm{f}h{h}"))
                if f:
                    eng.wait_ge(*at(f"gsq{f - 1}"))
                    for h, (lo, hi) in enumerate(HALFS):
                        ps = open_(f"gv{f - 1}h{h}")
                        mm(ps[:, 0:hi - lo], blk[:, :], sq[:, (f - 1) % 2, lo:hi], start=True, stop=True)\
                            .then_inc(pe.done, pe.tick(f"gv{f - 1}h{h}"))
                    for h, (lo, hi) in enumerate(HALFS):
                        ps = open_(f"gg{f - 1}h{h}")
                        mm(ps[:, 0:hi - lo], g2w[:, (f - 1) * P:f * P], XR[:, 13, 1 + lo:1 + hi], start=True, stop=True)\
                            .then_inc(pe.done, pe.tick(f"gg{f - 1}h{h}"))
            pe.end("rwkv")

            pe.stage("ffn")
            for c in range(4):
                eng.wait_ge(*at(("lo", ("wo", c))))
                for j in range(2):
                    dense(f"wo{2 * c + j}", ("wo", c), j, x_hi, x_lo, used=(j == 1), wait=None if c or j else "olo")
            mean_square("ffn")
            pe.stage("ffn")
            first_dense(("wg0", "wg1"), ("wg", 0), x_hi, "ffn")
            for c in range(11):
                for w in ("wg", "wu"):
                    if (w, c) == ("wg", 0):
                        continue
                    eng.wait_ge(*at(("lo", (w, c))))
                    for j in range(2):
                        dense(f"{w}{2 * c + j}", (w, c), j, x_hi, x_lo, used=(j == 1))
            for c in range(4):
                pss = [[open_(f"wd{2 * c + j}h{h}") for h in range(2)] for j in range(2)]
                for i in range(3):
                    eng.wait_ge(*at(("lo", ("wd", c, i))))
                    eng.wait_ge(*at(f"act_lo{min(FT, 8 * i + 8) - 1}"))
                    for j in range(2):
                        dense(f"wd{2 * c + j}", ("wd", c, i), j, act_hi, act_lo, min(8, FT - 8 * i), 8 * i, start=(i == 0),
                               stop=(i == 2), pss=pss[j], used=(j == 1))
            eng.wait_ge(*at("p"))
            for k in range(2):
                ps = open_(f"pe{k}")
                for t in range(QT):
                    turn_(ps[:, t * P:(t + 1) * P], pst[:, t, k * P:(k + 1) * P], P)\
                        .then_inc(pe.done, pe.tick(*([f"pe{k}"] if t == QT - 1 else ())))
            ps = open_("pd")
            for k in range(2):
                turn_(ps[:, k * NB:(k + 1) * NB], pst[0:NB, QT, k * P:(k + 1) * P], NB)\
                    .then_inc(pe.done, pe.tick("pd"))
            mean_square("ple")
            pe.stage("ffn")
            eng.wait_ge(*at("pTs"))
            eng.wait_ge(*at(("got", ("wp", 0))))
            w = slot(("wp", 0), D)
            for m in range(KD):
                for h, (lo, hi) in enumerate(HALFS):
                    ps = open_(f"wp{m}h{h}")
                    for k in range(2):
                        names = [f"wp{m}h{h}"] if k == 1 else []
                        if m == KD - 1 and h == 1 and k == 1:
                            names.append(("used", ("wp", 0)))
                        mm(ps[:, 0:hi - lo], w[:, k, m * P:(m + 1) * P], pT[:, k, lo:hi], start=(k == 0), stop=(k == 1))\
                            .then_inc(pe.done, pe.tick(*names))
            first_dense(("wpg0", "wpg1"), ("wpg", 0), x_hi, "ple")
            for c in range(1, 4):
                eng.wait_ge(*at(("lo", ("wpg", c))))
                for j in range(2):
                    dense(f"wpg{2 * c + j}", ("wpg", c), j, x_hi, x_lo, used=(j == 1))
            for t in range(QT + 1):
                m = P if t < QT else NB
                for k2 in range(2):
                    ps = open_(f"out{t}{k2}")
                    for k in range(4):
                        eng.wait_ge(*at(f"xfin{k2 * 4 + k}"))
                        turn_(ps[0:m, k * P:(k + 1) * P], xT[:, k2 * 4 + k, t * P:t * P + m], P)\
                            .then_inc(pe.done, pe.tick(*([f"out{t}{k2}"] if k == 3 else ())))


        @block.scalar
        def _(eng):
            ac = steps["act"]

            def squares(which, xs):
                ac.stage("norm")
                for k in range(KD):
                    eng.wait_ge(*at(xs(k)))
                    if k >= 2:
                        eng.wait_ge(*at(f"{which}sqd{k - 2}"))
                    eng.activation(sq[:, k % 2, :], xT[:, k, :], ACT.Square)\
                        .then_inc(ac.done, ac.tick(f"{which}sq{k}"))
                for h, (lo, hi) in enumerate(HALFS):
                    eng.wait_ge(*at(f"{which}ms{h}"))
                    eng.activation(rstd[:, lo:hi], bank(f"{which}ms{h}")[:, 0:hi - lo], ACT.Sqrt, scale=1.0 / D, bias=eps[:, 0:1])\
                        .then_inc(ac.done, ac.tick(f"{which}rt{h}", ("free", f"{which}ms{h}")))

            def hi_of_chunk(c):
                f, high, _ = split_parts(c)
                eng.wait_ge(*at(("got", c)))
                if split_before(c):
                    eng.wait_ge(*at(("used", split_before(c))))
                eng.activation(high, f, ACT.Copy)\
                    .then_inc(ac.done, ac.tick(("hi", c)))

            def hi_of_norm(which, into):
                for h, (lo, hi) in enumerate(HALFS):
                    for k in range(KD):
                        eng.wait_ge(*at(f"{which}h{k}h{h}"))
                        eng.activation(into[:, k, lo:hi], hT[:, k, lo:hi], ACT.Copy)\
                            .then_inc(ac.done, ac.tick(f"{which}hi{k}h{h}"))

            def hi_of_input(which, ready, into=x_hi, tiles=range(KD)):
                for k in tiles:
                    eng.wait_ge(*at(ready(k)))
                    eng.activation(into[:, k, :], hT[:, k, :], ACT.Copy)\
                        .then_inc(ac.done, ac.tick(f"{which}hi{k}"))

            for t in range(QT):
                eng.dma_start(xstage[:, t, :], a["x_prompt"][0, t * P:(t + 1) * P, :])\
                    .then_inc(sem("load_x"), ac.landed("load_x"))
            eng.dma_start(xstage[0:NB, QT, :], a["x_sample"][:, 0, :])\
                .then_inc(sem("load_x"), ac.landed("load_x", "x"))
            eng.wait_ge(*at("par_zero"))
            for name, (r0, n) in ROWS.items():
                src = a[name][0]
                if name in ("q_norm", "cmp_b2", "k_norm"):
                    src = src.rearrange("(r d) -> r d", r=1) if name == "q_norm" else src
                    for g in range(G):
                        eng.dma_start(par_rows[r0:r0 + n, g * HD:(g + 1) * HD], src)\
                            .then_inc(sem("load_par"), ac.landed("load_par", "par"))
                    continue
                if name == "r_k":
                    src = src.rearrange("(f h) d -> f (h d)", h=2)
                elif name == "cmp_b1":
                    src = src.rearrange("v (m c) -> (v m) c", c=P)
                else:
                    src = src.rearrange("(f c) -> f c", c=P)
                eng.dma_start(par_rows[r0:r0 + n, :], src)\
                    .then_inc(sem("load_par"), ac.landed("load_par", "par"))
            eng.dma_start(sst[0:NB, :], a["state_shift"][0])\
                .then_inc(sem("load_ss"), ac.landed("load_ss", "ss"))
            eng.wait_ge(*at("eps"))
            ac.stage("proj")
            eng.wait_ge(*at("xT"))
            hi_of_chunk(("xr", 0))
            squares("mix", lambda k: "xT")
            ac.stage("proj")
            def kv_rows(c):
                for t in range(QT + 1):
                    m = P if t < QT else NB
                    eng.wait_ge(*at(f"kv{c}_{t}"))
                    eng.activation(zkv[0:m, t, c * 256:(c + 1) * 256], bank(f"kv{c}_{t}")[0:m, 0:256], ACT.Copy)\
                        .then_inc(ac.done, ac.tick(("free", f"kv{c}_{t}"), "zkv"))

            def sigmoids(f):
                if f:
                    eng.wait_ge(*at(f"kk_a{f - 1}"))
                for name, i, bias in (("dec", 2, "w0"), ("av", 3, "a0")):
                    for h, (lo, hi) in enumerate(HALFS):
                        eng.wait_ge(*at(f"{name}{f}h{h}"))
                        eng.activation(tmp[i][:, lo:hi], bank(f"{name}{f}h{h}")[:, 0:hi - lo], ACT.Sigmoid, bias=col(bias, f))\
                            .then_inc(ac.done, ac.tick(("free", f"{name}{f}h{h}"), f"sig{f}"))

            def kk_norms(f):
                for h, (lo, hi) in enumerate(HALFS):
                    eng.wait_ge(*at(f"kks{f}h{h}"))
                    eng.activation(tmp[5][:, lo:hi], bank(f"kks{f}h{h}")[:, 0:hi - lo], ACT.Sqrt)\
                        .then_inc(ac.done, ac.tick(("free", f"kks{f}h{h}"), f"kkn{f}"))

            def store_factors(f):
                eng.wait_ge(*at(f"prep{f}"))
                eng.dma_start(scratch_f[:, f, :], staged)\
                    .then_inc(sem("store_f"), ac.landed("store_f", f"stored_f{f}"))

            def decays(f):
                if f:
                    store_factors(f - 1)
                eng.wait_ge(*at(f"cl{f}"))
                cl = tmp[6][:, 0:T].rearrange("p (c n) -> p c n", c=QT)
                eng.activation(em[:, f, :], cl[:, :, 63], ACT.Exp)\
                    .then_inc(ac.done, ac.tick())
                eng.activation(ec[:, f, :], cl[:, :, 127], ACT.Exp)\
                    .then_inc(ac.done, ac.tick())
                eng.activation(dv[:, 0, f, :], tmp[2][:, T:NT], ACT.Exp)\
                    .then_inc(ac.done, ac.tick(f"dvw{f}"))
                eng.wait_ge(*at(f"clm{f}"))
                clm = tmp[7][:, 0:T].rearrange("p (c n) -> p c n", c=QT)
                eng.activation(ecr[:, f, :], clm[:, :, 127], ACT.Exp)\
                    .then_inc(ac.done, ac.tick())
                eng.activation(tmp[8][:, 0:T], tmp[8][:, 0:T], ACT.Exp)\
                    .then_inc(ac.done, ac.tick())
                eng.wait_ge(*ac.latest())
                eng.activation(tmp[6][:, 0:T], tmp[7][:, 0:T], ACT.Exp)\
                    .then_inc(ac.done, ac.tick())
                eng.activation(tmp[1][:, 0:T], tmp[7][:, 0:T], ACT.Exp, scale=-1.0)\
                    .then_inc(ac.done, ac.tick(f"E{f}"))

            hi_of_norm("mix", early_x_hi)
            hi_of_chunk(("xr", 1))
            hi_of_chunk(("xr", 2))
            eng.wait_ge(*at("sh12"))
            eng.activation(XR[0:HD, 12, 1:1 + NT], XR[0:HD, 12, 1:1 + NT], ACT.Tanh)\
                .then_inc(ac.done, ac.tick("lr_w_in"))
            eng.wait_ge(*at("sh13"))
            eng.activation(XR[:, 13, 1:1 + NT], XR[:, 13, 1:1 + NT], ACT.Sigmoid)\
                .then_inc(ac.done, ac.tick("lr_in"))
            hi_of_chunk(("xr", 3))
            hi_of_chunk(("xr", 4))
            sigmoids(0)
            hi_of_chunk(("xr", 5))
            kk_norms(0)
            decays(0)
            hi_of_chunk(("xr", 6))
            sigmoids(1)
            hi_of_chunk(("kv", 0))
            kk_norms(1)
            decays(1)
            hi_of_chunk(("kv", 1))
            sigmoids(2)
            hi_of_chunk(("kv", 2))
            kv_rows(0)
            kk_norms(2)
            decays(2)
            kv_rows(1)
            sigmoids(3)
            hi_of_chunk(("q", 0))
            kk_norms(3)
            kv_rows(2)
            decays(3)
            store_factors(3)
            eng.wait_ge(*at("gates_p"))
            ps = bank("gates_p")
            eng.activation(gate[:, 0:QT, :], ps[:, 0:QT * GATES].rearrange("p (t n) -> p t n", t=QT), ACT.Sigmoid)\
                .then_inc(ac.done, ac.tick())
            eng.activation(gate[0:NB, QT, :], ps[0:NB, QT * GATES:(QT + 1) * GATES], ACT.Sigmoid)\
                .then_inc(ac.done, ac.tick("gates", ("free", "gates_p")))
            hi_of_chunk(("q", 1))
            for r in range(R):
                eng.wait_ge(*at(("used", ("q", r // 2))))
                for h, (lo, hi) in enumerate(HALFS):
                    eng.wait_ge(*at(f"q{r}h{h}"))
                    eng.activation(qT[:, r, lo:hi], bank(f"q{r}h{h}")[:, 0:hi - lo], ACT.Copy)\
                        .then_inc(ac.done, ac.tick(("free", f"q{r}h{h}"), f"q_s{r}"))
            ac.stage("att")

            def q_squares(r):
                eng.wait_ge(*at(f"q_s{r}"))
                if r >= 2:
                    eng.wait_ge(*at(f"qms{r - 2}h1"))
                eng.activation(sq[:, r % 2, :], qT[:, r, :], ACT.Square)\
                    .then_inc(ac.done, ac.tick(f"qsq{r}"))

            def q_roots(r):
                for h, (lo, hi) in enumerate(HALFS):
                    eng.wait_ge(*at(f"qms{r}h{h}"))
                    if r:
                        eng.wait_ge(*at(f"q_n{r - 1}"))
                    eng.activation(rstd[:, lo:hi], bank(f"qms{r}h{h}")[:, 0:hi - lo], ACT.Sqrt, scale=1.0 / HD, bias=eps[:, 0:1])\
                        .then_inc(ac.done, ac.tick(f"qrt{r}", ("free", f"qms{r}h{h}")))

            q_squares(0)
            q_squares(1)
            eng.wait_ge(*at("kss"))
            eng.activation(krs, krs, ACT.Sqrt, scale=1.0 / HD, bias=eps[:, 0:1])\
                .then_inc(ac.done, ac.tick())
            eng.activation(drs, drs, ACT.Sqrt, scale=1.0 / HD, bias=eps[0:NB, 0:1])\
                .then_inc(ac.done, ac.tick("krt"))
            for v in range(2):
                for g in range(G):
                    for s0 in (0, 4, 8):
                        n = min(4, 10 - s0) * P
                        eng.wait_ge(*at(f"pair{v}{g}{s0}"))
                        col0 = g * PAIR_SEQ + s0 * P
                        eng.activation(xcmp[:, v, col0:col0 + n], bank(f"pair{v}{g}{s0}")[:, 0:n], ACT.Copy)\
                            .then_inc(ac.done, ac.tick(("free", f"pair{v}{g}{s0}")))
            eng.wait_ge(*at("pe_t"))
            eng.activation(xcmp[:, :, G * PAIR_SEQ:XCMP], bank("pe_t")[:, 0:32].rearrange("p (v n) -> p v n", v=2), ACT.Copy)\
                .then_inc(ac.done, ac.tick(("free", "pe_t"), "xcmp"))
            for r in range(2):
                q_roots(r)
                q_squares(r + 2)
            for v in range(2):
                eng.wait_ge(*at(f"kT{v}"))
                eng.activation(kT[:, v, :], bank(f"kT{v}"), ACT.Copy, scale=col("k_norm", 1 + v))\
                    .then_inc(ac.done, ac.tick(("free", f"kT{v}"), "kTs"))
            q_roots(2)
            q_roots(3)
            for v in range(2):
                eng.wait_ge(*at(f"cache{v}"))
                eng.activation(csq, cache[:, v, :, 0:P], ACT.Square)\
                    .then_inc(ac.done, ac.tick(f"csq{v}"))
                eng.wait_ge(*at(f"css{v}"))
                eng.activation(crs, crs, ACT.Sqrt, scale=1.0 / HD, bias=eps[:, 0:1])\
                    .then_inc(ac.done, ac.tick(f"crt{v}"))
                eng.wait_ge(*at("dv_stored"))
                for m in range(2):
                    eng.wait_ge(*at(f"cb{v}{m}"))
                    if v:
                        eng.wait_ge(*at("cmp0"))
                    eng.activation(gel[:, m, :], bank(f"conv{v}{m}")[:, 0:320], ACT.Gelu_apprx_tanh, bias=stc[:, 2 * v + m:2 * v + m + 1])\
                        .then_inc(ac.done, ac.tick(f"gel{v}", ("free", f"conv{v}{m}")))
            for v in range(2):
                if v == 0:
                    eng.wait_ge(*at("pairs_turned"))
                for i0 in range(0, NPG, 4):
                    eng.wait_ge(*at(f"ck{v}_{i0}"))
                    eng.activation(kTd[:, v, i0 // 2:i0 // 2 + 2, 0:PAST], bank(f"ck{v}_{i0}").rearrange("p (b n) -> p b n", b=2), ACT.Copy, scale=col("k_norm", 1 + v))\
                        .then_inc(ac.done, ac.tick(("free", f"ck{v}_{i0}")))
                eng.wait_ge(*at(f"dk{v}"))
                eng.activation(kTd[:, v, :, PAST], bank(f"dk{v}")[:, 0:NB], ACT.Copy, scale=col("k_norm", 1 + v))\
                    .then_inc(ac.done, ac.tick(("free", f"dk{v}"), f"kTd{v}"))
            eng.wait_ge(*at("kcms"))
            eng.activation(kcn, bank("kcms")[:, 0:160], ACT.Sqrt, scale=1.0 / HD, bias=eps[:, 0:1])\
                .then_inc(ac.done, ac.tick("kcrt", ("free", "kcms")))
            for v in range(2):
                eng.wait_ge(*at(f"sdm{v}"))
                eng.activation(pbuf[0:64, v, 0:257], bank(f"sd{v}")[0:64, 0:257], ACT.Exp, bias=st[0:64, v:v + 1], accum_out=st[0:64, 4 + v:5 + v])\
                    .then_inc(ac.done, ac.tick(f"sde{v}", ("free", f"sd{v}")))
            eng.wait_ge(*at("sdm2"))
            eng.activation(pcs, pcs, ACT.Exp, bias=st[0:64, 2:3], accum_out=st[0:64, 6:7])\
                .then_inc(ac.done, ac.tick("sde2"))
            eng.wait_ge(*at("ptc"))
            eng.activation(ptb[:, 0, 448:512], bank("ptc")[:, 0:64], ACT.Copy)\
                .then_inc(ac.done, ac.tick(("free", "ptc"), "ptcs"))
            for v in range(2):
                eng.wait_ge(*at(f"ptd{v}"))
                eng.activation(ptb[:, v, 0:128], bank(f"ptd{v}")[:, 0:128], ACT.Copy)\
                    .then_inc(ac.done, ac.tick())
                eng.activation(ptb[0:NB, v, 128:192], bank(f"ptd{v}")[0:NB, 128:192], ACT.Copy)\
                    .then_inc(ac.done, ac.tick(("free", f"ptd{v}"), f"ptds{v}"))
            PER, AHEAD = 16, 3
            UNITS = QT * PER

            def exp_unit(i):
                n = (i // PER + 1) * P
                eng.wait_ge(*at(f"sm{i}"))
                eng.wait_ge(*at("od" if i < 4 else f"pt{i - 4}"))
                eng.activation(pbuf[:, i % 4, 0:n], bank(f"s{i}")[:, 0:n], ACT.Exp, bias=st[:, i % 4:i % 4 + 1], accum_out=st[:, 8 + i % 4:9 + i % 4])\
                    .then_inc(ac.done, ac.tick(f"se{i}", ("free", f"s{i}")))

            def evac_unit(i):
                n = (i // PER + 1) * P
                eng.wait_ge(*at(f"pt{i}"))
                eng.wait_ge(*at("od" if i < 2 else f"pv{i - 2}"))
                eng.activation(ptb[:, i % 2, 0:n], bank(f"pt{i}")[:, 0:n], ACT.Copy)\
                    .then_inc(ac.done, ac.tick(f"pts{i}", ("free", f"pt{i}")))

            def block_exp(qt):
                eng.wait_ge(*at(f"scm{qt}"))
                eng.activation(pcm, pcm, ACT.Exp)\
                    .then_inc(ac.done, ac.tick(f"sce{qt}"))

            def block_evac(qt):
                for h2 in range(2):
                    eng.wait_ge(*at(f"ptc{qt}_{h2}"))
                    eng.wait_ge(*at("od" if qt < 2 else f"o{qt - 2}"))
                    eng.activation(ptcb[0:NCP, qt % 2, h2 * 4:h2 * 4 + 4, :], bank(f"ptc{qt}_{h2}")[0:NCP, :].rearrange("p (h n) -> p h n", h=4), ACT.Copy)\
                        .then_inc(ac.done, ac.tick(("free", f"ptc{qt}_{h2}"), f"ptcs{qt}_{h2}"))

            block_exp(0)
            for i in range(AHEAD):
                exp_unit(i)
            block_evac(0)
            for i in range(UNITS):
                qt, u = divmod(i, PER)
                if qt + 1 < QT and u == 9:
                    block_exp(qt + 1)
                if qt + 1 < QT and u == 12:
                    block_evac(qt + 1)
                if i + AHEAD < UNITS:
                    exp_unit(i + AHEAD)
                evac_unit(i)
            ac.end("att")

            ac.stage("rwkv")
            eng.wait_ge(*at("end:att:pe"))
            eng.wait_ge(*at("end:att:dve"))
            eng.wait_ge(*at("stored_att"))

            def rows_of_tokens(w, c):
                eng.wait_ge(*at(f"tm{w}{c}"))
                eng.activation(tmv[:, c, :] if w == 3 else tm[:, w, c % 2, :], bank(f"tm{w}{c}"), ACT.Copy)\
                    .then_inc(ac.done, ac.tick(("free", f"tm{w}{c}"), f"tms{w}{c}"))

            for c in range(QT):
                rows_of_tokens(3, c)
            for w in range(3):
                rows_of_tokens(w, 0)
            for c in range(QT):
                for n in LEVELS:
                    if n in (8, 16, 32) and c + 1 < QT:
                        rows_of_tokens((8, 16, 32).index(n), c + 1)
                    for hg in range(2):
                        if n < 64:
                            eng.wait_ge(*at(f"T{c}{hg}_{n}"))
                            eng.activation(side(Tsb[:, hg, :], n, 0), side(bank(f"T{c}{hg}"), n, 0), ACT.Copy)\
                                .then_inc(ac.done, ac.tick(f"Ts{c}{hg}_{n}", *([("free", f"T{c}{hg}")] if n == 32 else [])))
                        eng.wait_ge(*at(f"TT{c}{hg}_{n}"))
                        eng.activation(side(TTsb[:, hg, :], n, 1), side(bank(f"TT{c}{hg}"), n, 1), ACT.Copy)\
                            .then_inc(ac.done, ac.tick(f"TTs{c}{hg}_{n}", *([("free", f"TT{c}{hg}")] if n == 64 else [])))
                eng.wait_ge(*at(f"ap{c}"))
                eng.activation(ApT.rearrange("p f n -> p (f n)"), bank(f"ap{c}"), ACT.Copy)\
                    .then_inc(ac.done, ac.tick(f"aps{c}", ("free", f"ap{c}")))
                eng.wait_ge(*at(f"u{c}"))
                eng.activation(U, bank(f"u{c}"), ACT.Copy)\
                    .then_inc(ac.done, ac.tick(f"us{c}", ("free", f"u{c}")))
                eng.wait_ge(*at(f"y{c}p"))
                eng.activation(oT[:, 4:8, c * P:(c + 1) * P], bank(f"y{c}p").rearrange("p (f n) -> p f n", f=4), ACT.Copy)\
                    .then_inc(ac.done, ac.tick(("free", f"y{c}p")))
            eng.wait_ge(*at("yd"))
            eng.activation(oT[:, 4:8, T:NT], bank("yd")[:, 0:4 * NB].rearrange("p (f b) -> p f b", f=4), ACT.Copy)\
                .then_inc(ac.done, ac.tick(("free", "yd"), "yall"))
            eng.wait_ge(*at("wkt"))
            eng.wait_ge(*at("yd_sum1"))
            hi_of_chunk(("wo", 0))
            hi_of_input("o", lambda k: "wkt", tiles=range(4))
            for f in range(4):
                if f >= 2:
                    eng.wait_ge(*at(f"gn{f - 2}"))
                for h, (lo, hi) in enumerate(HALFS):
                    eng.wait_ge(*at(f"gv{f}h{h}"))
                    eng.activation(grstd[f % 2][:, lo:hi], bank(f"gv{f}h{h}")[:, 0:hi - lo], ACT.Sqrt, scale=1.0 / HD, bias=eps[:, 1:2])\
                        .then_inc(ac.done, ac.tick(f"grt{f}", ("free", f"gv{f}h{h}")))
                if f == 0:
                    hi_of_chunk(("wo", 1))
                if f >= 2:
                    hi_of_input("o", lambda k: f"yf{k - 4}", tiles=[4 + f - 2])
            ac.end("rwkv")
            ac.stage("ffn")
            hi_of_input("o", lambda k: f"yf{k - 4}", tiles=[6, 7])
            hi_of_chunk(("wo", 2))
            hi_of_chunk(("wo", 3))
            hi_of_chunk(("wg", 0))
            squares("ffn", lambda k: f"x1_{k}")
            ac.stage("ffn")
            eng.wait_ge(*at("end:rwkv:dve"))
            eng.wait_ge(*at("end:rwkv:pe"))
            eng.wait_ge(*at("end:rwkv:pool"))
            eng.wait_ge(*at("stored_rwkv"))
            hi_of_norm("ffn", x_hi)
            hi_of_chunk(("wu", 0))
            for c in range(11):
                for m in (2 * c, 2 * c + 1):
                    if m >= 2:
                        eng.wait_ge(*at(f"act_f{m - 2}"))
                    for h, (lo, hi) in enumerate(HALFS):
                        eng.wait_ge(*at(f"wg{m}h{h}"))
                        eng.activation(silu[:, m % 2, lo:hi], bank(f"wg{m}h{h}")[:, 0:hi - lo], ACT.Silu)\
                            .then_inc(ac.done, ac.tick(f"silu{m}h{h}", ("free", f"wg{m}h{h}")))
                hi_of_chunk(("wg", c + 1) if c < 10 else ("wd", 0, 0))
                for m in (2 * c, 2 * c + 1):
                    eng.wait_ge(*at(f"act_f{m}"))
                    eng.activation(act_hi[:, m, :], act_f[:, m % 2, :], ACT.Copy)\
                        .then_inc(ac.done, ac.tick(f"act_hi{m}"))
                hi_of_chunk(("wu", c + 1) if c < 10 else ("wd", 0, 1))
            for i in range(2, 12):
                hi_of_chunk(("wd", i // 3, i % 3))
            for k in range(2):
                eng.wait_ge(*at(f"pe{k}"))
                eng.activation(pT[:, k, 0:T], bank(f"pe{k}"), ACT.Copy)\
                    .then_inc(ac.done, ac.tick(("free", f"pe{k}")))
            eng.wait_ge(*at("pd"))
            eng.activation(pT[:, :, T:NT], bank("pd")[:, 0:2 * NB].rearrange("p (k b) -> p k b", k=2), ACT.Copy)\
                .then_inc(ac.done, ac.tick(("free", "pd"), "pTs"))
            squares("ple", lambda k: f"x2_{k}")
            ac.stage("ffn")
            hi_of_chunk(("wpg", 0))
            hi_of_norm("ple", x_hi)
            for m in range(KD):
                for h, (lo, hi) in enumerate(HALFS):
                    eng.wait_ge(*at(f"wp{m}h{h}"))
                    eng.activation(pep[:, m, lo:hi], bank(f"wp{m}h{h}")[:, 0:hi - lo], ACT.Copy)\
                        .then_inc(ac.done, ac.tick(f"pep{m}", ("free", f"wp{m}h{h}")))
            hi_of_chunk(("wpg", 1))
            for m in range(KD):
                if m >= 2:
                    eng.wait_ge(*at(f"xfin{m - 2}"))
                for h, (lo, hi) in enumerate(HALFS):
                    eng.wait_ge(*at(f"wpg{m}h{h}"))
                    eng.activation(silu[:, m % 2, lo:hi], bank(f"wpg{m}h{h}")[:, 0:hi - lo], ACT.Sigmoid)\
                        .then_inc(ac.done, ac.tick(f"sg{m}h{h}", ("free", f"wpg{m}h{h}")))
                if m in (1, 3):
                    hi_of_chunk(("wpg", m // 2 + 2))
            for t in range(QT + 1):
                m = P if t < QT else NB
                eng.wait_ge(*at(f"out{t}1"))
                eng.activation(ot[0:m, t, T:2 * T], bank(f"out{t}1")[0:m, :], ACT.Copy)\
                    .then_inc(ac.done, ac.tick(("free", f"out{t}1"), f"ya{t}"))

        @block.vector
        def _(eng):
            v_ = steps["dve"]
            tt, ts, stt, cp = eng.tensor_tensor, eng.tensor_scalar, eng.scalar_tensor_tensor, eng.tensor_copy

            def normalise(which, gain, high, chunk=None):
                v_.stage("norm")
                for h, (lo, hi) in enumerate(HALFS):
                    eng.wait_ge(*at(f"{which}rt{h}"))
                    eng.reciprocal(rstd[:, lo:hi], rstd[:, lo:hi])\
                        .then_inc(v_.done, v_.tick())
                    eng.wait_ge(*v_.latest())
                    for k in range(KD):
                        stt(out=hT[:, k, lo:hi], in0=xT[:, k, lo:hi], scalar=col(gain, k), in1=rstd[:, lo:hi], op0=ALU.mult, op1=ALU.mult)\
                            .then_inc(v_.done, v_.tick(f"{which}h{k}h{h}"))
                    if chunk and h == 0:
                        lo_of_chunk(chunk)
                    for k in range(KD):
                        eng.wait_ge(*at(f"{which}hi{k}h{h}"))
                        tt(x_lo[:, k, lo:hi], hT[:, k, lo:hi], high[:, k, lo:hi].bitcast(F32), ALU.subtract)\
                            .then_inc(v_.done, v_.tick(f"{which}lo{k}h{h}"))

            def lo_of_chunk(c):
                f, high, rest = split_parts(c)
                eng.wait_ge(*at(("hi", c)))
                tt(rest, f, high.bitcast(F32), ALU.subtract)\
                    .then_inc(v_.done, v_.tick(("lo", c)))

            def lo_of_input(which, high=x_hi, tiles=range(KD)):
                for k in tiles:
                    eng.wait_ge(*at(f"{which}hi{k}"))
                    tt(x_lo[:, k, :], hT[:, k, :], high[:, k, :].bitcast(F32), ALU.subtract)\
                        .then_inc(v_.done, v_.tick(f"{which}lo{k}"))

            v_.stage("load")
            for k in range(KD):
                eng.wait_ge(*at(f"x{k}"))
                cp(xT[:, k, 0:T], bank(f"x{k}"))\
                    .then_inc(v_.done, v_.tick(("free", f"x{k}")))
            eng.wait_ge(*at("xd"))
            cp(xT[:, :, T:NT], bank("xd")[:, 0:KD * NB].rearrange("p (k b) -> p k b", k=KD))\
                .then_inc(v_.done, v_.tick(("free", "xd"), "xT"))
            eng.wait_ge(*at("par_t"))
            cp(par[:, :], bank("par_t")[:, 0:NROWS])\
                .then_inc(v_.done, v_.tick(("free", "par_t")))
            eng.wait_ge(*at("ss_t"))
            cp(ssf[:, :, :], bank("ss_t")[:, 0:XF * NB].rearrange("p (f b) -> p f b", f=XF))\
                .then_inc(v_.done, v_.tick(("free", "ss_t")))
            eng.wait_ge(*v_.latest())
            ts(qgain[:, :], col("q_norm"), HD ** -0.5, None, ALU.mult)\
                .then_inc(v_.done, v_.tick())
            c0 = ROWS["k_a"][0]
            ts(ka1[:, :], par[:, c0:c0 + 4], -1.0, 1.0, ALU.mult, ALU.add)\
                .then_inc(v_.done, v_.tick())
            eng.wait_ge(*v_.latest())
            lo_of_chunk(("xr", 0))
            normalise("mix", "norm_mix", early_x_hi)
            v_.stage("proj")
            def keys_normal(f):
                k_ = XR[:, 4 + f, 1:1 + NT]
                eng.wait_ge(*at(f"sh{4 + f}"))
                eng.wait_ge(*v_.latest())
                ts(tmp[4], k_, col("k_k", f), None, ALU.mult)\
                    .then_inc(v_.done, v_.tick())
                eng.wait_ge(*v_.latest())
                tt(sq[:, 0, :], tmp[4], tmp[4], ALU.mult)\
                    .then_inc(v_.done, v_.tick(f"kks_in{f}"))

            def log_decays(f):
                r_, k_ = XR[:, f, 1:1 + NT], XR[:, 4 + f, 1:1 + NT]
                eng.wait_ge(*at(f"sh{f}"))
                eng.wait_ge(*v_.latest())
                eng.wait_ge(*at(f"sig{f}"))
                ts(tmp[2], tmp[2], -0.6065306597126334, None, ALU.mult)\
                    .then_inc(v_.done, v_.tick())
                ts(tmp[0], tmp[3], col("k_a", f), ka1[:, f:f + 1], ALU.mult, ALU.add)\
                    .then_inc(v_.done, v_.tick())
                eng.wait_ge(*v_.latest())
                for c in range(QT):
                    s_ = slice(c * P, (c + 1) * P)
                    eng.tensor_tensor_scan(tmp[6][:, s_], ones[:, :], tmp[2][:, s_], 0.0, ALU.mult, ALU.add)\
                        .then_inc(v_.done, v_.tick(f"cl{f}"))
                tt(k_, k_, tmp[0], ALU.mult)\
                    .then_inc(v_.done, v_.tick())
                eng.wait_ge(*v_.latest())
                cl = tmp[6][:, 0:T].rearrange("p (c n) -> p c n", c=QT)
                clm = tmp[7][:, 0:T].rearrange("p (c n) -> p c n", c=QT)
                tt(clm, cl, cl[:, :, 63:64].to_broadcast([P, QT, P]), ALU.subtract)\
                    .then_inc(v_.done, v_.tick())
                stt(out=sq[:, 1, :], in0=r_, scalar=col("r_k", f), in1=k_, op0=ALU.mult, op1=ALU.mult)\
                    .then_inc(v_.done, v_.tick(f"bs_in{f}"))
                eng.wait_ge(*v_.latest())
                tt(tmp[8][:, 0:T], tmp[7][:, 0:T], tmp[2][:, 0:T], ALU.subtract)\
                    .then_inc(v_.done, v_.tick(f"clm{f}"))

            def kk_and_a(f):
                eng.wait_ge(*at(f"kkn{f}"))
                ts(tmp[5], tmp[5], 1e-12, None, ALU.max)\
                    .then_inc(v_.done, v_.tick())
                eng.wait_ge(*v_.latest())
                eng.reciprocal(tmp[5], tmp[5])\
                    .then_inc(v_.done, v_.tick())
                eng.wait_ge(*v_.latest())
                tt(tmp[4], tmp[4], tmp[5], ALU.mult)\
                    .then_inc(v_.done, v_.tick())
                eng.wait_ge(*v_.latest())
                tt(tmp[5], tmp[4], tmp[3], ALU.mult)\
                    .then_inc(v_.done, v_.tick(f"kk_a{f}"))

            def factors_made(f):
                r_, k_, vv = XR[:, f, 1:1 + NT], XR[:, 4 + f, 1:1 + NT], XR[:, 8 + f, 1:1 + NT]
                cl = tmp[6][:, 0:T].rearrange("p (c n) -> p c n", c=QT)
                eng.wait_ge(*at(f"sh{8 + f}"))
                if f:
                    eng.wait_ge(*at(f"stored_f{f - 1}"))
                eng.wait_ge(*at(f"E{f}"))
                eng.wait_ge(*v_.latest())
                stt(out=ARs[:, 0, :, 0:P], in0=tmp[4][:, 0:T].rearrange("p (c n) -> p c n", c=QT), scalar=-1.0, in1=tmp[8][:, 0:T].rearrange("p (c n) -> p c n", c=QT), op0=ALU.mult, op1=ALU.mult)\
                    .then_inc(v_.done, v_.tick())
                tt(ARs[:, 0, :, P:2 * P], r_[:, 0:T].rearrange("p (c n) -> p c n", c=QT), cl, ALU.mult)\
                    .then_inc(v_.done, v_.tick())
                tt(BHs[:, 0, :], tmp[5][:, 0:T], tmp[1][:, 0:T], ALU.mult)\
                    .then_inc(v_.done, v_.tick())
                tt(KHs[:, 0, :], k_[:, 0:T], tmp[1][:, 0:T], ALU.mult)\
                    .then_inc(v_.done, v_.tick(f"tmf{f}"))
                ts(dv[:, 1, f, :], tmp[4][:, T:NT], -1.0, None, ALU.mult)\
                    .then_inc(v_.done, v_.tick())
                cp(dv[:, 2, f, :], tmp[5][:, T:NT])\
                    .then_inc(v_.done, v_.tick())
                cp(dv[:, 3, f, :], k_[:, T:NT])\
                    .then_inc(v_.done, v_.tick())
                cp(dv[:, 4, f, :], r_[:, T:NT])\
                    .then_inc(v_.done, v_.tick())
                cp(dv[:, 5, f, :], vv[:, T:NT])\
                    .then_inc(v_.done, v_.tick(f"prep{f}"))

            def bonus(f):
                eng.wait_ge(*v_.latest())
                for h, (lo, hi) in enumerate(HALFS):
                    eng.wait_ge(*at(f"bs{f}h{h}"))
                    tt(XR[:, 4 + f, 1 + lo:1 + hi], bank(f"bs{f}h{h}")[:, 0:hi - lo], XR[:, 8 + f, 1 + lo:1 + hi], ALU.mult)\
                        .then_inc(v_.done, v_.tick(("free", f"bs{f}h{h}"), f"bonus{f}"))

            def xr_tiles(c):
                for f in XR_PAIRS[c]:
                    for h, (lo, hi) in enumerate(HALFS):
                        eng.wait_ge(*at(f"xr{f}h{h}"))
                        cp(XR[:, f, 1 + lo:1 + hi], bank(f"xr{f}h{h}")[:, 0:hi - lo])\
                            .then_inc(v_.done, v_.tick(("free", f"xr{f}h{h}"), f"xr_s{f}"))

            lo_of_chunk(("xr", 1))
            xr_tiles(0)
            lo_of_chunk(("xr", 2))
            xr_tiles(1)
            lo_of_chunk(("xr", 3))
            xr_tiles(2)
            lo_of_chunk(("xr", 4))
            keys_normal(0)
            xr_tiles(3)
            lo_of_chunk(("xr", 5))
            log_decays(0)
            kk_and_a(0)
            xr_tiles(4)
            lo_of_chunk(("xr", 6))
            factors_made(0)
            bonus(0)
            keys_normal(1)
            xr_tiles(5)
            lo_of_chunk(("kv", 0))
            log_decays(1)
            kk_and_a(1)
            xr_tiles(6)
            lo_of_chunk(("kv", 1))
            factors_made(1)
            bonus(1)
            keys_normal(2)
            lo_of_chunk(("kv", 2))
            log_decays(2)
            kk_and_a(2)
            factors_made(2)
            bonus(2)
            keys_normal(3)
            log_decays(3)
            lo_of_chunk(("q", 0))
            kk_and_a(3)
            factors_made(3)
            lo_of_chunk(("q", 1))
            bonus(3)
            eng.wait_ge(*v_.latest())
            for w in range(6):
                eng.wait_ge(*at(f"dv{w}"))
                cp(dvt[:, w, :], bank(f"dv{w}")[0:NB, :])\
                    .then_inc(v_.done, v_.tick(("free", f"dv{w}"), "dvt"))
            v_.stage("att")
            eng.wait_ge(*at("masks"))
            for i in range(4):
                n = min(4, XF - 4 * i) * P
                eng.wait_ge(*at(f"xrl{i}"))
                cp(sst[:, i * 512:i * 512 + n], bank(f"xrl{i}")[0:9, 0:n])\
                    .then_inc(v_.done, v_.tick(("free", f"xrl{i}"), "shift_rows"))
            eng.wait_ge(*at("zkv"))
            eng.wait_ge(*at("sh11"))
            for v in range(2):
                k_ = zkv[:, 0:QT, 256 + 256 * v:384 + 256 * v]
                tt(kn[:, v, :, :], k_, k_, ALU.mult)\
                    .then_inc(v_.done, v_.tick())
                k_ = zkv[0:NB, QT, 256 + 256 * v:384 + 256 * v]
                tt(dkn[:, v * P:(v + 1) * P], k_, k_, ALU.mult)\
                    .then_inc(v_.done, v_.tick())
            eng.wait_ge(*v_.latest())
            eng.tensor_reduce(krs.rearrange("p v t g -> p (v t g)"), kn.rearrange("p v t (g d) -> p (v t g) d", d=HD), AX.X, ALU.add)\
                .then_inc(v_.done, v_.tick())
            eng.tensor_reduce(drs, dkn.rearrange("p (j d) -> p j d", d=HD), AX.X, ALU.add)\
                .then_inc(v_.done, v_.tick("kss"))
            eng.wait_ge(*at("krt"))
            eng.reciprocal(krs, krs)\
                .then_inc(v_.done, v_.tick())
            eng.reciprocal(drs, drs)\
                .then_inc(v_.done, v_.tick())
            eng.wait_ge(*v_.latest())
            for v in range(2):
                tt(kn[:, v, :, :].rearrange("p t (g d) -> p t g d", d=HD), zkv[:, 0:QT, 256 + 256 * v:384 + 256 * v].rearrange("p t (g d) -> p t g d", d=HD), krs[:, v, :, :].unsqueeze(3).to_broadcast([P, QT, G, HD]), ALU.mult)\
                    .then_inc(v_.done, v_.tick(f"kn{v}"))
                tt(dkn[:, v * P:(v + 1) * P].rearrange("p (g d) -> p g d", d=HD), zkv[0:NB, QT, 256 + 256 * v:384 + 256 * v].rearrange("p (g d) -> p g d", d=HD), drs[:, 2 * v:2 * v + 2].unsqueeze(2).to_broadcast([NB, G, HD]), ALU.mult)\
                    .then_inc(v_.done, v_.tick(f"dkn{v}"))
            for r in range(R):
                eng.wait_ge(*at(f"qrt{r}"))
                eng.reciprocal(rstd[:, :], rstd[:, :])\
                    .then_inc(v_.done, v_.tick())
                eng.wait_ge(*v_.latest())
                stt(out=qT[:, r, :], in0=qT[:, r, :], scalar=qgain[:, 0:1], in1=rstd[:, :], op0=ALU.mult, op1=ALU.mult)\
                    .then_inc(v_.done, v_.tick(f"q_n{r}", "qTs"))
            eng.memset(qall, 0.0)\
                .then_inc(v_.done, v_.tick())
            eng.memset(qb, 0.0)\
                .then_inc(v_.done, v_.tick())
            eng.wait_ge(*v_.latest())
            for g in range(G):
                lo, hi = g * HD, (g + 1) * HD
                cp(qall[lo:hi, :].rearrange("p (b h) -> p b h", h=NH)[:, :, g * R:(g + 1) * R], qT[lo:hi, :, T:NT].rearrange("p r b -> p b r"))\
                    .then_inc(v_.done, v_.tick())
            eng.wait_ge(*v_.latest())
            for b in range(NB):
                cp(qb[:, b, b * NH:(b + 1) * NH], qall[:, b * NH:(b + 1) * NH])\
                    .then_inc(v_.done, v_.tick("qb"))
            for v in range(2):
                eng.wait_ge(*at(f"cache{v}"))
                eng.wait_ge(*at(f"csq{v}"))
                eng.tensor_reduce(crs, csq.rearrange("p t (g d) -> p (t g) d", d=HD).rearrange("p (t g) d -> p t g d", g=G), AX.X, ALU.add)\
                    .then_inc(v_.done, v_.tick(f"css{v}"))
                eng.wait_ge(*at(f"crt{v}"))
                eng.reciprocal(crs, crs)\
                    .then_inc(v_.done, v_.tick())
                eng.wait_ge(*v_.latest())
                k_ = cache[:, v, :, 0:P].rearrange("p t (g d) -> p t g d", d=HD)
                tt(k_, k_, crs.unsqueeze(3).to_broadcast([P, NPG, G, HD]), ALU.mult)\
                    .then_inc(v_.done, v_.tick(f"ckn{v}"))
                eng.wait_ge(*v_.latest())
                for m in range(2):
                    eng.wait_ge(*at(f"conv{v}{m}"))
                    tt(stc[:, 2 * v + m:2 * v + m + 1], bank(f"conv{v}{m}")[:, 320:321], col("cmp_b1", 2 * v + m), ALU.add)\
                        .then_inc(v_.done, v_.tick(f"cb{v}{m}"))
            for v in range(2):
                eng.wait_ge(*at(f"cmp{v}"))
                ts([kc, vc][v], bank(f"cmp{v}")[:, 0:160], col("cmp_b2", v), None, ALU.add)\
                    .then_inc(v_.done, v_.tick(("free", f"cmp{v}"), *(["vc"] if v else [])))
            eng.wait_ge(*v_.latest())
            eng.wait_ge(*at("qms2h1"))
            eng.wait_ge(*at("qms3h1"))
            tt(sq[:, 0, 0:160], kc, kc, ALU.mult)\
                .then_inc(v_.done, v_.tick("kcsq"))
            eng.wait_ge(*at("kcrt"))
            eng.reciprocal(kcn, kcn)\
                .then_inc(v_.done, v_.tick())
            eng.wait_ge(*v_.latest())
            stt(out=kcn, in0=kc, scalar=col("k_norm", 0), in1=kcn, op0=ALU.mult, op1=ALU.mult)\
                .then_inc(v_.done, v_.tick("kcn"))
            eng.wait_ge(*at("vc_t"))
            cp(vcd, bank("vc_t")[:, 0:P])\
                .then_inc(v_.done, v_.tick())
            cp(vcp[0:NCP, :], bank("vc_t")[0:NCP, P:2 * P])\
                .then_inc(v_.done, v_.tick("vcd", ("free", "vc_t")))
            for v in range(2):
                eng.wait_ge(*at(f"sd{v}"))
                eng.tensor_reduce(st[0:64, v:v + 1], bank(f"sd{v}")[0:64, 0:257], AX.X, ALU.max, negate=True)\
                    .then_inc(v_.done, v_.tick(f"sdm{v}"))
            eng.wait_ge(*at("sdc"))
            tt(pcs, bank("sdc")[0:64, 0:P], dec_add[:, :, :].rearrange("p b n -> p (b n)"), ALU.add)\
                .then_inc(v_.done, v_.tick(("free", "sdc")))
            eng.wait_ge(*v_.latest())
            eng.tensor_reduce(st[0:64, 2:3], pcs, AX.X, ALU.max, negate=True)\
                .then_inc(v_.done, v_.tick("sdm2"))
            eng.wait_ge(*at("sde0"))
            eng.wait_ge(*at("sde1"))
            eng.wait_ge(*at("sde2"))
            eng.wait_ge(*at("gd"))
            eng.reciprocal(st[0:64, 8:11], st[0:64, 4:7])\
                .then_inc(v_.done, v_.tick())
            eng.wait_ge(*v_.latest())
            for i, br in enumerate((1, 2, 0)):
                tt(st[0:64, 12 + i:13 + i], st[0:64, 8 + i:9 + i], scol[0:64, br:br + 1], ALU.mult)\
                    .then_inc(v_.done, v_.tick())
            eng.wait_ge(*v_.latest())
            ts(diag[0:64, 2, 0:64], ident[0:64, 0:64], st[0:64, 14:15], None, ALU.mult)\
                .then_inc(v_.done, v_.tick("pdc"))
            for v in range(2):
                ts(diag[0:64, v, 0:64], ident[0:64, 0:64], st[0:64, 12 + v:13 + v], None, ALU.mult)\
                    .then_inc(v_.done, v_.tick())
                ts(st[0:64, 64 + v * NB:64 + (v + 1) * NB], dec_own[:, :], pbuf[0:64, v, 256:257], None, ALU.mult)\
                    .then_inc(v_.done, v_.tick(f"pd{v}"))
            eng.wait_ge(*at("od"))
            for g in range(G):
                lo, hi = g * HD, (g + 1) * HD
                cp(oT[lo:hi, 0:R, T:NT], bank("od")[lo:hi, 0:64].rearrange("p (b g r) -> p g r b", g=G, r=R)[:, g])\
                    .then_inc(v_.done, v_.tick(("free", "od")))
            eng.wait_ge(*v_.latest())

            PER, AHEAD = 16, 3
            UNITS = QT * PER

            def max_unit(i):
                qt = i // PER
                eng.wait_ge(*at(f"s{i}"))
                if i >= 4:
                    eng.wait_ge(*at(f"se{i - 4}"))
                ps = bank(f"s{i}")
                tt(ps[:, qt * P:(qt + 1) * P], ps[:, qt * P:(qt + 1) * P], causal[:, :], ALU.add)\
                    .then_inc(v_.done, v_.tick())
                eng.wait_ge(*v_.latest())
                eng.tensor_reduce(st[:, i % 4:i % 4 + 1], ps[:, 0:(qt + 1) * P], AX.X, ALU.max, negate=True)\
                    .then_inc(v_.done, v_.tick(f"sm{i}"))

            def scale_unit(i):
                qt, u = divmod(i, PER)
                r, g, v = u // 4, u // 2 % 2, u % 2
                h = g * R + r
                eng.wait_ge(*at(f"se{i}"))
                eng.reciprocal(st[:, 16 + i % 4:17 + i % 4], st[:, 8 + i % 4:9 + i % 4])\
                    .then_inc(v_.done, v_.tick())
                eng.wait_ge(*v_.latest())
                ts(pbuf[:, i % 4, 0:(qt + 1) * P], pbuf[:, i % 4, 0:(qt + 1) * P], st[:, 16 + i % 4:17 + i % 4], gate[:, qt, 3 * h + 1 + v:3 * h + 2 + v], ALU.mult, ALU.mult)\
                    .then_inc(v_.done, v_.tick(f"p{i}"))

            def block_max(qt):
                eng.wait_ge(*at(f"sc{qt}"))
                if qt:
                    eng.wait_ge(*at(f"ptc{qt - 1}_1"))
                tt(pcm, bank(f"sc{qt}")[:, 0:NH * NCP].rearrange("p (h n) -> p h n", h=NH), cmp_add[:, qt, :].unsqueeze(1).to_broadcast([P, NH, NCP]), ALU.add)\
                    .then_inc(v_.done, v_.tick(("free", f"sc{qt}")))
                eng.wait_ge(*v_.latest())
                eng.tensor_reduce(stc[:, 8:16], pcm, AX.X, ALU.max)\
                    .then_inc(v_.done, v_.tick())
                eng.wait_ge(*v_.latest())
                tt(pcm, pcm, stc[:, 8:16].unsqueeze(2).to_broadcast([P, NH, NCP]), ALU.subtract)\
                    .then_inc(v_.done, v_.tick(f"scm{qt}"))

            def block_scale(qt):
                eng.wait_ge(*at(f"sce{qt}"))
                tt(pcm, pcm, cmp_keep[:, qt, :].unsqueeze(1).to_broadcast([P, NH, NCP]), ALU.mult)\
                    .then_inc(v_.done, v_.tick())
                eng.wait_ge(*v_.latest())
                eng.tensor_reduce(stc[:, 16:24], pcm, AX.X, ALU.add)\
                    .then_inc(v_.done, v_.tick())
                eng.wait_ge(*v_.latest())
                ts(stc[:, 16:24], stc[:, 16:24], 1e-30, None, ALU.max)\
                    .then_inc(v_.done, v_.tick())
                eng.wait_ge(*v_.latest())
                eng.reciprocal(stc[:, 16:24], stc[:, 16:24])\
                    .then_inc(v_.done, v_.tick())
                eng.wait_ge(*v_.latest())
                tt(stc[:, 16:24], stc[:, 16:24], gate[:, qt, :].rearrange("p (h n) -> p h n", n=3)[:, :, 0], ALU.mult)\
                    .then_inc(v_.done, v_.tick())
                eng.wait_ge(*v_.latest())
                tt(pcm, pcm, stc[:, 16:24].unsqueeze(2).to_broadcast([P, NH, NCP]), ALU.mult)\
                    .then_inc(v_.done, v_.tick(f"pc{qt}"))

            def mixed(qt):
                eng.wait_ge(*at(f"o{qt}"))
                cp(oT[:, 0:R, qt * P:(qt + 1) * P], bank(f"o{qt}").rearrange("p (r n) -> p r n", r=R))\
                    .then_inc(v_.done, v_.tick(("free", f"o{qt}")))

            block_max(0)
            for i in range(AHEAD):
                max_unit(i)
            block_scale(0)
            for i in range(UNITS):
                qt, u = divmod(i, PER)
                if qt + 1 < QT and u == 8:
                    block_max(qt + 1)
                if qt + 1 < QT and u == 10:
                    block_scale(qt + 1)
                scale_unit(i)
                if i + AHEAD < UNITS:
                    max_unit(i + AHEAD)
                if qt and u == 2:
                    mixed(qt - 1)
            mixed(QT - 1)
            v_.end("att")

            v_.stage("rwkv")
            eng.wait_ge(*at("end:att:pe"))
            eng.wait_ge(*at("end:att:act"))
            eng.wait_ge(*at("stored_att"))
            for f in range(4):
                eng.wait_ge(*at("tms33"))
                cp(XR[:, 8 + f, 1:1 + NT], XR[:, 4 + f, 1:1 + NT])\
                    .then_inc(v_.done, v_.tick())
            eng.memset(Hs, 0.0)\
                .then_inc(v_.done, v_.tick())
            eng.memset(Hm, 0.0)\
                .then_inc(v_.done, v_.tick("Hm0"))
            v_.end("prep")
            eng.wait_ge(*v_.latest())
            mask2 = us_ui[:, :, :].rearrange("p s n -> p (s n)").unsqueeze(1).to_broadcast([P, 2, 256])

            def four(m):
                return m.unsqueeze(1).to_broadcast([P, 4, P])

            UNITS = [(hg, name, i) for hg in range(2) for name in ("ln", "mq") for i in range(2)]

            def chunk_products(c, unit):
                hg, name, i = UNITS[unit]
                h0 = hg * 4 + i * 2
                into = (LNs if name == "ln" else MQs)[c % 2]
                eng.wait_ge(*at(f"{name}{c}{hg}{i}"))
                tt(into[:, h0:h0 + 2, :], bank(f"{name}{c}{hg}{i}").rearrange("p (h n) -> p h n", h=2), mask2, ALU.mult)\
                    .then_inc(v_.done, v_.tick(("free", f"{name}{c}{hg}{i}")))

            def start_t(c):
                for hg in range(2):
                    t4 = Tsb[:, hg, :].rearrange("p (h n) -> p h n", h=4)
                    eng.wait_ge(*at(f"l{c}{hg}"))
                    tt(t4, bank(f"l{c}{hg}").rearrange("p (h n) -> p h n", h=4), four(level[:, 0, :]), ALU.mult)\
                        .then_inc(v_.done, v_.tick(("free", f"l{c}{hg}")))
                eng.wait_ge(*v_.latest())
                for hg in range(2):
                    t4 = Tsb[:, hg, :].rearrange("p (h n) -> p h n", h=4)
                    tt(t4, t4, four(ident[:, :]), ALU.add)\
                        .then_inc(v_.done, v_.tick(f"Ts{c}{hg}_1"))

            def start_tt(c):
                for hg in range(2):
                    tt4 = TTsb[:, hg, :].rearrange("p (h n) -> p h n", h=4)
                    tt(tt4, LNs[c % 2][:, hg * 4:hg * 4 + 4, 0:P], four(level1T[:, :]), ALU.mult)\
                        .then_inc(v_.done, v_.tick())
                eng.wait_ge(*v_.latest())
                for hg in range(2):
                    tt4 = TTsb[:, hg, :].rearrange("p (h n) -> p h n", h=4)
                    tt(tt4, tt4, four(ident[:, :]), ALU.add)\
                        .then_inc(v_.done, v_.tick(f"TTs{c}{hg}_1"))

            for unit in range(8):
                chunk_products(0, unit)
            start_t(0)
            start_tt(0)
            for c in range(QT):
                def blocks(x, n, which):
                    return x.rearrange("p (h m s n) -> p h m s n", h=4, s=2, n=n)[:, :, :, which, :]

                def mask(m, n, which):
                    x = m.rearrange("p (m s n) -> p m s n", s=2, n=n)[:, :, which, :]
                    return x.unsqueeze(1).to_broadcast([P, 4, P // (2 * n), n])

                for i, n in enumerate(LEVELS):
                    for hg in range(2):
                        if i:
                            eng.wait_ge(*at(f"TT{c}{hg}_{n // 2}"))
                            eng.memset(side(Xs[:, hg, :], n, 1), 0.0)\
                                .then_inc(v_.done, v_.tick())
                        else:
                            cp(blocks(Xs[:, hg, :], n, 1), mask(ident[:, :], n, 1))\
                                .then_inc(v_.done, v_.tick())
                    for hg in range(2):
                        eng.wait_ge(*at(f"X{c}{hg}_{n}"))
                        tt(blocks(Xs[:, hg, :], n, 0), blocks(bank(f"X{c}{hg}_{n}"), n, 0), mask(level[:, 1 + i, :], n, 0), ALU.mult)\
                            .then_inc(v_.done, v_.tick(f"Xs{c}{hg}_{n}", ("free", f"X{c}{hg}_{n}")))
                        if i == 0:
                            eng.wait_ge(*v_.latest())
                            tt(blocks(Xs[:, hg, :], n, 0), blocks(Xs[:, hg, :], n, 0), mask(ident[:, :], n, 0), ALU.add)\
                                .then_inc(v_.done, v_.tick(f"Xs{c}{hg}_{n}"))
                    if c + 1 < QT:
                        for unit in UNITS_OF[n]:
                            chunk_products(c + 1, unit)
                if c + 1 < QT:
                    start_t(c + 1)
                eng.wait_ge(*at(f"mv{c}"))
                cp(MV, bank(f"mv{c}"))\
                    .then_inc(v_.done, v_.tick(f"mvs{c}", ("free", f"mv{c}")))
                eng.wait_ge(*at(f"us{c}"))
                eng.wait_ge(*at(f"sa{c}"))
                tt(SA, bank(f"sa{c}"), U, ALU.add)\
                    .then_inc(v_.done, v_.tick(f"sas{c}", ("free", f"sa{c}")))

                if c + 1 < QT:
                    eng.wait_ge(*at(f"ap{c}"))
                    eng.wait_ge(*at(f"u{c}"))
                    start_tt(c + 1)

                def per_key(x, i):
                    return x[:, :, i:i + 1].to_broadcast([P, 4, HD])

                tt(Hd, Hs, per_key(ec, c), ALU.mult)\
                    .then_inc(v_.done, v_.tick())
                eng.wait_ge(*at(f"H{c}"))
                eng.wait_ge(*v_.latest())
                tt(Hs, bank(f"H{c}")[:, 0:256].rearrange("p (f n) -> p f n", f=4), per_key(ecr, c), ALU.mult)\
                    .then_inc(v_.done, v_.tick(("free", f"H{c}")))
                eng.wait_ge(*v_.latest())
                tt(Hs, Hs, Hd, ALU.add)\
                    .then_inc(v_.done, v_.tick("Hend"))
                eng.wait_ge(*v_.latest())
                if c + 1 < QT:
                    eng.wait_ge(*at(f"y{c}p"))
                    tt(Hm, Hs, per_key(em, c + 1), ALU.mult)\
                        .then_inc(v_.done, v_.tick(f"Hm{c + 1}"))
                (kind, into), h = (("sa", sa), ("yd", yd))[c % 2], c // 2
                eng.wait_ge(*v_.latest())
                eng.wait_ge(*at(f"{kind}_in{h}"))
                eng.tensor_reduce(into[:, h * 16:(h + 1) * 16], S2, AX.X, ALU.add)\
                    .then_inc(v_.done, v_.tick(f"{kind}_sum{h}"))
            eng.wait_ge(*at("wk"))
            cp(wkt, bank("wk")[0:HD, :])\
                .then_inc(v_.done, v_.tick("wkt", ("free", "wk")))
            def centred(f):
                y = oT[:, 4 + f, :]
                for h, (lo, hi) in enumerate(HALFS):
                    eng.wait_ge(*at(f"gm{f}h{h}"))
                    stt(out=y[:, lo:hi], in0=bank(f"gm{f}h{h}")[:, 0:hi - lo], scalar=-1.0 / HD, in1=y[:, lo:hi], op0=ALU.mult, op1=ALU.add)\
                        .then_inc(v_.done, v_.tick(("free", f"gm{f}h{h}")))
                eng.wait_ge(*v_.latest())
                if f >= 2:
                    eng.wait_ge(*at(f"gv{f - 2}h1"))
                tt(sq[:, f % 2, :], y, y, ALU.mult)\
                    .then_inc(v_.done, v_.tick(f"gsq{f}"))

            def gated(f):
                y, rs = oT[:, 4 + f, :], grstd[f % 2]
                eng.wait_ge(*at(f"grt{f}"))
                eng.reciprocal(rs, rs)\
                    .then_inc(v_.done, v_.tick())
                eng.wait_ge(*v_.latest())
                stt(out=y, in0=y, scalar=col("ln_w", f), in1=rs, op0=ALU.mult, op1=ALU.mult)\
                    .then_inc(v_.done, v_.tick(f"gn{f}"))
                eng.wait_ge(*v_.latest())
                stt(out=y, in0=y, scalar=col("ln_b", f), in1=XR[:, 8 + f, 1:1 + NT], op0=ALU.add, op1=ALU.add)\
                    .then_inc(v_.done, v_.tick())
                eng.wait_ge(*v_.latest())
                for h, (lo, hi) in enumerate(HALFS):
                    eng.wait_ge(*at(f"gg{f}h{h}"))
                    tt(y[:, lo:hi], bank(f"gg{f}h{h}")[:, 0:hi - lo], y[:, lo:hi], ALU.mult)\
                        .then_inc(v_.done, v_.tick(("free", f"gg{f}h{h}"), f"yf{f}"))

            centred(0)
            lo_of_chunk(("wo", 0))
            lo_of_input("o", tiles=range(4))
            centred(1)
            gated(0)
            centred(2)
            gated(1)
            centred(3)
            lo_of_input("o", tiles=[4])
            gated(2)
            lo_of_input("o", tiles=[5])
            gated(3)
            lo_of_input("o", tiles=[6, 7])
            v_.end("rwkv")
            v_.stage("ffn")
            lo_of_chunk(("wo", 1))
            for m in range(KD):
                for h, (lo, hi) in enumerate(HALFS):
                    eng.wait_ge(*at(f"wo{m}h{h}"))
                    tt(xT[:, m, lo:hi], bank(f"wo{m}h{h}")[:, 0:hi - lo], xT[:, m, lo:hi], ALU.add)\
                        .then_inc(v_.done, v_.tick(("free", f"wo{m}h{h}"), f"x1_{m}"))
                if m in (1, 3, 5):
                    lo_of_chunk(("wo", m // 2 + 2) if m < 5 else ("wg", 0))
            eng.wait_ge(*v_.latest())
            eng.wait_ge(*at("end:rwkv:pe"))
            eng.wait_ge(*at("end:rwkv:act"))
            eng.wait_ge(*at("end:rwkv:pool"))
            eng.wait_ge(*at("stored_rwkv"))
            normalise("ffn", "norm_ffn", x_hi)
            v_.stage("ffn")
            lo_of_chunk(("wu", 0))
            for c in range(11):
                lo_of_chunk(("wg", c + 1) if c < 10 else ("wd", 0, 0))
                for m in (2 * c, 2 * c + 1):
                    if m >= 2:
                        eng.wait_ge(*at(f"act_lo{m - 2}"))
                    for h, (lo, hi) in enumerate(HALFS):
                        eng.wait_ge(*at(f"wu{m}h{h}"))
                        eng.wait_ge(*at(f"silu{m}h{h}"))
                        tt(act_f[:, m % 2, lo:hi], bank(f"wu{m}h{h}")[:, 0:hi - lo], silu[:, m % 2, lo:hi], ALU.mult)\
                            .then_inc(v_.done, v_.tick(("free", f"wu{m}h{h}"), f"act_f{m}"))
                for m in (2 * c, 2 * c + 1):
                    eng.wait_ge(*at(f"act_hi{m}"))
                    tt(act_lo[:, m, :], act_f[:, m % 2, :], act_hi[:, m, :].bitcast(F32), ALU.subtract)\
                        .then_inc(v_.done, v_.tick(f"act_lo{m}"))
                lo_of_chunk(("wu", c + 1) if c < 10 else ("wd", 0, 1))
            lo_of_chunk(("wd", 0, 2))
            for c in range(4):
                if c < 3:
                    lo_of_chunk(("wd", c + 1, 0))
                for m in (2 * c, 2 * c + 1):
                    for h, (lo, hi) in enumerate(HALFS):
                        eng.wait_ge(*at(f"wd{m}h{h}"))
                        tt(xT[:, m, lo:hi], bank(f"wd{m}h{h}")[:, 0:hi - lo], xT[:, m, lo:hi], ALU.add)\
                            .then_inc(v_.done, v_.tick(("free", f"wd{m}h{h}"), f"x2_{m}"))
                if c < 3:
                    lo_of_chunk(("wd", c + 1, 1))
                    lo_of_chunk(("wd", c + 1, 2))
            eng.wait_ge(*v_.latest())
            normalise("ple", "norm_ple", x_hi, ("wpg", 0))
            v_.stage("ffn")
            lo_of_chunk(("wpg", 1))
            for m in range(KD):
                s_ = silu[:, m % 2, :]
                eng.wait_ge(*at(f"pep{m}"))
                for h, (lo, hi) in enumerate(HALFS):
                    eng.wait_ge(*at(f"sg{m}h{h}"))
                    tt(s_[:, lo:hi], s_[:, lo:hi], pep[:, m, lo:hi], ALU.mult)\
                        .then_inc(v_.done, v_.tick())
                eng.wait_ge(*v_.latest())
                tt(xT[:, m, :], xT[:, m, :], s_, ALU.add)\
                    .then_inc(v_.done, v_.tick(f"xfin{m}"))
                if m in (1, 3):
                    lo_of_chunk(("wpg", m // 2 + 2))
            for t in range(QT + 1):
                m = P if t < QT else NB
                eng.wait_ge(*at(f"out{t}0"))
                eng.wait_ge(*at(f"ya{t}"))
                cp(ot[0:m, t, 0:T], bank(f"out{t}0")[0:m, :])\
                    .then_inc(v_.done, v_.tick(("free", f"out{t}0"), f"y{t}"))

        return sems


_INS = ["x_prompt", "x_sample", "p_prompt", "p_sample", "cache_kv", "cache_win", "state_wkv", "state_shift",
        "page_table", "norm_mix", "w_in", "q_norm", "k_norm", "cmp_pe", "cmp_w1", "cmp_b1", "cmp_w2", "cmp_b2",
        "shift_mu", "w0", "w2", "a0", "a2", "g2", "k_k", "k_a", "r_k", "ln_w", "ln_b", "w_out", "norm_ffn", "w_gate",
        "w_up", "w_down", "norm_ple", "w_ple_gate", "w_ple"]
_OUTS = [("y_prompt", (1, T, D)), ("y_sample", (NB, 1, D)), ("kv_prompt", (1, 1, T, 4, G, HD)),
         ("kv_sample", (1, NB, 1, 4, G, HD)), ("win_prompt", (1, 1, T, 2, G, HD)),
         ("win_sample", (1, NB, PAST, 2, G, HD)), ("wkv_prompt", (1, 1, NH, HD, HD)),
         ("wkv_sample", (1, NB, NH, HD, HD)), ("shift_prompt", (1, 1, XRC)), ("shift_sample", (1, NB, XRC))]


def kernel(**inputs):
    import numpy as _np
    import concourse.bacc as _bacc
    from concourse import mybir as _mybir
    from concourse.bass_utils import run_bass_kernel_spmd as _run

    arrays = {n: _np.ascontiguousarray(inputs[n]) for n in _INS}
    points = Points()
    for _ in range(2):
        nc = _bacc.Bacc("TRN2", target_bir_lowering=False, num_devices=1, dynamic_dma_scratch_size=4096)
        a = {n: nc.dram_tensor(f"in_{n}", x.shape, _mybir.dt.from_np(x.dtype), kind="ExternalInput").ap()
             for n, x in arrays.items()}
        out = {n: nc.dram_tensor(f"out_{n}", shape, F32, kind="ExternalOutput").ap() for n, shape in _OUTS}
        build(nc, a, out, points)
        points = Points(points.new)
    r = _run(nc, [{f"in_{n}": x for n, x in arrays.items()}], core_ids=[0])
    return tuple(r.results[0][f"out_{n}"] for n, _ in _OUTS)
```
